# Optimizing a Trainium2 kernel written in Bass

```python
import functools
import jax, jax.numpy as jnp
from jax import lax
import numpy as np

D_MODEL = 1024
BATCH = 1
SEQ = 1024
DEPTH = 1
DEC_BATCH = 8
DEC_SEQ = 1
PAST_LEN = 8192
PAGE_SIZE = 128

N_META = 16
RMS_EPS = 1e-6
MLA_HEADS = 16
Q_LORA = 384
KV_LORA = 256
NOPE_DIM = 64
ROPE_DIM = 32
V_DIM = D_MODEL // MLA_HEADS
ROPE_THETA = 10000.0
Q_BLOCK = 128
MLA_SCALE = (NOPE_DIM + ROPE_DIM) ** -0.5
NEG_BIG = -1e30
GDN_HEADS = 8
GDN_DK = 128
GDN_DV = D_MODEL // GDN_HEADS
GDN_KEY = GDN_HEADS * GDN_DK
GDN_VAL = GDN_HEADS * GDN_DV
GDN_QKV = 2 * GDN_KEY + GDN_VAL
CONV_W = 4
CHUNK = 64
N_GROUPS = 4
EXPERTS_PER_GROUP = 8
N_EXPERTS = N_GROUPS * EXPERTS_PER_GROUP
TOP_K = 2
D_EXPERT = 256
MOE_BLOCK = 128
OFF_KV = Q_LORA
OFF_QKV = OFF_KV + KV_LORA + ROPE_DIM
OFF_Z = OFF_QKV + GDN_QKV
OFF_B = OFF_Z + GDN_VAL
OFF_A = OFF_B + GDN_HEADS
OFF_GM = OFF_A + GDN_HEADS
OFF_GG = OFF_GM + D_MODEL
D_IN = OFF_GG + D_MODEL
IN_SPLITS = [OFF_KV, OFF_QKV, OFF_Z, OFF_B, OFF_A, OFF_GM, OFF_GG]

kernel_name = 'hybrid_mla_gdn_hmoe_step'

def rms_norm(x, w):
    xf = x.astype(jnp.float32)
    y = xf * lax.rsqrt(jnp.mean(xf * xf, axis=-1, keepdims=True) + RMS_EPS)
    return (y * w.astype(jnp.float32)).astype(x.dtype)

def l2norm(x):
    return x * lax.rsqrt(jnp.sum(x * x, axis=-1, keepdims=True) + RMS_EPS)

def rope_tables(pos):
    inv_freq = ROPE_THETA ** (-jnp.arange(0, ROPE_DIM, 2, dtype=jnp.float32) / ROPE_DIM)
    ang = pos.astype(jnp.float32)[:, None] * inv_freq[None, :]
    return jnp.cos(ang), jnp.sin(ang)

def apply_rope(x, cos, sin):
    x1, x2 = jnp.split(x.astype(jnp.float32), 2, axis=-1)
    return jnp.concatenate([x1 * cos - x2 * sin, x2 * cos + x1 * sin], axis=-1).astype(x.dtype)

def causal_conv(x_pad, conv_w):
    c = x_pad.shape[-1]
    return lax.conv_general_dilated(x_pad, conv_w.astype(x_pad.dtype)[:, None, :], window_strides=(1,),
                                    padding='VALID', dimension_numbers=('NWC', 'WIO', 'NWC'),
                                    feature_group_count=c)

def mla_prompt(q_nope, q_rope, c_kv, k_rope, w_uk, w_uv):
    b, t = c_kv.shape[:2]
    k_nope = jnp.einsum('btc,chn->bthn', c_kv, w_uk)
    v = jnp.einsum('btc,chv->bthv', c_kv, w_uv)
    n_blk = -(-t // Q_BLOCK)
    pad = n_blk * Q_BLOCK - t
    qn = jnp.pad(q_nope, ((0, 0), (0, pad), (0, 0), (0, 0)))
    qr = jnp.pad(q_rope, ((0, 0), (0, pad), (0, 0), (0, 0)))
    key_pos = jnp.arange(t)

    def query_block(i):
        start = i * Q_BLOCK
        qn_b = lax.dynamic_slice_in_dim(qn, start, Q_BLOCK, axis=1)
        qr_b = lax.dynamic_slice_in_dim(qr, start, Q_BLOCK, axis=1)
        s = (jnp.einsum('bqhn,bkhn->bhqk', qn_b, k_nope).astype(jnp.float32)
             + jnp.einsum('bqhr,bkr->bhqk', qr_b, k_rope).astype(jnp.float32)) * MLA_SCALE
        q_pos = start + jnp.arange(Q_BLOCK)
        s = jnp.where(key_pos[None, :] <= q_pos[:, None], s, NEG_BIG)
        p = jax.nn.softmax(s, axis=-1)
        return jnp.einsum('bhqk,bkhv->bqhv', p.astype(v.dtype), v)

    o = lax.map(query_block, jnp.arange(n_blk))
    o = jnp.swapaxes(o, 0, 1).reshape(b, n_blk * Q_BLOCK, MLA_HEADS, V_DIM)
    return o[:, :t]

def mla_sample(q_nope, q_rope, c_new, kr_new, w_uk, w_uv, cache_kv_latent, cache_k_rope, page_table):
    f32 = jnp.float32
    q_lat = jnp.einsum('bshn,chn->bshc', q_nope, w_uk).astype(f32)
    qr = q_rope.astype(f32)
    db, s_len = q_lat.shape[:2]

    def page_step(carry, pages):
        m, l, acc = carry
        c = cache_kv_latent[pages].astype(f32)
        kr = cache_k_rope[pages].astype(f32)
        s = (jnp.einsum('bshc,bpc->bshp', q_lat, c) + jnp.einsum('bshr,bpr->bshp', qr, kr)) * MLA_SCALE
        m_new = jnp.maximum(m, s.max(-1))
        corr = jnp.exp(m - m_new)
        p = jnp.exp(s - m_new[..., None])
        return (m_new, l * corr + p.sum(-1), acc * corr[..., None] + jnp.einsum('bshp,bpc->bshc', p, c)), None

    init = (jnp.full((db, s_len, MLA_HEADS), NEG_BIG, f32), jnp.zeros((db, s_len, MLA_HEADS), f32),
            jnp.zeros((db, s_len, MLA_HEADS, KV_LORA), f32))
    (m, l, acc), _ = lax.scan(page_step, init, page_table.T)
    cn = c_new.astype(f32)
    s = (jnp.einsum('bshc,btc->bsht', q_lat, cn) + jnp.einsum('bshr,btr->bsht', qr, kr_new.astype(f32))) * MLA_SCALE
    causal = jnp.tril(jnp.ones((s_len, s_len), bool))[:, None, :]
    s = jnp.where(causal, s, NEG_BIG)
    m_new = jnp.maximum(m, s.max(-1))
    corr = jnp.exp(m - m_new)
    p = jnp.exp(s - m_new[..., None])
    l = l * corr + p.sum(-1)
    acc = acc * corr[..., None] + jnp.einsum('bsht,btc->bshc', p, cn)
    o = jnp.einsum('bshc,chv->bshv', acc / l[..., None], w_uv.astype(f32))
    return o.astype(q_nope.dtype)

def gdn_heads(xc):
    xf = jax.nn.silu(xc.astype(jnp.float32))
    b, t = xf.shape[:2]
    q = l2norm(xf[..., :GDN_KEY].reshape(b, t, GDN_HEADS, GDN_DK)) * (GDN_DK ** -0.5)
    k = l2norm(xf[..., GDN_KEY:2 * GDN_KEY].reshape(b, t, GDN_HEADS, GDN_DK))
    v = xf[..., 2 * GDN_KEY:].reshape(b, t, GDN_HEADS, GDN_DV)
    return q, k, v

def gdn_chunk(state, inp):
    q, k, v, g, beta = inp
    c = q.shape[2]
    G = jnp.cumsum(g, axis=-1)
    causal = jnp.tril(jnp.ones((c, c), bool))
    strict = jnp.tril(jnp.ones((c, c), bool), -1)
    decay = jnp.where(causal, jnp.exp(jnp.where(causal, G[..., :, None] - G[..., None, :], 0.0)), 0.0)
    kb = k * beta[..., None]
    m = jnp.where(strict, jnp.einsum('bhik,bhjk->bhij', kb, k) * decay, 0.0) + jnp.eye(c, dtype=q.dtype)
    rhs = jnp.concatenate([v * beta[..., None], kb * jnp.exp(G)[..., None]], axis=-1)
    sol = lax.linalg.triangular_solve(m, rhs, left_side=True, lower=True, unit_diagonal=True)
    u, w = sol[..., :GDN_DV], sol[..., GDN_DV:]
    v_new = u - jnp.einsum('bhck,bhkv->bhcv', w, state)
    attn = jnp.where(causal, jnp.einsum('bhik,bhjk->bhij', q, k) * decay, 0.0)
    out = jnp.einsum('bhck,bhkv->bhcv', q * jnp.exp(G)[..., None], state) + jnp.einsum('bhij,bhjv->bhiv', attn, v_new)
    g_last = G[..., -1]
    state = state * jnp.exp(g_last)[..., None, None] + jnp.einsum(
        'bhck,bhcv->bhkv', k * jnp.exp(g_last[..., None] - G)[..., None], v_new)
    return state, out

def gdn_prompt(qkv, g, beta, conv_w):
    b, t, _ = qkv.shape
    conv_state = qkv[:, t - (CONV_W - 1):]
    q, k, v = gdn_heads(causal_conv(jnp.pad(qkv, ((0, 0), (CONV_W - 1, 0), (0, 0))), conv_w))
    q, k, v = jnp.swapaxes(q, 1, 2), jnp.swapaxes(k, 1, 2), jnp.swapaxes(v, 1, 2)
    g, beta = jnp.swapaxes(g, 1, 2), jnp.swapaxes(beta, 1, 2)
    s0 = jnp.zeros((b, GDN_HEADS, GDN_DK, GDN_DV), jnp.float32)
    s_meta, o_meta = gdn_chunk(s0, (q[:, :, :N_META], k[:, :, :N_META], v[:, :, :N_META],
                                    g[:, :, :N_META], beta[:, :, :N_META]))
    n_chunks = (t - N_META) // CHUNK

    def to_chunks(a):
        a = a[:, :, N_META:]
        return jnp.moveaxis(a.reshape(a.shape[:2] + (n_chunks, CHUNK) + a.shape[3:]), 2, 0)

    s_fin, o_real = lax.scan(gdn_chunk, s_meta, (to_chunks(q), to_chunks(k), to_chunks(v),
                                                 to_chunks(g), to_chunks(beta)))
    o_real = jnp.moveaxis(o_real, 0, 2).reshape(b, GDN_HEADS, n_chunks * CHUNK, GDN_DV)
    o = jnp.concatenate([o_meta, o_real], axis=2)
    return jnp.swapaxes(o, 1, 2), conv_state, s_fin

def gdn_sample(qkv, g, beta, conv_w, conv_state, rec_state):
    xcat = jnp.concatenate([conv_state.astype(qkv.dtype), qkv], axis=1)
    q, k, v = gdn_heads(causal_conv(xcat, conv_w))

    def step(s, inp):
        q_t, k_t, v_t, g_t, b_t = inp
        s = s * jnp.exp(g_t)[..., None, None]
        delta = (v_t - jnp.einsum('bhkv,bhk->bhv', s, k_t)) * b_t[..., None]
        s = s + jnp.einsum('bhk,bhv->bhkv', k_t, delta)
        return s, jnp.einsum('bhkv,bhk->bhv', s, q_t)

    tm = lambda a: jnp.moveaxis(a, 1, 0)
    s_fin, o = lax.scan(step, rec_state.astype(jnp.float32), (tm(q), tm(k), tm(v), tm(g), tm(beta)))
    return jnp.moveaxis(o, 0, 1), xcat[:, xcat.shape[1] - (CONV_W - 1):], s_fin

def hier_route(h, w_group, b_group, w_router, b_router):
    lg = (h @ w_group).astype(jnp.float32) + b_group.astype(jnp.float32)
    grp = jnp.argmax(lg, axis=-1).astype(jnp.int32)
    gate_g = jnp.take_along_axis(jax.nn.softmax(lg, axis=-1), grp[:, None], axis=-1)
    le = ((h @ w_router).astype(jnp.float32) + b_router.astype(jnp.float32)).reshape(
        -1, N_GROUPS, EXPERTS_PER_GROUP)
    le = jnp.take_along_axis(le, grp[:, None, None], axis=1)[:, 0]
    top_v, top_i = lax.top_k(le, TOP_K)
    return grp[:, None] * EXPERTS_PER_GROUP + top_i, gate_g * jax.nn.softmax(top_v, axis=-1)

def moe_experts(h, expert_id, weight, w_gate, w_up, w_down):
    n_tok = h.shape[0]
    n_asg = n_tok * TOP_K
    n_blocks = (n_asg + N_EXPERTS * (MOE_BLOCK - 1) + MOE_BLOCK - 1) // MOE_BLOCK
    n_slots = n_blocks * MOE_BLOCK
    e_flat = expert_id.reshape(n_asg)
    t_flat = jnp.repeat(jnp.arange(n_tok, dtype=jnp.int32), TOP_K)
    w_flat = weight.reshape(n_asg).astype(h.dtype)
    order = jnp.argsort(e_flat)
    e_sorted = e_flat[order]
    counts = jnp.bincount(e_flat, length=N_EXPERTS)
    padded = (counts + MOE_BLOCK - 1) // MOE_BLOCK * MOE_BLOCK
    pad_end = jnp.cumsum(padded)
    dest = (pad_end - padded)[e_sorted] + jnp.arange(n_asg) - (jnp.cumsum(counts) - counts)[e_sorted]
    slot_tok = jnp.zeros((n_slots,), jnp.int32).at[dest].set(t_flat[order])
    slot_w = jnp.zeros((n_slots,), h.dtype).at[dest].set(w_flat[order])
    blk_expert = jnp.minimum(jnp.searchsorted(pad_end, jnp.arange(n_blocks) * MOE_BLOCK, side='right'),
                             N_EXPERTS - 1)

    def expert_block(args):
        tok, e = args
        xb = h[tok]
        return (jax.nn.silu(xb @ w_gate[e]) * (xb @ w_up[e])) @ w_down[e]

    y = lax.map(expert_block, (slot_tok.reshape(n_blocks, MOE_BLOCK), blk_expert))
    y = y.reshape(n_slots, -1) * slot_w[:, None]
    return jnp.zeros_like(h).at[slot_tok].add(y)

def block_forward(x, pos, mla_core, gdn_core, norm_mix, w_in, q_norm, w_uq, kv_norm, w_uk, w_uv,
                  conv_w, a_log, dt_bias, gdn_norm, w_out, norm_ffn, w_group, b_group,
                  w_router, b_router, w_gate, w_up, w_down):
    b, t, _ = x.shape
    hn = rms_norm(x, norm_mix)
    q_down, kv_down, qkv, z, b_raw, a_raw, gm, gg = jnp.split(hn @ w_in, IN_SPLITS, axis=-1)
    cos, sin = rope_tables(pos)
    q = jnp.einsum('btr,rhd->bthd', rms_norm(q_down, q_norm), w_uq)
    q_nope = q[..., :NOPE_DIM]
    q_rope = apply_rope(q[..., NOPE_DIM:], cos[:, None], sin[:, None])
    c_kv = rms_norm(kv_down[..., :KV_LORA], kv_norm)
    k_rope = apply_rope(kv_down[..., KV_LORA:], cos, sin)
    o_mla = mla_core(q_nope, q_rope, c_kv, k_rope, w_uk, w_uv).reshape(b, t, D_MODEL)
    g = -jnp.exp(a_log.astype(jnp.float32)) * jax.nn.softplus(a_raw.astype(jnp.float32) + dt_bias.astype(jnp.float32))
    beta = jax.nn.sigmoid(b_raw.astype(jnp.float32))
    o, conv_state, rec_state = gdn_core(qkv, g, beta, conv_w)
    zf = z.astype(jnp.float32).reshape(b, t, GDN_HEADS, GDN_DV)
    o_gdn = (rms_norm(o, gdn_norm) * jax.nn.silu(zf)).reshape(b, t, D_MODEL).astype(x.dtype)
    x = x + (jax.nn.sigmoid(gm) * o_mla + jax.nn.sigmoid(gg) * o_gdn) @ w_out
    hf = rms_norm(x, norm_ffn).reshape(b * t, D_MODEL)
    eid, ew = hier_route(hf, w_group, b_group, w_router, b_router)
    x = x + moe_experts(hf, eid, ew, w_gate, w_up, w_down).reshape(b, t, D_MODEL)
    return x, c_kv, k_rope, conv_state, rec_state

def setup_inputs(seed: int = 0) -> dict:
    key = jax.random.key(seed)
    ks = jax.random.split(key, 32)
    f32 = jnp.float32

    def nrm(k, shape, scale):
        return jax.random.normal(k, shape, f32) * scale

    def gain(k, shape):
        return 1.0 + 0.02 * jax.random.normal(k, shape, f32)

    n_pages = PAST_LEN // PAGE_SIZE
    n_pool = (DEC_BATCH * n_pages * 5) // 4
    page_table = jax.random.permutation(ks[4], n_pool)[:DEC_BATCH * n_pages].reshape(
        DEC_BATCH, n_pages).astype(jnp.int32)
    dt = jnp.exp(jax.random.uniform(ks[17], (DEPTH, GDN_HEADS), f32, np.log(1e-3), np.log(1e-1)))
    return {
        'x_prompt': nrm(ks[0], (BATCH, SEQ, D_MODEL), 1.0),
        'x_sample': nrm(ks[1], (DEC_BATCH, DEC_SEQ, D_MODEL), 1.0),
        'cache_kv_latent': nrm(ks[2], (DEPTH, n_pool, PAGE_SIZE, KV_LORA), 1.0),
        'cache_k_rope': nrm(ks[3], (DEPTH, n_pool, PAGE_SIZE, ROPE_DIM), 1.0),
        'page_table': page_table,
        'state_conv': nrm(ks[5], (DEPTH, DEC_BATCH, CONV_W - 1, GDN_QKV), 1.0),
        'state_gdn': nrm(ks[6], (DEPTH, DEC_BATCH, GDN_HEADS, GDN_DK, GDN_DV), 0.1),
        'meta_tokens': nrm(ks[7], (N_META, D_MODEL), 1.0),
        'norm_mix': gain(ks[8], (DEPTH, D_MODEL)),
        'w_in': nrm(ks[9], (DEPTH, D_MODEL, D_IN), D_MODEL ** -0.5),
        'q_norm': gain(ks[10], (DEPTH, Q_LORA)),
        'w_uq': nrm(ks[11], (DEPTH, Q_LORA, MLA_HEADS, NOPE_DIM + ROPE_DIM), Q_LORA ** -0.5),
        'kv_norm': gain(ks[12], (DEPTH, KV_LORA)),
        'w_uk': nrm(ks[13], (DEPTH, KV_LORA, MLA_HEADS, NOPE_DIM), KV_LORA ** -0.5),
        'w_uv': nrm(ks[14], (DEPTH, KV_LORA, MLA_HEADS, V_DIM), KV_LORA ** -0.5),
        'conv_w': nrm(ks[15], (DEPTH, CONV_W, GDN_QKV), CONV_W ** -0.5),
        'a_log': jnp.log(jax.random.uniform(ks[16], (DEPTH, GDN_HEADS), f32, 1.0, 16.0)),
        'dt_bias': dt + jnp.log(-jnp.expm1(-dt)),
        'gdn_norm': gain(ks[18], (DEPTH, GDN_DV)),
        'w_out': nrm(ks[19], (DEPTH, D_MODEL, D_MODEL), D_MODEL ** -0.5),
        'norm_ffn': gain(ks[20], (DEPTH, D_MODEL)),
        'w_group': nrm(ks[21], (DEPTH, D_MODEL, N_GROUPS), D_MODEL ** -0.5),
        'b_group': nrm(ks[22], (DEPTH, N_GROUPS), 0.01),
        'w_router': nrm(ks[23], (DEPTH, D_MODEL, N_EXPERTS), D_MODEL ** -0.5),
        'b_router': nrm(ks[24], (DEPTH, N_EXPERTS), 0.01),
        'w_gate': nrm(ks[25], (DEPTH, N_EXPERTS, D_MODEL, D_EXPERT), D_MODEL ** -0.5),
        'w_up': nrm(ks[26], (DEPTH, N_EXPERTS, D_MODEL, D_EXPERT), D_MODEL ** -0.5),
        'w_down': nrm(ks[27], (DEPTH, N_EXPERTS, D_EXPERT, D_MODEL), D_EXPERT ** -0.5),
        'norm_final': gain(ks[28], (D_MODEL,)),
    }

def reference(x_prompt, x_sample, cache_kv_latent, cache_k_rope, page_table, state_conv, state_gdn,
              meta_tokens, norm_mix, w_in, q_norm, w_uq, kv_norm, w_uk, w_uv, conv_w, a_log, dt_bias,
              gdn_norm, w_out, norm_ffn, w_group, b_group, w_router, b_router, w_gate, w_up, w_down,
              norm_final):
    b_p, s_p, _ = x_prompt.shape
    meta = jnp.broadcast_to(meta_tokens.astype(x_prompt.dtype)[None], (b_p, N_META, D_MODEL))
    xp = jnp.concatenate([meta, x_prompt], axis=1)
    xs = x_sample
    pos_p = jnp.arange(N_META + s_p)
    pos_s = PAST_LEN + jnp.arange(x_sample.shape[1])
    ckv_p, kr_p, cv_p, st_p = [], [], [], []
    ckv_s, kr_s, cv_s, st_s = [], [], [], []
    for layer in range(DEPTH):
        lw = (norm_mix[layer], w_in[layer], q_norm[layer], w_uq[layer], kv_norm[layer], w_uk[layer],
              w_uv[layer], conv_w[layer], a_log[layer], dt_bias[layer], gdn_norm[layer], w_out[layer],
              norm_ffn[layer], w_group[layer], b_group[layer], w_router[layer], b_router[layer],
              w_gate[layer], w_up[layer], w_down[layer])
        xp, c1, k1, v1, s1 = block_forward(xp, pos_p, mla_prompt, gdn_prompt, *lw)
        mla_core = functools.partial(mla_sample, cache_kv_latent=cache_kv_latent[layer],
                                     cache_k_rope=cache_k_rope[layer], page_table=page_table)
        gdn_core = functools.partial(gdn_sample, conv_state=state_conv[layer], rec_state=state_gdn[layer])
        xs, c2, k2, v2, s2 = block_forward(xs, pos_s, mla_core, gdn_core, *lw)
        ckv_p.append(c1); kr_p.append(k1); cv_p.append(v1); st_p.append(s1)
        ckv_s.append(c2); kr_s.append(k2); cv_s.append(v2); st_s.append(s2)
    y_prompt = rms_norm(xp, norm_final)[:, N_META:]
    y_sample = rms_norm(xs, norm_final)
    return (y_prompt, y_sample, jnp.stack(ckv_p), jnp.stack(kr_p), jnp.stack(ckv_s), jnp.stack(kr_s),
            jnp.stack(cv_p), jnp.stack(cv_s), jnp.stack(st_p), jnp.stack(st_s))


_drawn_inputs = setup_inputs


def setup_inputs(seed=0):
    import zlib

    import numpy as np

    out = dict(_drawn_inputs(seed))
    spreads = {}
    factors = {'cache_kv_latent': 5.803,
     'cache_k_rope': 8.0,
     'q_norm': 8.0,
     'kv_norm': 2.992,
     'gdn_norm': 15.505,
     'b_group': 12.203,
     'b_router': 14.135,
     'norm_final': 7.367,
     'norm_ffn': 4.328}
    for name, (base, spread) in spreads.items():
        noise = np.random.default_rng([zlib.crc32(name.encode()), seed]).standard_normal(out[name].shape)
        drawn = base * np.exp(spread * noise) if base else spread * noise
        out[name] = __import__('jax').numpy.asarray(drawn.astype(out[name].dtype))
    for name, factor in factors.items():
        out[name] = (out[name] * factor).astype(out[name].dtype)
    return out
```

```python
from contextlib import ExitStack

import concourse.bass as bass
from concourse import mybir

F32 = mybir.dt.float32
I32 = mybir.dt.int32
ALU = mybir.AluOpType
ACT = mybir.ActivationFunctionType
AX_X = mybir.AxisListType.X

P = 128
D = 1024
KD = D // P
NS = 8
META = 16
SEQ = 1024
PROMPT = META + SEQ
ROWS = NS + PROMPT
HEAD_ROWS = NS + META
NT = 1 + SEQ // P
TILES = [(0, HEAD_ROWS)] + [(HEAD_ROWS + P * i, P) for i in range(NT - 1)]
CHUNKS = [(NS, META)] + TILES[1:]
EPS = 1e-6
HEADS = 16
QL = 384
KQ = QL // P
CL = 256
NOPE = 64
ROPE = 32
HALF = ROPE // 2
QK = NOPE + ROPE
CK = CL + ROPE
MLA_SCALE = QK ** -0.5
NEG = -1e30
PAGES = 64
PAGE = 128
GH = 8
DK = 128
GC = 3 * GH
OFF_QKV = QL + CK
OFF_BA = OFF_QKV + 4 * D
OFF_G = OFF_BA + 2 * GH
GROUPS = 4
PER_GROUP = 8
EXPERTS = GROUPS * PER_GROUP
DE = 256
BLOCKS = (2 * ROWS + EXPERTS * (P - 1) + P - 1) // P
SLOTS = BLOCKS * P
BANK = 512
SPANS = [(0, 512), (512, 1024), (1024, ROWS)]
Z0, GM0, GG0 = GC, GC + GH, GC + 2 * GH
V_CONV, V_MIX, V_Q, V_GDN = 0, 96, 104, 107


class Scope:

    def __init__(self, nc):
        self.nc = nc
        self.stack = ExitStack()
        self.sems = []

    def __enter__(self):
        return self

    def __exit__(self, *a):
        self.stack.close()
        if self.sems:
            self.nc.clear_and_free_semaphores(self.sems)
            self.nc.all_engine_barrier()

    def sb(self, name, shape, dt=F32):
        return self.stack.enter_context(self.nc.sbuf_tensor(name, shape, dt))

    def ps(self, name, shape):
        return self.stack.enter_context(self.nc.psum_tensor(name, shape, F32))

    def sem(self, name):
        self.sems.append(self.nc.alloc_semaphore(name=name))
        return self.sems[-1]


class Core(Scope):

    def __init__(self, nc, dram):
        super().__init__(nc)
        self.dram = dram

    def scope(self):
        return Scope(self.nc)


def chained(eng, sem):
    count = [0]

    def link(ins):
        count[0] += 1
        ins.then_inc(sem, 1)
        eng.wait_ge(sem, count[0])

    return link


def load_constants(k):
    nc, d = k.nc, k.dram
    k.ident = k.sb("ident", [P, P])
    k.ones = k.sb("ones", [P, P])
    k.upto = k.sb("upto", [P, P])
    k.vecT = k.sb("vecT", [P, P])
    k.eps = k.sb("eps", [P, 1])
    k.ba = k.sb("ba", [P, NT + 1, 2 * GH])
    with k.scope() as s:
        rows = s.sb("vec_rows", [P, P])
        turned = s.ps("vec_ps", [P, P])
        c_loaded, c_turned, c_kept = s.sem("c_loaded"), s.sem("c_turned"), s.sem("c_kept")
        c_zero = s.sem("c_zero")
        with nc.Block() as block:
            @block.sync
            def _(sp):
                sp.dma_start(k.ident[:], d["c_ident"]).then_inc(c_loaded, 16)
                sp.dma_start(k.upto[:], d["c_upto"]).then_inc(c_loaded, 16)
                sp.wait_ge(c_zero, 1)
                sp.dma_start(rows[V_CONV:V_MIX, :], d["conv_w"].rearrange("a w (j p) -> (a w j) p", p=P)).then_inc(c_loaded, 16)
                sp.dma_start(rows[V_MIX:V_Q, :], d["norm_mix"].rearrange("a (j p) -> (a j) p", p=P)).then_inc(c_loaded, 16)
                sp.dma_start(rows[V_Q:V_GDN, :], d["q_norm"].rearrange("a (j p) -> (a j) p", p=P)).then_inc(c_loaded, 16)
                sp.dma_start(rows[V_GDN:V_GDN + 1, :], d["gdn_norm"]).then_inc(c_loaded, 16)

            @block.vector
            def _(dve):
                nc.vector.memset(k.ones[:], 1.0)
                nc.vector.memset(k.eps[:], EPS)
                nc.vector.memset(k.ba[:], 0.0)
                nc.vector.memset(rows[:], 0.0).then_inc(c_zero, 1)
                dve.wait_ge(c_turned, 1)
                nc.vector.tensor_copy(k.vecT[:], turned[:]).then_inc(c_kept, 1)

            @block.tensor
            def _(pe):
                pe.wait_ge(c_loaded, 6 * 16)
                nc.tensor.transpose(turned[:], rows[:], k.ident[:]).then_inc(c_turned, 1)


def normalise_input(k):
    nc, d = k.nc, k.dram
    with k.scope() as s:
        x = s.sb("na_x", [P, 2, D])
        xn = s.sb("na_xn", [P, 2, D])
        square = s.sb("na_square", [P, D])
        ss, mean, inv, rstd = (s.sb(f"na_{n}", [P, NT]) for n in ("ss", "mean", "inv", "rstd"))
        turned = s.ps("na_ps", [P, 2, KD, P])
        loaded = [s.sem(f"na_loaded{i}") for i in range(2)]
        zeroed = s.sem("na_zeroed")
        squared, meaned, inverted, rooted, scaled, turn_done, kept = (s.sem(f"na_{n}") for n in (
            "squared", "meaned", "inverted", "rooted", "scaled", "turned", "kept"))
        with nc.Block() as block:
            @block.sync
            def _(sp):
                for t, (r0, n) in enumerate(TILES):
                    if t >= 2:
                        sp.wait_ge(scaled, t - 1)
                        sp.wait_ge(squared, t - 1)
                    if t == 0:
                        sp.dma_start(x[0:NS, 0, :], d["x_sample"].rearrange("b t d -> (b t) d")).then_inc(loaded[0], 16)
                        sp.dma_start(x[NS:HEAD_ROWS, 0, :], d["meta_tokens"]).then_inc(loaded[0], 16)
                    else:
                        sp.dma_start(x[:, t % 2, :], d["x_prompt"][0, (t - 1) * P:t * P, :]).then_inc(loaded[t % 2], 16)

            @block.gpsimd
            def _(pool):
                nc.gpsimd.memset(k.qd[:, 0, :], 0.0)
                nc.gpsimd.memset(k.kvd[:, 0, :], 0.0).then_inc(zeroed, 1)

            @block.scalar
            def _(act):
                def root(t):
                    act.wait_ge(inverted, t + 1)
                    n = TILES[t][1]
                    nc.scalar.activation(rstd[0:n, t:t + 1], inv[0:n, t:t + 1], ACT.Sqrt).then_inc(rooted, 1)

                for t, (r0, n) in enumerate(TILES):
                    act.wait_ge(loaded[t % 2], 16 * (t // 2 + 1) + (16 if t % 2 == 0 else 0))
                    if t:
                        act.wait_ge(squared, t)
                    nc.scalar.activation(square[0:n, :], x[0:n, t % 2, :], ACT.Square,
                                         accum_out=ss[0:n, t:t + 1]).then_inc(squared, 1)
                    root(t)

            @block.vector
            def _(dve):
                def keep(t):
                    r0, n = TILES[t]
                    dve.wait_ge(turn_done, t + 1)
                    nc.vector.tensor_tensor(k.hT[:, :, r0:r0 + n], turned[:, t % 2, :, 0:n],
                                            k.vecT[:, V_MIX:V_Q].unsqueeze(2).to_broadcast([P, KD, n]),
                                            ALU.mult).then_inc(kept, 1)

                for t, (r0, n) in enumerate(TILES):
                    dve.wait_ge(squared, t + 1)
                    nc.vector.tensor_scalar(mean[0:n, t:t + 1], ss[0:n, t:t + 1], 1.0 / D, EPS,
                                            ALU.mult, ALU.add).then_inc(meaned, 1)
                    dve.wait_ge(meaned, t + 1)
                    nc.vector.reciprocal(inv[0:n, t:t + 1], mean[0:n, t:t + 1]).then_inc(inverted, 1)
                    dve.wait_ge(rooted, t + 1)
                    if t >= 2:
                        dve.wait_ge(turn_done, t - 1)
                    nc.vector.tensor_scalar(xn[0:n, t % 2, :], x[0:n, t % 2, :], rstd[0:n, t:t + 1], None,
                                            ALU.mult).then_inc(scaled, 1)
                    if t:
                        keep(t - 1)
                keep(NT - 1)

            @block.tensor
            def _(pe):
                for t, (r0, n) in enumerate(TILES):
                    pe.wait_ge(scaled, t + 1)
                    if t >= 2:
                        pe.wait_ge(kept, t - 1)
                    for c in range(KD):
                        last = nc.tensor.transpose(turned[:, t % 2, c, 0:n], xn[0:n, t % 2, c * P:(c + 1) * P],
                                                   k.ident[0:n, 0:n])
                    last.then_inc(turn_done, 1)


def project_input(k):
    nc, d = k.nc, k.dram
    w_in = d["w_in"][0].rearrange("(c p) n -> p c n", p=P)
    projT = d["projT"].rearrange("(g c) p t -> g p c t", c=4)
    with k.scope() as s:
        w = s.sb("pi_w", [P, 2, KD, BANK])
        out = s.sb("pi_out", [P, 2, 4, ROWS])
        acc = s.ps("pi_acc", [P, 2, 3, BANK])
        w_loaded = [s.sem(f"pi_w_loaded{i}") for i in range(2)]
        acc_ready, acc_kept = s.sem("pi_acc_ready"), s.sem("pi_acc_kept")
        stored = [s.sem(f"pi_stored{i}") for i in range(2)]
        latents_out = s.sem("pi_latents_out")
        whole = [(r0, n, t) for t, (r0, n) in enumerate(TILES)]
        jobs = [(0, QL, whole, lambda n, t: k.qd[0:n, t, :]),
                (QL, CK, whole, lambda n, t: k.kvd[0:n, t, :]),
                (OFF_BA, 2 * GH, [(r0, n, t) for t, (r0, n) in enumerate(CHUNKS)] + [(0, NS, NT)],
                 lambda n, t: k.ba[0:n, t, :])]
        token_units = sum(len(j[2]) for j in jobs)
        assert token_units % 2 == 0
        J = len(jobs)
        runs = [(OFF_QKV, 0, 2, ACT.Copy), (OFF_QKV + 2 * BANK, 2, 4, ACT.Copy), (OFF_QKV + 6 * BANK, 6, 2, ACT.Silu), (OFF_G, 8, 4, ACT.Sigmoid)]

        with nc.Block() as block:
            @block.sync
            def _(sp):
                for i, (c0, n, tiles, _) in enumerate(jobs):
                    if i >= 2:
                        sp.wait_ge(acc_ready, NT * (i - 1))
                    sp.dma_start(w[:, i % 2, :, 0:n], w_in[:, :, c0:c0 + n]).then_inc(w_loaded[i % 2], 16)
                for c0, g0, ng, _ in runs:
                    with sp.Fori(0, ng // 2) as i:
                        for h in range(2):
                            slot = (J + h) % 2
                            sp.wait_ge(acc_ready, i * 8 + (token_units + 4 * (g0 + h - 1)))
                            sp.dma_start(w[:, slot], w_in[:, :, bass.ds(i * (2 * BANK) + (c0 + h * BANK), BANK)]).then_inc(w_loaded[slot], 16)

            @block.tensor
            def _(pe):
                unit = 0
                for i, (c0, n, tiles, _) in enumerate(jobs):
                    pe.wait_ge(w_loaded[i % 2], 16 * (i // 2 + 1))
                    for r0, m, t in tiles:
                        if unit >= 2:
                            pe.wait_ge(acc_kept, unit - 1)
                        for c in range(KD):
                            last = nc.tensor.matmul(acc[0:m, unit % 2, 0, 0:n], k.hT[:, c, r0:r0 + m],
                                                    w[:, i % 2, c, 0:n], start=(c == 0), stop=(c == KD - 1))
                        last.then_inc(acc_ready, 1)
                        unit += 1
                for _, g0, ng, _ in runs:
                    with pe.Fori(0, ng // 2) as i:
                        for h in range(2):
                            slot = (J + h) % 2
                            pe.wait_ge(w_loaded[slot], i * 16 + 16 * ((J + g0 + h) // 2 + 1))
                            for c4 in range(4):
                                u = 4 * (g0 + h) + c4
                                pe.wait_ge(acc_kept, i * 8 + (token_units + u - 1))
                                for c in range(KD):
                                    for b, (a0, a1) in enumerate(SPANS):
                                        last = nc.tensor.matmul(acc[:, u % 2, b, 0:a1 - a0],
                                                                w[:, slot, c, c4 * P:(c4 + 1) * P],
                                                                k.hT[:, c, a0:a1], start=(c == 0), stop=(c == KD - 1))
                                last.then_inc(acc_ready, 1)

            @block.scalar
            def _(act):
                unit = 0
                for i, (c0, n, tiles, to) in enumerate(jobs):
                    for r0, m, t in tiles:
                        act.wait_ge(acc_ready, unit + 1)
                        nc.scalar.activation(to(m, t), acc[0:m, unit % 2, 0, 0:n], ACT.Copy).then_inc(acc_kept, 1)
                        unit += 1
                for _, g0, ng, func in runs:
                    with act.Fori(0, ng // 2) as i:
                        for h in range(2):
                            if g0:
                                act.wait_ge(stored[h], i * 16 + 16 * (g0 // 2))
                            for c4 in range(4):
                                u = 4 * (g0 + h) + c4
                                act.wait_ge(acc_ready, i * 8 + (token_units + u + 1))
                                for b, (a0, a1) in enumerate(SPANS):
                                    last = nc.scalar.activation(out[:, h, c4, a0:a1], acc[:, u % 2, b, 0:a1 - a0], func)
                                last.then_inc(acc_kept, 1)

            @block.gpsimd
            def _(pool):
                for _, g0, ng, _ in runs:
                    with pool.Fori(0, ng // 2) as i:
                        for h in range(2):
                            pool.wait_ge(acc_kept, i * 8 + (token_units + 4 * (g0 + h) + 4))
                            pool.dma_start(projT[bass.ds(i * 2 + (g0 + h), 1)].rearrange("g p c t -> p (g c) t"),
                                           out[:, h]).then_inc(stored[h], 16)
                for h in range(2):
                    pool.wait_ge(stored[h], 16 * 6)
                pool.dma_start(d["latents"][:, :, 0:QL], k.qd[:]).then_inc(latents_out, 16)
                pool.dma_start(d["latents"][:, :, QL:], k.kvd[:]).then_inc(latents_out, 16)
                pool.wait_ge(latents_out, 32)


def convolve(k):
    nc, d = k.nc, k.dram
    with k.scope() as s:
        state_rows = s.sb("cv_state_rows", [3 * NS, 3 * D])
        stateT = s.sb("cv_stateT", [P, GC, 3 * NS])
        x = s.sb("cv_x", [P, 2, ROWS])
        y = s.sb("cv_y", [P, 2, ROWS])
        tail = s.sb("cv_tail", [NS, 3 * D])
        tail_p = s.sb("cv_tail_p", [3, 3 * D])
        norm = s.sb("cv_norm", [P, 2, ROWS])
        state_ps = s.ps("cv_state_ps", [P, 2, BANK])
        tail_ps = s.ps("cv_tail_ps", [NS, 2, BANK])
        sum_ps = s.ps("cv_sum_ps", [P, 3, BANK])
        state_loaded, state_turned, state_kept = s.sem("cv_state_loaded"), s.sem("cv_state_turned"), s.sem("cv_state_kept")
        x_loaded = [s.sem(f"cv_x_loaded{i}") for i in range(2)]
        tap, conv_done, silu_done = s.sem("cv_tap"), s.sem("cv_conv_done"), s.sem("cv_silu_done")
        tail_turned, tail_kept, tails_out = s.sem("cv_tail_turned"), s.sem("cv_tail_kept"), s.sem("cv_tails_out")
        squared, summed, rooted, inverted, normed = (s.sem(f"cv_{n}") for n in (
            "squared", "summed", "rooted", "inverted", "normed"))
        HB = GC // 2

        def w(j, i):
            return k.vecT[:, V_CONV + i * GC + j:V_CONV + i * GC + j + 1]

        def earlier(j, i):
            return stateT[:, j, :].rearrange("p (b r) -> p r b", r=3)[:, i, :]

        with nc.Block() as block:
            @block.sync
            def _(sp):
                sp.dma_start(state_rows[:], d["state_conv"].rearrange("a b r c -> (a b r) c")).then_inc(state_loaded, 16)
                for j in range(GC):
                    if j >= 2:
                        sp.wait_ge(conv_done, j - 1)
                        sp.wait_ge(tail_turned, j - 1)
                    sp.dma_start(x[:, j % 2, :], d["projT"][j]).then_inc(x_loaded[j % 2], 16)
                sp.dma_start(d["new_conv_sample"][0, :, 0:2, :], d["state_conv"][0, :, 1:3, :]).then_inc(tails_out, 16)
                sp.wait_ge(tail_kept, 2 * GC)
                sp.dma_start(d["new_conv_sample"][0, :, 2, :], tail[:]).then_inc(tails_out, 16)
                sp.dma_start(d["new_conv_prompt"][0, 0], tail_p[:]).then_inc(tails_out, 16)
                sp.wait_ge(tails_out, 3 * 16)

            @block.vector
            def _(dve):
                for b in range(2):
                    dve.wait_ge(state_turned, b + 1)
                    nc.vector.tensor_copy(stateT[:, b * HB:(b + 1) * HB, :],
                                          state_ps[:, b, 0:HB * 3 * NS].rearrange("p (j r) -> p j r", j=HB)).then_inc(state_kept, 1)
                dve.wait_ge(state_kept, 2)
                for j in range(GC):
                    xj, yj = x[:, j % 2, :], y[:, j % 2, :]
                    dve.wait_ge(x_loaded[j % 2], 16 * (j // 2 + 1))
                    if j >= 2:
                        dve.wait_ge(silu_done, j - 1)
                    nc.vector.tensor_scalar(yj, xj, w(j, 3), None, ALU.mult).then_inc(tap, 1)
                    for i in range(3):
                        dve.wait_ge(tap, 3 * j + i + 1)
                        back = i + 1
                        nc.vector.scalar_tensor_tensor(out=yj[:, NS + back:], in0=xj[:, NS:ROWS - back], scalar=w(j, 2 - i),
                                                       in1=yj[:, NS + back:], op0=ALU.mult, op1=ALU.add)
                        nc.vector.scalar_tensor_tensor(out=yj[:, 0:NS], in0=earlier(j, 2 - i), scalar=w(j, 2 - i),
                                                       in1=yj[:, 0:NS], op0=ALU.mult, op1=ALU.add).then_inc(
                                                           tap if i < 2 else conv_done, 1)
                for j in range(2 * GH):
                    dve.wait_ge(rooted, j + 1)
                    nc.vector.reciprocal(norm[:, j % 2, :], norm[:, j % 2, :]).then_inc(inverted, 1)
                    dve.wait_ge(inverted, j + 1)
                    nc.vector.scalar_tensor_tensor(out=k.convT[:, j, :], in0=norm[:, j % 2, :],
                                                   scalar=DK ** -0.5 if j < GH else 1.0, in1=k.convT[:, j, :],
                                                   op0=ALU.mult, op1=ALU.mult).then_inc(normed, 1)

            @block.scalar
            def _(act):
                for j in range(GC):
                    act.wait_ge(conv_done, j + 1)
                    nc.scalar.activation(k.convT[:, j, :], y[:, j % 2, :], ACT.Silu).then_inc(silu_done, 1)
                    act.wait_ge(tail_turned, j + 1)
                    nc.scalar.activation(tail[:, j * P:(j + 1) * P], tail_ps[:, j % 2, 0:P], ACT.Copy).then_inc(tail_kept, 1)
                    nc.scalar.activation(tail_p[:, j * P:(j + 1) * P], tail_ps[0:3, j % 2, P:2 * P], ACT.Copy).then_inc(tail_kept, 1)
                act.wait_ge(silu_done, GC)

                def root(j):
                    act.wait_ge(summed, j + 1)
                    if j >= 2:
                        act.wait_ge(normed, j - 1)
                    for b, (a0, a1) in enumerate(SPANS):
                        last = nc.scalar.activation(norm[:, j % 2, a0:a1], sum_ps[:, b, 0:a1 - a0], ACT.Sqrt, bias=k.eps[:])
                    last.then_inc(rooted, 1)

                for j in range(2 * GH):
                    if j >= 2:
                        act.wait_ge(summed, j - 1)
                    nc.scalar.activation(y[:, j % 2, :], k.convT[:, j, :], ACT.Square).then_inc(squared, 1)
                    if j:
                        root(j - 1)
                root(2 * GH - 1)

            @block.tensor
            def _(pe):
                pe.wait_ge(state_loaded, 16)
                for b in range(2):
                    for j in range(HB):
                        last = nc.tensor.transpose(state_ps[:, b, j * 3 * NS:(j + 1) * 3 * NS],
                                                   state_rows[:, (b * HB + j) * P:(b * HB + j + 1) * P],
                                                   k.ident[0:3 * NS, 0:3 * NS])
                    last.then_inc(state_turned, 1)
                for j in range(GC):
                    pe.wait_ge(x_loaded[j % 2], 16 * (j // 2 + 1))
                    if j >= 2:
                        pe.wait_ge(tail_kept, 2 * (j - 1))
                    nc.tensor.transpose(tail_ps[:, j % 2, 0:P], x[:, j % 2, 0:NS], k.ident[:])
                    nc.tensor.transpose(tail_ps[0:3, j % 2, P:2 * P], x[:, j % 2, ROWS - 3:], k.ident[:]).then_inc(tail_turned, 1)
                for j in range(2 * GH):
                    pe.wait_ge(squared, j + 1)
                    if j:
                        pe.wait_ge(rooted, j)
                    for b, (a0, a1) in enumerate(SPANS):
                        last = nc.tensor.matmul(sum_ps[:, b, 0:a1 - a0], k.ones[:], y[:, j % 2, a0:a1], start=True, stop=True)
                    last.then_inc(summed, 1)


def gdn_gates(k):
    nc, d = k.nc, k.dram
    NB = NT + 1
    with k.scope() as s:
        bias = s.sb("gg_bias", [P, GH])
        rate = s.sb("gg_rate", [P, GH])
        v, m, e, l = (s.sb(f"gg_{n}", [P, NB, GH]) for n in ("v", "neg_abs", "exp", "ln"))
        total = s.sb("gg_total", [P, NT, GH])
        g_ps = s.ps("gg_g_ps", [P, NT, GH])
        t_ps = s.ps("gg_t_ps", [P, NT, GH])
        loaded, step, acted = s.sem("gg_loaded"), s.sem("gg_step"), s.sem("gg_acted")
        sums = s.sem("gg_sums")
        sums_kept, diffed = s.sem("gg_sums_kept"), s.sem("gg_diffed")
        with nc.Block() as block:
            @block.sync
            def _(sp):
                sp.dma_start(bias[:], d["dt_bias"][0].partition_broadcast(P)).then_inc(loaded, 16)
                sp.dma_start(rate[:], d["a_log"][0].partition_broadcast(P)).then_inc(loaded, 16)

            @block.vector
            def _(dve):
                link = chained(dve, step)
                dve.wait_ge(loaded, 32)
                link(nc.vector.tensor_tensor(v[:], k.ba[:, :, GH:], bias[:].unsqueeze(1).to_broadcast([P, NB, GH]), ALU.add))
                link(nc.vector.scalar_tensor_tensor(out=m[:], in0=v[:], scalar=-1.0, in1=v[:], op0=ALU.mult, op1=ALU.min))
                link(nc.vector.tensor_scalar(v[:], v[:], 0.0, None, ALU.max))
                dve.wait_ge(acted, 3)
                link(nc.vector.tensor_tensor(v[:], v[:], l[:], ALU.add))
                link(nc.vector.tensor_scalar(rate[:], rate[:], -1.0, None, ALU.mult))
                link(nc.vector.tensor_tensor(k.g[:], v[:], rate[:].unsqueeze(1).to_broadcast([P, NB, GH]), ALU.mult))
                dve.wait_ge(sums, 1)
                nc.vector.tensor_copy(k.G[:], g_ps[:]).then_inc(sums_kept, 1)
                nc.vector.tensor_copy(total[:], t_ps[:]).then_inc(sums_kept, 1)
                dve.wait_ge(sums_kept, 2)
                nc.vector.tensor_tensor(k.left[:], total[:], k.G[:], ALU.subtract).then_inc(diffed, 1)

            @block.scalar
            def _(act):
                act.wait_ge(step, 2)
                nc.scalar.activation(e[:], m[:], ACT.Exp).then_inc(acted, 1)
                act.wait_ge(acted, 1)
                nc.scalar.activation(l[:], e[:], ACT.Ln, bias=k.ones[:, 0:1]).then_inc(acted, 1)
                act.wait_ge(loaded, 32)
                nc.scalar.activation(rate[:], rate[:], ACT.Exp).then_inc(acted, 1)
                act.wait_ge(diffed, 1)
                nc.scalar.activation(k.left[:], k.left[:], ACT.Exp).then_inc(acted, 1)
                nc.scalar.activation(k.total_exp[:], total[:], ACT.Exp).then_inc(acted, 1)
                nc.scalar.activation(k.g_exp[:], k.g[:, NT, :], ACT.Exp).then_inc(acted, 1)
                nc.scalar.activation(k.beta[:], k.ba[:, :, 0:GH], ACT.Sigmoid).then_inc(acted, 1)

            @block.tensor
            def _(pe):
                pe.wait_ge(step, 6)
                nc.tensor.matmul(g_ps[:], k.upto[:], k.g[:, 0:NT, :], start=True, stop=True)
                nc.tensor.matmul(t_ps[:], k.ones[:], k.g[:, 0:NT, :], start=True, stop=True)
                nc.tensor.matmul(g_ps[:, 0, :], k.upto[0:META, :], k.g[0:META, 0, :], start=True, stop=True)
                nc.tensor.matmul(t_ps[:, 0, :], k.ones[0:META, :], k.g[0:META, 0, :], start=True, stop=True).then_inc(sums, 1)


def gdn_prompt(k):
    nc, d = k.nc, k.dram
    with k.scope() as s:
        levels = s.sb("gp_levels", [P, 7, P])
        S = s.sb("gp_state", [P, GH, DK])
        decayed = s.sb("gp_decayed", [P, GH, DK])
        decay, row_exp, kg, qg, LT, attn, ktok, vtok, B, X, Y, M, r, vn, o = (s.sb(f"gp_{n}", [P, GH, P]) for n in (
            "decay", "row_exp", "kg", "qg", "LT", "attn", "ktok", "vtok", "B", "X", "Y", "M", "r", "vn", "o"))
        ps = [s.ps(f"gp_ps{i}", [P, GH, P]) for i in range(4)]
        consts, zeroed = s.sem("gp_consts"), s.sem("gp_zeroed")
        prods, exps, local, scaled_k = s.sem("gp_prods"), s.sem("gp_exps"), s.sem("gp_local"), s.sem("gp_scaled_k")
        turned, ktok_kept, vtok_kept = s.sem("gp_turned"), s.sem("gp_ktok_kept"), s.sem("gp_vtok_kept")
        masked, b_turned, m_done, m_kept, xy_done, x_kept, y_kept = (s.sem(f"gp_{n}") for n in (
            "masked", "b_turned", "m_done", "m_kept", "xy_done", "x_kept", "y_kept"))
        ks_done, r_ready, vn_done, vn_kept, out_done, out_kept, out_stored = (s.sem(f"gp_{n}") for n in (
            "ks_done", "r_ready", "vn_done", "vn_kept", "out_done", "out_kept", "out_stored"))
        upd_done, S_decayed, S_ready, dve_step = (s.sem(f"gp_{n}") for n in ("upd_done", "S_decayed", "S_ready", "dve_step"))
        H2 = GH // 2
        halves = [slice(0, H2), slice(H2, GH)]
        LV = [4] + [7] * (NT - 1)
        UP = [sum(LV[:c]) for c in range(NT + 1)]
        UM = [UP[c] - c for c in range(NT + 1)]

        def cols(c):
            r0, n = CHUNKS[c]
            return slice(r0, r0 + n), n

        with nc.Block() as block:
            @block.sync
            def _(sp):
                sp.dma_start(levels[:], d["c_levels"]).then_inc(consts, 16)
                for c in range(NT):
                    sl, n = cols(c)
                    sp.wait_ge(out_kept, c + 1)
                    sp.dma_start(d["gdnT"][:, :, sl].rearrange("h p t -> p h t"), o[:, :, 0:n]).then_inc(out_stored, 16)
                sp.wait_ge(S_ready, NT)
                sp.dma_start(d["new_gdn_prompt"][0, 0].rearrange("h p v -> p h v"), S[:]).then_inc(out_stored, 16)
                sp.wait_ge(out_stored, 16 * (NT + 1))

            @block.tensor
            def _(pe):
                pe.wait_ge(consts, 16)
                for c in range(NT):
                    sl, n = cols(c)
                    q, kk, v = (k.convT[:, i * GH:(i + 1) * GH, sl] for i in range(3))
                    if c:
                        pe.wait_ge(out_kept, c)
                        pe.wait_ge(S_ready, c)
                        pe.wait_ge(r_ready, c)
                        pe.wait_ge(vn_kept, c)
                    for h in range(GH):
                        nc.tensor.matmul(ps[0][:, h, 0:n], k.g[0:n, c, h:h + 1].to_broadcast([n, P]), k.upto[0:n, 0:n], start=True, stop=True)
                    for h in range(GH):
                        nc.tensor.matmul(ps[2][0:n, h, 0:n], kk[:, h, :], kk[:, h, :], start=True, stop=True)
                    for h in range(GH):
                        nc.tensor.matmul(ps[1][:, h, 0:n], k.beta[0:n, c, h:h + 1].to_broadcast([n, P]), k.ident[0:n, 0:n], start=True, stop=True)
                    for h in range(GH):
                        last = nc.tensor.matmul(ps[3][0:n, h, 0:n], kk[:, h, :], q[:, h, :], start=True, stop=True)
                    last.then_inc(prods, 1)
                    pe.wait_ge(exps, 2 * c + 1)
                    pe.wait_ge(local, 4 * c + 1)
                    for h in range(GH):
                        last = nc.tensor.transpose(ps[0][0:n, h, :], kk[:, h, :], k.ident[:])
                    last.then_inc(turned, 1)
                    pe.wait_ge(local, 4 * c + 4)
                    for h in range(GH):
                        last = nc.tensor.transpose(ps[1][0:n, h, :], v[:, h, :], k.ident[:])
                    last.then_inc(turned, 1)
                    for hv in range(2):
                        pe.wait_ge(masked, UP[c] + 1)
                        for h in range(hv * H2, hv * H2 + H2):
                            last = nc.tensor.transpose(ps[2][0:n, h, 0:n], B[0:n, h, 0:n], k.ident[0:n, 0:n])
                        last.then_inc(b_turned, 1)
                    pe.wait_ge(ktok_kept, c + 1)
                    pe.wait_ge(vtok_kept, c + 1)
                    for l in range(1, LV[c]):
                        u = UM[c] + l - 1
                        for hv in range(2):
                            pe.wait_ge(masked, UP[c] + l + 1)
                            pe.wait_ge(x_kept, 2 * (UP[c] + l - 1) + hv + 1)
                            for h in range(hv * H2, hv * H2 + H2):
                                last = nc.tensor.matmul(ps[3][0:n, h, 0:n], B[0:n, h, 0:n], X[0:n, h, 0:n], start=True, stop=True)
                            last.then_inc(m_done, 1)
                        for hv in range(2):
                            pe.wait_ge(m_kept, 2 * u + hv + 1)
                            pe.wait_ge(y_kept, 2 * (UP[c] + l - 1) + hv + 1)
                            for h in range(hv * H2, hv * H2 + H2):
                                nc.tensor.matmul(ps[2][0:n, h, 0:n], Y[0:n, h, 0:n], M[0:n, h, 0:n], start=True, stop=True)
                            for h in range(hv * H2, hv * H2 + H2):
                                last = nc.tensor.matmul(ps[0][0:n, h, 0:n], M[0:n, h, 0:n], Y[0:n, h, 0:n], start=True, stop=True)
                            last.then_inc(xy_done, 1)
                    pe.wait_ge(scaled_k, 2 * c + 2)
                    if c:
                        pe.wait_ge(S_ready, c)
                    else:
                        pe.wait_ge(zeroed, 1)
                    for h in range(GH):
                        last = nc.tensor.matmul(ps[1][0:n, h, :], kg[:, h, 0:n], S[:, h, :], start=True, stop=True)
                    last.then_inc(ks_done, 1)
                    pe.wait_ge(r_ready, c + 1)
                    pe.wait_ge(y_kept, 2 * UP[c + 1])
                    for h in range(GH):
                        last = nc.tensor.matmul(ps[3][0:n, h, :], Y[0:n, h, 0:n], r[0:n, h, :], start=True, stop=True)
                    last.then_inc(vn_done, 1)
                    pe.wait_ge(vn_kept, c + 1)
                    pe.wait_ge(x_kept, 2 * UP[c + 1])
                    for h in range(GH):
                        last = nc.tensor.matmul(ps[2][:, h, :], ktok[0:n, h, :], vn[0:n, h, :], start=True, stop=True)
                    last.then_inc(upd_done, 1)
                    for h in range(GH):
                        nc.tensor.matmul(ps[0][:, h, 0:n], S[:, h, :], qg[:, h, 0:n], start=True, stop=False)
                        last = nc.tensor.matmul(ps[0][:, h, 0:n], vn[0:n, h, :], attn[0:n, h, 0:n], start=False, stop=True)
                    last.then_inc(out_done, 1)

            @block.vector
            def _(dve):
                nc.vector.memset(S[:], 0.0).then_inc(zeroed, 1)
                dve.wait_ge(consts, 16)
                for c in range(NT):
                    sl, n = cols(c)

                    def bc(ap):
                        return ap.unsqueeze(2).to_broadcast([n, GH, n])

                    upto = k.upto[0:n, 0:n].unsqueeze(1).to_broadcast([n, GH, n])
                    step = 4 * c
                    dve.wait_ge(prods, c + 1)
                    nc.vector.tensor_tensor(decay[0:n, :, 0:n], ps[0][0:n, :, 0:n], bc(k.G[0:n, c, :]), ALU.subtract).then_inc(local, 1)
                    dve.wait_ge(local, step + 1)
                    nc.vector.tensor_scalar(decay[0:n, :, 0:n], decay[0:n, :, 0:n], 0.0, None, ALU.min).then_inc(local, 1)
                    dve.wait_ge(exps, 2 * c + 2)
                    nc.vector.tensor_tensor(LT[0:n, :, 0:n], ps[2][0:n, :, 0:n], decay[0:n, :, 0:n], ALU.mult)
                    nc.vector.tensor_tensor(decay[0:n, :, 0:n], decay[0:n, :, 0:n], upto, ALU.mult).then_inc(local, 1)
                    dve.wait_ge(local, step + 3)
                    nc.vector.tensor_tensor(LT[0:n, :, 0:n], LT[0:n, :, 0:n], ps[1][0:n, :, 0:n], ALU.mult)
                    nc.vector.tensor_tensor(attn[0:n, :, 0:n], decay[0:n, :, 0:n], ps[3][0:n, :, 0:n], ALU.mult).then_inc(local, 1)
                    dve.wait_ge(turned, 2 * c + 1)
                    nc.vector.tensor_tensor(ktok[0:n], ps[0][0:n], k.left[0:n, c, :].unsqueeze(2).to_broadcast([n, GH, P]), ALU.mult).then_inc(ktok_kept, 1)
                    ident = k.ident[0:n, 0:n].unsqueeze(1).to_broadcast([n, H2, n])
                    dve.wait_ge(masked, UP[c] + 1)
                    for hv in range(2):
                        hs = halves[hv]
                        nc.vector.tensor_tensor(Y[0:n, hs, 0:n], ident, B[0:n, hs, 0:n], ALU.subtract).then_inc(y_kept, 1)
                        dve.wait_ge(b_turned, 2 * c + hv + 1)
                        nc.vector.tensor_tensor(X[0:n, hs, 0:n], ident, ps[2][0:n, hs, 0:n], ALU.subtract).then_inc(x_kept, 1)
                    for l in range(1, LV[c]):
                        u = UM[c] + l - 1
                        for hv in range(2):
                            hs = halves[hv]
                            dve.wait_ge(xy_done, 2 * u + hv + 1)
                            nc.vector.tensor_tensor(X[0:n, hs, 0:n], X[0:n, hs, 0:n], ps[2][0:n, hs, 0:n], ALU.subtract).then_inc(x_kept, 1)
                            nc.vector.tensor_tensor(Y[0:n, hs, 0:n], Y[0:n, hs, 0:n], ps[0][0:n, hs, 0:n], ALU.subtract).then_inc(y_kept, 1)
                    dve.wait_ge(ks_done, c + 1)
                    dve.wait_ge(vtok_kept, c + 1)
                    nc.vector.tensor_tensor(r[0:n], vtok[0:n], ps[1][0:n], ALU.subtract).then_inc(dve_step, 1)
                    dve.wait_ge(dve_step, c + 1)
                    nc.vector.tensor_tensor(r[0:n], r[0:n], k.beta[0:n, c, :].unsqueeze(2).to_broadcast([n, GH, P]), ALU.mult).then_inc(r_ready, 1)
                    dve.wait_ge(upd_done, c + 1)
                    dve.wait_ge(out_done, c + 1)
                    dve.wait_ge(S_decayed, c + 1)
                    nc.vector.tensor_tensor(S[:], decayed[:], ps[2][:], ALU.add).then_inc(S_ready, 1)

            @block.gpsimd
            def _(pool):
                pool.wait_ge(consts, 16)
                pool.wait_ge(zeroed, 1)
                for c in range(NT):
                    sl, n = cols(c)
                    pool.wait_ge(local, 4 * c + 4)
                    for l in range(LV[c]):
                        if l == 1:
                            pool.wait_ge(y_kept, 2 * (UP[c] + 1))
                            pool.wait_ge(b_turned, 2 * (c + 1))
                        if l > 1:
                            pool.wait_ge(m_done, 2 * (UM[c] + l - 1))
                        nc.gpsimd.tensor_tensor(B[0:n, :, 0:n], LT[0:n, :, 0:n],
                                                levels[0:n, l, 0:n].unsqueeze(1).to_broadcast([n, GH, n]), ALU.mult).then_inc(masked, 1)
                        if l == 1:
                            pool.wait_ge(exps, 2 * c + 1)
                            for i, to in ((GH, kg), (0, qg)):
                                nc.gpsimd.tensor_tensor(to[:, :, 0:n], k.convT[:, i:i + GH, sl], row_exp[:, :, 0:n], ALU.mult).then_inc(scaled_k, 1)
                        if l == 2:
                            if c:
                                pool.wait_ge(S_ready, c)
                            nc.gpsimd.tensor_tensor(decayed[:], S[:], k.total_exp[:, c, :].unsqueeze(2).to_broadcast([P, GH, DK]), ALU.mult).then_inc(S_decayed, 1)

            @block.scalar
            def _(act):
                for c in range(NT):
                    sl, n = cols(c)
                    act.wait_ge(local, 4 * c + 1)
                    nc.scalar.activation(row_exp[:, :, 0:n], ps[0][:, :, 0:n], ACT.Exp).then_inc(exps, 1)
                    act.wait_ge(local, 4 * c + 2)
                    nc.scalar.activation(decay[0:n, :, 0:n], decay[0:n, :, 0:n], ACT.Exp).then_inc(exps, 1)
                    act.wait_ge(turned, 2 * c + 2)
                    nc.scalar.activation(vtok[0:n], ps[1][0:n], ACT.Copy).then_inc(vtok_kept, 1)
                    for l in range(1, LV[c]):
                        u = UM[c] + l - 1
                        for hv in range(2):
                            hs = halves[hv]
                            act.wait_ge(m_done, 2 * u + hv + 1)
                            nc.scalar.activation(M[0:n, hs, 0:n], ps[3][0:n, hs, 0:n], ACT.Copy).then_inc(m_kept, 1)
                    act.wait_ge(vn_done, c + 1)
                    nc.scalar.activation(vn[0:n], ps[3][0:n], ACT.Copy).then_inc(vn_kept, 1)
                    act.wait_ge(out_done, c + 1)
                    if c:
                        act.wait_ge(out_stored, 16 * c)
                    nc.scalar.activation(o[:, :, 0:n], ps[0][:, :, 0:n], ACT.Copy).then_inc(out_kept, 1)


def gdn_sample(k):
    nc, d = k.nc, k.dram
    W = NS * DK
    with k.scope() as s:
        S = s.sb("gs_state", [P, NS, GH, DK])
        diag = s.sb("gs_diag", [NS, NS, P])
        own = s.sb("gs_own", [NS, NS, P])
        gx = s.sb("gs_gx", [NS, GH, NS])
        gall = s.sb("gs_gall", [P, GH, NS])
        krow, vrow, delta, orow, picked = (s.sb(f"gs_{n}", [NS, P]) for n in ("krow", "vrow", "delta", "orow", "picked"))
        oT = s.sb("gs_oT", [P, GH, NS])
        prod = s.ps("gs_prod", [NS, NS, P])
        upd = s.ps("gs_upd", [P, NS, P])
        rows = s.ps("gs_rows", [P, 4, P])
        gps = s.ps("gs_gps", [P, GH, NS])
        loaded, stored = s.sem("gs_loaded"), s.sem("gs_stored")
        pe_step, dve_step, k_own = s.sem("gs_pe_step"), s.sem("gs_dve_step"), s.sem("gs_own_again")
        PE, DV = 4, 9
        with nc.Block() as block:
            @block.sync
            def _(sp):
                sp.dma_start(S[:], d["state_gdn"][0].rearrange("b h p v -> p b h v")).then_inc(loaded, 16)
                sp.dma_start(diag[:], d["c_diag8"]).then_inc(loaded, 16)
                sp.wait_ge(dve_step, 2 + DV * GH)
                sp.dma_start(d["new_gdn_sample"][0].rearrange("b h p v -> p b h v"), S[:]).then_inc(stored, 16)
                sp.dma_start(d["gdnT"][:, :, 0:NS].rearrange("h p t -> p h t"), oT[:]).then_inc(stored, 16)
                sp.wait_ge(stored, 32)

            @block.tensor
            def _(pe):
                pe.wait_ge(loaded, 32)
                pe.wait_ge(dve_step, 1)
                nc.tensor.matmul(gps[:], k.ones[0:NS, :], gx[:], start=True, stop=True).then_inc(pe_step, 1)
                for h in range(GH):
                    pe.wait_ge(dve_step, 2 + DV * h)
                    nc.tensor.transpose(rows[0:NS, 0, :], k.convT[:, GH + h, 0:NS], k.ident[:])
                    nc.tensor.transpose(rows[0:NS, 1, :], k.convT[:, 2 * GH + h, 0:NS], k.ident[:])
                    for x in range(2):
                        last = nc.tensor.matmul(prod[:, 4 * x:4 * x + 4, :], k.convT[:, GH + h, 0:NS], S[:, 4 * x:4 * x + 4, h, :], start=True, stop=True)
                    last.then_inc(pe_step, 1)
                    pe.wait_ge(dve_step, 2 + DV * h + 6)
                    for x in range(2):
                        last = nc.tensor.matmul(upd[:, 4 * x:4 * x + 4, :], krow[:], own[:, 4 * x:4 * x + 4, :], start=True, stop=True)
                    last.then_inc(pe_step, 1)
                    pe.wait_ge(dve_step, 2 + DV * h + 7)
                    for x in range(2):
                        last = nc.tensor.matmul(prod[:, 4 * x:4 * x + 4, :], k.convT[:, h, 0:NS], S[:, 4 * x:4 * x + 4, h, :], start=True, stop=True)
                    last.then_inc(pe_step, 1)
                    pe.wait_ge(dve_step, 2 + DV * h + 8)
                    nc.tensor.transpose(rows[:, 2, 0:NS], orow[:], k.ident[0:NS, 0:NS]).then_inc(pe_step, 1)

            @block.vector
            def _(dve):
                link = chained(dve, dve_step)
                dve.wait_ge(loaded, 32)
                link(nc.vector.tensor_tensor(gx[:], k.g_exp[0:NS, :].unsqueeze(2).to_broadcast([NS, GH, NS]),
                                             diag[:, :, 0].unsqueeze(1).to_broadcast([NS, GH, NS]), ALU.mult))
                dve.wait_ge(pe_step, 1)
                link(nc.vector.tensor_copy(gall[:], gps[:]))
                for h in range(GH):
                    at = 1 + PE * h
                    dve.wait_ge(pe_step, at + 1)
                    nc.vector.tensor_copy(krow[:], rows[0:NS, 0, :])
                    nc.vector.tensor_copy(vrow[:], rows[0:NS, 1, :])
                    link(nc.vector.tensor_tensor(own[:], prod[:], diag[:], ALU.mult))
                    link(nc.vector.tensor_reduce(picked[:], own[:].rearrange("p b v -> p v b"), AX_X, ALU.add))
                    link(nc.vector.tensor_scalar(picked[:], picked[:], k.g_exp[0:NS, h:h + 1], None, ALU.mult))
                    link(nc.vector.tensor_tensor(delta[:], vrow[:], picked[:], ALU.subtract))
                    link(nc.vector.tensor_scalar(delta[:], delta[:], k.beta[0:NS, NT, h:h + 1], None, ALU.mult))
                    link(nc.vector.tensor_tensor(own[:], delta[:].unsqueeze(1).to_broadcast([NS, NS, P]), diag[:], ALU.mult))
                    dve.wait_ge(pe_step, at + 2)
                    for b in range(NS):
                        last = nc.vector.scalar_tensor_tensor(out=S[:, b, h, :], in0=S[:, b, h, :], scalar=gall[:, h, b:b + 1],
                                                              in1=upd[:, b, :], op0=ALU.mult, op1=ALU.add)
                    link(last)
                    dve.wait_ge(pe_step, at + 3)
                    nc.vector.tensor_tensor(own[:], prod[:], diag[:], ALU.mult).then_inc(k_own, 1)
                    dve.wait_ge(k_own, h + 1)
                    link(nc.vector.tensor_reduce(orow[:], own[:].rearrange("p b v -> p v b"), AX_X, ALU.add))
                    dve.wait_ge(pe_step, at + 4)
                    link(nc.vector.tensor_copy(oT[:, h, :], rows[:, 2, 0:NS]))


def gate_gdn(k):
    nc, d = k.nc, k.dram
    with k.scope() as s:
        o, z, g, sq, m = (s.sb(f"ge_{n}", [P, 2, ROWS]) for n in ("o", "z", "g", "square", "mix"))
        sums = s.ps("ge_sums", [P, 2, 3, BANK])
        loaded = [s.sem(f"ge_loaded{i}") for i in range(2)]
        squared, summed, logged, rooted, step, done = (s.sem(f"ge_{n}") for n in ("squared", "summed", "logged", "rooted", "step", "done"))
        stored = [s.sem(f"ge_stored{i}") for i in range(2)]
        with nc.Block() as block:
            @block.sync
            def _(sp):
                for h in range(GH):
                    if h >= 2:
                        sp.wait_ge(done, h - 1)
                    sp.dma_start(o[:, h % 2, :], d["gdnT"][h]).then_inc(loaded[h % 2], 16)
                    sp.dma_start(z[:, h % 2, :], d["projT"][Z0 + h]).then_inc(loaded[h % 2], 16)
                    sp.dma_start(g[:, h % 2, :], d["projT"][GG0 + h]).then_inc(loaded[h % 2], 16)
                    if h:
                        sp.wait_ge(done, h)
                        sp.dma_start(d["mixT"][h - 1], m[:, (h - 1) % 2, :]).then_inc(stored[(h - 1) % 2], 16)
                sp.wait_ge(done, GH)
                sp.dma_start(d["mixT"][GH - 1], m[:, 1, :]).then_inc(stored[1], 16)
                for i in range(2):
                    sp.wait_ge(stored[i], 16 * GH // 2)

            @block.scalar
            def _(act):
                def root(h):
                    act.wait_ge(summed, h + 1)
                    for b, (a0, a1) in enumerate(SPANS):
                        last = nc.scalar.activation(sq[:, h % 2, a0:a1], sums[:, h % 2, b, 0:a1 - a0], ACT.Ln, bias=k.eps[:], scale=1.0 / DK)
                    last.then_inc(logged, 1)
                    act.wait_ge(logged, h + 1)
                    nc.scalar.activation(sq[:, h % 2, :], sq[:, h % 2, :], ACT.Exp, scale=-0.5).then_inc(rooted, 1)

                for h in range(GH):
                    act.wait_ge(loaded[h % 2], 48 * (h // 2 + 1))
                    if h >= 2:
                        act.wait_ge(done, h - 1)
                    nc.scalar.activation(sq[:, h % 2, :], o[:, h % 2, :], ACT.Square).then_inc(squared, 1)
                    if h:
                        root(h - 1)
                root(GH - 1)

            @block.tensor
            def _(pe):
                for h in range(GH):
                    pe.wait_ge(squared, h + 1)
                    if h >= 2:
                        pe.wait_ge(logged, h - 1)
                    for b, (a0, a1) in enumerate(SPANS):
                        last = nc.tensor.matmul(sums[:, h % 2, b, 0:a1 - a0], k.ones[:], sq[:, h % 2, a0:a1], start=True, stop=True)
                    last.then_inc(summed, 1)

            @block.vector
            def _(dve):
                for h in range(GH):
                    i = h % 2
                    dve.wait_ge(loaded[i], 48 * (h // 2 + 1))
                    dve.wait_ge(squared, h + 1)
                    nc.vector.tensor_tensor(z[:, i], z[:, i], g[:, i], ALU.mult)
                    nc.vector.tensor_scalar(o[:, i], o[:, i], k.vecT[:, V_GDN:V_GDN + 1], None, ALU.mult).then_inc(step, 1)
                    dve.wait_ge(step, 2 * h + 1)
                    nc.vector.tensor_tensor(o[:, i], o[:, i], z[:, i], ALU.mult).then_inc(step, 1)
                    dve.wait_ge(step, 2 * h + 2)
                    dve.wait_ge(rooted, h + 1)
                    if h >= 2:
                        dve.wait_ge(stored[i], 16 * (h // 2))
                    nc.vector.tensor_tensor(m[:, i], o[:, i], sq[:, i], ALU.mult).then_inc(done, 1)


def mla_latents(k):
    nc, d = k.nc, k.dram
    with k.scope() as s:
        rope = k.rope
        qd, kvd = s.sb("ml_qd", [P, NT, QL]), s.sb("ml_kvd", [P, NT, CK])
        wkv = s.sb("ml_wkv", [P, CL])
        pad = s.sb("ml_pad", [P, NT, QK])
        ropeT = s.sb("ml_ropeT", [QK, ROWS])
        square = s.sb("ml_square", [P, QL])
        ss = s.sb("ml_ss", [P, 2, NT])
        t1, t2 = (s.sb(f"ml_t{i}", [P, NT, 2, HALF]) for i in range(2))
        turned = s.ps("ml_turned", [P, 2, 2, BANK])
        loaded, step, acted, turn_done, turn_kept = (s.sem(f"ml_{n}") for n in ("loaded", "step", "acted", "turned", "kept"))
        stored, spread = s.sem("ml_stored"), s.sem("ml_spread")
        rope_kept = s.sem("ml_rope_kept")
        with nc.Block() as block:
            @block.sync
            def _(sp):
                sp.dma_start(qd[:], d["latents"][:, :, 0:QL]).then_inc(loaded, 16)
                sp.dma_start(kvd[:], d["latents"][:, :, QL:]).then_inc(loaded, 16)
                sp.dma_start(rope[:], d["c_rope"]).then_inc(loaded, 16)
                sp.dma_start(wkv[:], d["kv_norm"][0].partition_broadcast(P)).then_inc(loaded, 16)
                sp.wait_ge(step, 7)
                lat, ro = kvd[:, :, 0:CL], pad[:, :, NOPE:QK]
                for name, src, w in (("latent", lat, CL), ("rope", ro, ROPE)):
                    op, os = d[f"new_{name}_prompt"][0, 0], d[f"new_{name}_sample"][0, :, 0, :]
                    sp.dma_start(os, src[0:NS, 0, :]).then_inc(stored, 16)
                    sp.dma_start(op[0:META], src[NS:HEAD_ROWS, 0, :]).then_inc(stored, 16)
                    sp.dma_start(op[META:].rearrange("(t p) c -> p t c", p=P), src[:, 1:, :]).then_inc(stored, 16)
                sp.wait_ge(turn_kept, NT)
                for h in range(HEADS):
                    sp.dma_start(k.keyT[NOPE:QK, h, :], ropeT[NOPE:QK, NS:]).then_inc(spread, 16)
                sp.wait_ge(spread, 16 * HEADS)
                sp.wait_ge(stored, 16 * 6)

            @block.vector
            def _(dve):
                link = chained(dve, step)
                nc.vector.memset(ss[:], 1.0)
                link(nc.vector.memset(pad[:], 0.0))
                dve.wait_ge(loaded, 64)
                x1, x2 = kvd[:, :, CL:CL + HALF], kvd[:, :, CL + HALF:CK]
                cos, sin = rope[:, :, 0:HALF], rope[:, :, HALF:ROPE]
                nc.vector.tensor_tensor(t1[:, :, 0, :], x1, cos, ALU.mult)
                nc.vector.tensor_tensor(t1[:, :, 1, :], x2, cos, ALU.mult)
                nc.vector.tensor_tensor(t2[:, :, 0, :], x2, sin, ALU.mult)
                link(nc.vector.tensor_tensor(t2[:, :, 1, :], x1, sin, ALU.mult))
                nc.vector.tensor_tensor(pad[:, :, NOPE:NOPE + HALF], t1[:, :, 0, :], t2[:, :, 0, :], ALU.subtract)
                link(nc.vector.tensor_tensor(pad[:, :, NOPE + HALF:QK], t1[:, :, 1, :], t2[:, :, 1, :], ALU.add))
                dve.wait_ge(acted, 2 * NT)
                nc.vector.tensor_scalar(ss[:, 0, :], ss[:, 0, :], 1.0 / CL, EPS, ALU.mult, ALU.add)
                link(nc.vector.tensor_scalar(ss[:, 1, :], ss[:, 1, :], 1.0 / QL, EPS, ALU.mult, ALU.add))
                link(nc.vector.reciprocal(ss[:], ss[:]))
                dve.wait_ge(acted, 2 * NT + 1)
                nc.vector.tensor_tensor(qd[:], qd[:], ss[:, 1, :].unsqueeze(2).to_broadcast([P, NT, QL]), ALU.mult)
                link(nc.vector.tensor_tensor(kvd[:, :, 0:CL], kvd[:, :, 0:CL], ss[:, 0, :].unsqueeze(2).to_broadcast([P, NT, CL]), ALU.mult))
                link(nc.vector.tensor_tensor(kvd[:, :, 0:CL], kvd[:, :, 0:CL], wkv[:].unsqueeze(1).to_broadcast([P, NT, CL]), ALU.mult))
                nc.vector.tensor_copy(k.new_row[:, 0:CL], kvd[0:NS, 0, 0:CL])
                nc.vector.tensor_copy(k.new_row[:, CL:CK], pad[0:NS, 0, NOPE:QK])
                for t, (r0, n) in enumerate(TILES):
                    dve.wait_ge(turn_done, t + 1)
                    bank = turned[:, t % 2]
                    nc.vector.tensor_copy(k.latT[:, :, r0:r0 + n], bank[:, 0, 0:2 * P].rearrange("p (c r) -> p c r", c=2)[:, :, 0:n])
                    nc.vector.tensor_copy(ropeT[:, r0:r0 + n], bank[0:QK, 0, 2 * P:2 * P + n])
                    nc.vector.tensor_tensor(k.qlT[:, :, r0:r0 + n], bank[:, 1, 0:KQ * P].rearrange("p (c r) -> p c r", c=KQ)[:, :, 0:n],
                                            k.vecT[:, V_Q:V_GDN].unsqueeze(2).to_broadcast([P, KQ, n]), ALU.mult).then_inc(turn_kept, 1)

            @block.scalar
            def _(act):
                act.wait_ge(step, 1)
                act.wait_ge(loaded, 64)
                at = 0
                for t, (r0, n) in enumerate(TILES):
                    for i, (src, w) in enumerate(((kvd, CL), (qd, QL))):
                        if at:
                            act.wait_ge(acted, at)
                        nc.scalar.activation(square[0:n, 0:w], src[0:n, t, 0:w], ACT.Square, accum_out=ss[0:n, i, t:t + 1]).then_inc(acted, 1)
                        at += 1
                act.wait_ge(step, 5)
                nc.scalar.activation(ss[:], ss[:], ACT.Sqrt).then_inc(acted, 1)

            @block.tensor
            def _(pe):
                pe.wait_ge(step, 7)
                for t, (r0, n) in enumerate(TILES):
                    if t >= 2:
                        pe.wait_ge(turn_kept, t - 1)
                    bank, eye = turned[:, t % 2], k.ident[0:n, 0:n]
                    for c in range(2):
                        nc.tensor.transpose(bank[:, 0, c * P:c * P + n], kvd[0:n, t, c * P:(c + 1) * P], eye)
                    nc.tensor.transpose(bank[0:QK, 0, 2 * P:2 * P + n], pad[0:n, t, :], eye)
                    for c in range(KQ):
                        last = nc.tensor.transpose(bank[:, 1, c * P:c * P + n], qd[0:n, t, c * P:(c + 1) * P], eye)
                    last.then_inc(turn_done, 1)


def mla_keys_values(k):
    nc, d = k.nc, k.dram
    KSP = [(0, 512), (512, 1024), (1024, PROMPT)]
    with k.scope() as s:
        wuk = s.sb("kv_wuk", [P, 2, HEADS * NOPE])
        wuv = s.sb("kv_wuv", [P, 2, D])
        acc = s.ps("kv_acc", [P, 2, 3, BANK])
        loaded, made, kept = s.sem("kv_loaded"), s.sem("kv_made"), s.sem("kv_kept")
        with nc.Block() as block:
            @block.sync
            def _(sp):
                sp.dma_start(wuk[:], d["w_uk"][0].rearrange("(c p) h n -> p c (h n)", p=P)).then_inc(loaded, 16)
                sp.dma_start(wuv[:], d["w_uv"][0].rearrange("(c p) h n -> p c (h n)", p=P)).then_inc(loaded, 16)

            @block.tensor
            def _(pe):
                pe.wait_ge(loaded, 32)
                for u in range(HEADS + NT):
                    if u >= 2:
                        pe.wait_ge(kept, u - 1)
                    if u < HEADS:
                        for c in range(2):
                            for b, (a0, a1) in enumerate(KSP):
                                last = nc.tensor.matmul(acc[0:NOPE, u % 2, b, 0:a1 - a0], wuk[:, c, u * NOPE:(u + 1) * NOPE],
                                                        k.latT[:, c, NS + a0:NS + a1], start=(c == 0), stop=(c == 1))
                    else:
                        r0, n = CHUNKS[u - HEADS]
                        for c in range(2):
                            for b in range(2):
                                last = nc.tensor.matmul(acc[0:n, u % 2, b, :], k.latT[:, c, r0:r0 + n],
                                                        wuv[:, c, b * BANK:(b + 1) * BANK], start=(c == 0), stop=(c == 1))
                    last.then_inc(made, 1)

            def keep(eng, copy, mine):
                for u in range(HEADS + NT):
                    if u % 2 == mine:
                        eng.wait_ge(made, u + 1)
                        if u >= 1:
                            eng.wait_ge(kept, u)
                        if u < HEADS:
                            for b, (a0, a1) in enumerate(KSP):
                                last = copy(k.keyT[0:NOPE, u, a0:a1], acc[0:NOPE, u % 2, b, 0:a1 - a0])
                        else:
                            n = CHUNKS[u - HEADS][1]
                            last = copy(k.val[0:n, u - HEADS, :].rearrange("p (b n) -> p b n", b=2), acc[0:n, u % 2, 0:2, :])
                        last.then_inc(kept, 1)

            @block.vector
            def _(dve):
                keep(dve, nc.vector.tensor_copy, 0)

            @block.scalar
            def _(act):
                keep(act, nc.scalar.copy, 1)


def attend_prompt(k):
    nc, d = k.nc, k.dram
    with k.scope() as s:
        wuq = s.sb("at_wuq", [P, KQ, HEADS * QK])
        future = s.sb("at_future", [P, P])
        q = s.sb("at_q", [P, HEADS, QK])
        t1, t2 = (s.sb(f"at_t{i}", [P, HEADS, 2, HALF]) for i in range(2))
        qT = s.sb("at_qT", [QK, HEADS, P])
        gm = s.sb("at_gm", [P, KD, P])
        mix = s.sb("at_mix", [P, KD, P])
        p = s.sb("at_p", [P, 2, PROMPT])
        pT = s.sb("at_pT", [P, 3, 4, P])
        og = s.sb("at_og", [P, P])
        zero = s.sb("at_zero", [P, D])
        mx, nm, l, il = (s.sb(f"at_{n}", [P, 2]) for n in ("mx", "nm", "l", "il"))
        sc = s.ps("at_sc", [P, 3, BANK])
        scf = sc[:].rearrange("p b n -> p (b n)")
        tp = s.ps("at_tp", [P, 3, 4, P])
        op = s.ps("at_op", [P, 2, BANK])
        loaded, gm_loaded, mix_stored = s.sem("at_loaded"), s.sem("at_gm_loaded"), s.sem("at_mix_stored")
        q_made, q_kept, roped, q_turned, qT_kept = (s.sem(f"at_{n}") for n in ("q_made", "q_kept", "roped", "q_turned", "qT_kept"))
        zero_made, zeroed = s.sem("at_zero_made"), s.sem("at_zeroed")
        scored, maxed, negated, expd, inverted, normed = (s.sem(f"at_{n}") for n in ("scored", "maxed", "negated", "expd", "inverted", "normed"))
        masked, p_turned, pT_kept, valued, gated, rotated, mixed = (s.sem(f"at_{n}") for n in ("masked", "p_turned", "pT_kept", "valued", "gated", "rotated", "mixed"))
        groups = []
        first = []
        for t in range(NT):
            for h in range(HEADS):
                first.append(len(groups))
                groups += [(t * HEADS + h, a, min(a + 4, t + 1)) for a in range(0, t + 1, 4)]
        first.append(len(groups))
        U = NT * HEADS

        def shape(u):
            t, h = divmod(u, HEADS)
            r0, n = CHUNKS[t]
            return t, h, r0, n, META + P * t

        def keys(j):
            return (0, META) if j == 0 else (META + P * (j - 1), P)

        with nc.Block() as block:
            @block.sync
            def _(sp):
                sp.dma_start(wuq[:], d["w_uq"][0].rearrange("(c p) h n -> p c (h n)", p=P)).then_inc(loaded, 16)
                sp.dma_start(future[:], d["c_future"]).then_inc(loaded, 16)
                for t in range(NT):
                    r0, n = CHUNKS[t]
                    sp.dma_start(gm[:, :, 0:n], d["projT"][GM0:GM0 + KD, :, r0:r0 + n].rearrange("c p r -> p c r")).then_inc(gm_loaded, 16)
                    sp.dma_start(mix[:, :, 0:n], d["mixT"][:, :, r0:r0 + n].rearrange("c p r -> p c r")).then_inc(gm_loaded, 16)
                    sp.wait_ge(mixed, 2 * KD * (t + 1))
                    sp.dma_start(d["mixT"][:, :, r0:r0 + n].rearrange("c p r -> p c r"), mix[:, :, 0:n]).then_inc(mix_stored, 16)
                    sp.wait_ge(mix_stored, 16 * (t + 1))

            @block.gpsimd
            def _(pool):
                nc.gpsimd.memset(zero[:], 0.0).then_inc(zero_made, 1)
                pool.wait_ge(zero_made, 1)
                with pool.Fori(2 * ROWS // P, BLOCKS) as b:
                    pool.dma_start(d["expert_out"][bass.ds(b * P, P), :], zero[:]).then_inc(zeroed, 16)
                pool.wait_ge(zeroed, 16 * (BLOCKS - 2 * ROWS // P))

            @block.tensor
            def _(pe):
                def queries(t):
                    r0, n = TILES[t]
                    if t:
                        pe.wait_ge(expd, HEADS * t)
                    for b in range(3):
                        for c in range(KQ):
                            last = nc.tensor.matmul(sc[0:n, b, :], k.qlT[:, c, r0:r0 + n], wuq[:, c, b * BANK:(b + 1) * BANK],
                                                    start=(c == 0), stop=(c == KQ - 1))
                    last.then_inc(q_made, 1)

                def turn_queries(t):
                    r0, n = TILES[t]
                    pe.wait_ge(roped, t + 1)
                    for g in range(4):
                        at = 4 * t + g
                        if at >= 2:
                            pe.wait_ge(qT_kept, at - 1)
                        for x in range(4):
                            last = nc.tensor.transpose(op[0:QK, g % 2, x * P:x * P + n], q[0:n, 4 * g + x, :], k.ident[0:n, 0:n])
                        last.then_inc(q_turned, 1)

                def scores(u):
                    t, h, r0, n, kl = shape(u)
                    q0 = NS if t == 0 else 0
                    if h:
                        pe.wait_ge(expd, u)
                    else:
                        pe.wait_ge(qT_kept, 4 * (t + 1))
                        pe.wait_ge(q_kept, t + 1)
                    for a0 in range(0, kl, BANK):
                        a1 = min(a0 + BANK, kl)
                        last = nc.tensor.matmul(scf[0:n, a0:a1], qT[:, h, q0:q0 + n], k.keyT[0:QK, h, a0:a1], start=True, stop=True)
                    last.then_inc(scored, 1)

                def values(u):
                    t, h, r0, n, kl = shape(u)
                    pe.wait_ge(normed, u + 1)
                    mine = range(first[u], first[u + 1])
                    for g in mine:
                        if g >= 3:
                            pe.wait_ge(pT_kept, g - 2)
                        for j in range(groups[g][1], groups[g][2]):
                            k0, kn = keys(j)
                            last = nc.tensor.transpose(tp[0:kn, g % 3, j - groups[g][1], 0:n], p[0:n, u % 2, k0:k0 + kn], k.ident[0:n, 0:n])
                        last.then_inc(p_turned, 1)
                    if u >= 2:
                        pe.wait_ge(gated, u - 1)
                    for g in mine:
                        pe.wait_ge(pT_kept, g + 1)
                        for j in range(groups[g][1], groups[g][2]):
                            kn = keys(j)[1]
                            last = nc.tensor.matmul(op[:, u % 2, 0:n], k.val[0:kn, j, (h // 2) * P:(h // 2 + 1) * P],
                                                    pT[0:kn, g % 3, j - groups[g][1], 0:n], start=(j == 0), stop=(j == t))
                    last.then_inc(valued, 1)

                pe.wait_ge(loaded, 32)
                for t in range(NT):
                    queries(t)
                    if t:
                        values(t * HEADS - 1)
                        pe.wait_ge(gated, t * HEADS)
                    turn_queries(t)
                    for h in range(HEADS):
                        scores(t * HEADS + h)
                        if h:
                            values(t * HEADS + h - 1)
                values(U - 1)

            @block.vector
            def _(dve):
                def rotate(t):
                    n = TILES[t][1]
                    cos = k.rope[0:n, t, 0:HALF].unsqueeze(1).to_broadcast([n, HEADS, HALF])
                    sin = k.rope[0:n, t, HALF:ROPE].unsqueeze(1).to_broadcast([n, HEADS, HALF])
                    x1, x2 = q[0:n, :, NOPE:NOPE + HALF], q[0:n, :, NOPE + HALF:QK]
                    dve.wait_ge(q_kept, t + 1)
                    nc.vector.tensor_tensor(t1[0:n, :, 0, :], x1, cos, ALU.mult)
                    nc.vector.tensor_tensor(t1[0:n, :, 1, :], x2, cos, ALU.mult)
                    nc.vector.tensor_tensor(t2[0:n, :, 0, :], x2, sin, ALU.mult)
                    nc.vector.tensor_tensor(t2[0:n, :, 1, :], x1, sin, ALU.mult).then_inc(rotated, 1)
                    dve.wait_ge(rotated, t + 1)
                    nc.vector.tensor_tensor(x1, t1[0:n, :, 0, :], t2[0:n, :, 0, :], ALU.subtract)
                    nc.vector.tensor_tensor(x2, t1[0:n, :, 1, :], t2[0:n, :, 1, :], ALU.add).then_inc(roped, 1)

                def softmax_max(u):
                    t, h, r0, n, kl = shape(u)
                    i = u % 2
                    dve.wait_ge(scored, u + 1)
                    diag = scf[0:n, kl - n:kl]
                    nc.vector.tensor_tensor(diag, diag, future[0:n, 0:n], ALU.add).then_inc(masked, 1)
                    dve.wait_ge(masked, u + 1)
                    nc.vector.reduce_max(mx[0:n, i:i + 1], scf[0:n, 0:kl], AX_X).then_inc(maxed, 1)
                    dve.wait_ge(maxed, u + 1)
                    nc.vector.tensor_scalar(nm[0:n, i:i + 1], mx[0:n, i:i + 1], -MLA_SCALE, None, ALU.mult).then_inc(negated, 1)

                def normalise(u):
                    t, h, r0, n, kl = shape(u)
                    i = u % 2
                    dve.wait_ge(expd, u + 1)
                    nc.vector.reciprocal(il[0:n, i:i + 1], l[0:n, i:i + 1]).then_inc(inverted, 1)
                    dve.wait_ge(inverted, u + 1)
                    nc.vector.tensor_scalar(p[0:n, i, 0:kl], p[0:n, i, 0:kl], il[0:n, i:i + 1], None, ALU.mult).then_inc(normed, 1)

                def gate(u):
                    t, h, r0, n, kl = shape(u)
                    half = slice(NOPE * (h % 2), NOPE * (h % 2) + NOPE)
                    dve.wait_ge(valued, u + 1)
                    dve.wait_ge(gm_loaded, 32 * (t + 1))
                    nc.vector.tensor_tensor(og[half, 0:n], op[half, u % 2, 0:n], gm[half, h // 2, 0:n], ALU.mult).then_inc(gated, 1)
                    dve.wait_ge(gated, u + 1)
                    nc.vector.tensor_tensor(mix[half, h // 2, 0:n], mix[half, h // 2, 0:n], og[half, 0:n], ALU.add).then_inc(mixed, 1)

                for u in range(U):
                    t, h = divmod(u, HEADS)
                    if h == 0:
                        if t:
                            gate(u - 1)
                        rotate(t)
                    softmax_max(u)
                    normalise(u)
                    if h:
                        gate(u - 1)
                gate(U - 1)

            @block.scalar
            def _(act):
                for u in range(U):
                    t, h, r0, n, kl = shape(u)
                    i = u % 2
                    if h == 0:
                        m = TILES[t][1]
                        act.wait_ge(q_made, t + 1)
                        if t:
                            act.wait_ge(q_turned, 4 * t)
                        nc.scalar.copy(q[0:m].rearrange("p h d -> p (h d)"), scf[0:m, :]).then_inc(q_kept, 1)
                        for g in range(4):
                            act.wait_ge(q_turned, 4 * t + g + 1)
                            src = op[0:QK, g % 2, :].rearrange("p (x r) -> p x r", x=4)[:, :, 0:m]
                            nc.scalar.copy(qT[:, 4 * g:4 * g + 4, 0:m], src).then_inc(qT_kept, 1)
                        if t == 0:
                            act.wait_ge(qT_kept, 4)
                            nc.scalar.copy(k.q0T[:], qT[:, :, 0:NS])
                    act.wait_ge(negated, u + 1)
                    if u >= 2:
                        act.wait_ge(p_turned, first[u - 1])
                    nc.scalar.activation(p[0:n, i, 0:kl], scf[0:n, 0:kl], ACT.Exp, bias=nm[0:n, i:i + 1], scale=MLA_SCALE,
                                         accum_out=l[0:n, i:i + 1]).then_inc(expd, 1)

                    def keep_turned(v):
                        for g in range(first[v], first[v + 1]):
                            x0, x1 = groups[g][1:]
                            m = shape(v)[3]
                            act.wait_ge(p_turned, g + 1)
                            if g >= 3:
                                act.wait_ge(valued, groups[g - 3][0] + 1)
                            if x0 == 0:
                                last = nc.scalar.copy(pT[0:META, g % 3, 0, 0:m], tp[0:META, g % 3, 0, 0:m])
                            lo = max(x0, 1)
                            if x1 > lo:
                                last = nc.scalar.copy(pT[:, g % 3, lo - x0:x1 - x0, 0:m], tp[:, g % 3, lo - x0:x1 - x0, 0:m])
                            last.then_inc(pT_kept, 1)

                    if h:
                        keep_turned(u - 1)
                    if h == HEADS - 1:
                        keep_turned(u)


def attend_sample(k):
    nc, d = k.nc, k.dram
    G = PAGES // 4
    W = HEADS
    STRIP = P + W
    with k.scope() as s:
        table = s.sb("as_table", [1, NS * PAGES], I32)
        wuk = s.sb("as_wuk", [P, 2, HEADS * NOPE])
        wuv = s.sb("as_wuv", [P, 2, D])
        wukT = s.sb("as_wukT", [NOPE, HEADS, CL])
        rep, pick = s.sb("as_rep", [NS, P]), s.sb("as_pick", [P, NS])
        qrp = s.sb("as_qrp", [QK, NS, W])
        qr4 = s.sb("as_qr4", [P, P])
        qlat = s.sb("as_qlat", [P, 2, P])
        qz = s.sb("as_qz", [P, 2, NS * STRIP])
        qzr = s.sb("as_qzr", [P, 4, NS * STRIP])
        lat = s.sb("as_lat", [P, 2, NS, 4 * CL])
        rop = s.sb("as_rop", [P, 2, NS, 4 * ROPE])
        cT = s.sb("as_cT", [P, 2, 2, BANK])
        rT = s.sb("as_rT", [P, 2, P])
        pr = s.sb("as_p", [P, BANK])
        pz = s.sb("as_pz", [P, 4, NS * STRIP])
        acc = s.sb("as_acc", [P, CL])
        m, nm, corr, rs = (s.sb(f"as_{n}", [P, 2]) for n in ("m", "nm", "corr", "rs"))
        smax, l, snew, pnew = (s.sb(f"as_{n}", [P, 1]) for n in ("smax", "l", "snew", "pnew"))
        newT = s.sb("as_newT", [P, 3, NS])
        picked = s.sb("as_picked", [P, NS])
        accT = s.sb("as_accT", [P, 2, P])
        gm, mix, og = (s.sb(f"as_{n}", [P, KD, NS]) for n in ("gm", "mix", "og"))
        tp = s.ps("as_tp", [P, 2, 3, BANK])
        sp_ = s.ps("as_s", [P, BANK])
        vp = s.ps("as_v", [P, BANK])
        loaded, setup, set_pe, repl = s.sem("as_loaded"), s.sem("as_setup"), s.sem("as_set_pe"), s.sem("as_repl")
        pages = [s.sem(f"as_pages{i}") for i in range(2)]
        turned, kept_a, kept_v, unit_done = (s.sem(f"as_{n}") for n in ("turned", "kept_a", "kept_v", "unit_done"))
        cleared = s.sem("as_cleared")
        maxed, negated, expd, p_turned, pz_kept, pv_done, acc_kept = (s.sem(f"as_{n}") for n in (
            "maxed", "negated", "expd", "p_turned", "pz_kept", "pv_done", "acc_kept"))
        fin_v, fin_a, fin_p, stored = (s.sem(f"as_fin_{n}") for n in ("v", "a", "p", "stored"))

        def strips(ap):
            return ap.rearrange("p (b x) -> p b x", x=STRIP)[:, :, 0:W]

        def turns(eng, body):
            body(0, 0, True)
            body(1, 1, False)
            with eng.Fori(1, G // 2) as i:
                body(i * 2, 0, False)
                body(i * 2 + 1, 1, False)

        with nc.Block() as block:
            @block.sync
            def _(sp):
                sp.dma_start(table[:], d["page_table"].rearrange("(a b) n -> a (b n)", a=1)).then_inc(loaded, 16)
                sp.dma_start(wuk[:], d["w_uk"][0].rearrange("(c p) h n -> p c (h n)", p=P)).then_inc(loaded, 16)
                sp.dma_start(wuv[:], d["w_uv"][0].rearrange("(c p) h n -> p c (h n)", p=P)).then_inc(loaded, 16)
                sp.dma_start(rep[:], d["c_rep16"]).then_inc(loaded, 16)
                sp.dma_start(pick[:], d["c_pick16"]).then_inc(loaded, 16)
                sp.dma_start(gm[:], d["projT"][GM0:GM0 + KD, :, 0:NS].rearrange("c p r -> p c r")).then_inc(loaded, 16)
                sp.dma_start(mix[:], d["mixT"][:, :, 0:NS].rearrange("c p r -> p c r")).then_inc(loaded, 16)
                sp.wait_ge(loaded, 16 * 7)

                def group(j, x, first):
                    if not isinstance(j, int):
                        sp.wait_ge(pv_done, j - 1)
                    for b in range(NS):
                        for i in range(4):
                            page = sp.value_load(table[0:1, bass.ds(j * 4 + (b * PAGES + i), 1)], min_val=0,
                                                 max_val=d["cache_k_rope"].shape[1] - 1)
                            rows = slice(32 * i, 32 * i + 32)
                            sp.dma_start(lat[rows, x, b, :], d["cache_kv_latent"][0, bass.ds(page, 1)].rearrange(
                                "g (q r) c -> q (g r c)", r=4)).then_inc(pages[x], 16)
                            sp.dma_start(rop[rows, x, b, :], d["cache_k_rope"][0, bass.ds(page, 1)].rearrange(
                                "g (q r) c -> q (g r c)", r=4)).then_inc(pages[x], 16)

                turns(sp, group)
                sp.wait_ge(fin_v, 13)
                sp.dma_start(d["mixT"][:, :, 0:NS].rearrange("c p r -> p c r"), mix[:]).then_inc(stored, 16)
                sp.wait_ge(stored, 16)

            @block.gpsimd
            def _(pool):
                nc.gpsimd.memset(qz[:], 0.0)
                nc.gpsimd.memset(qzr[:], 0.0)
                nc.gpsimd.memset(pz[:], 0.0)
                nc.gpsimd.memset(acc[:], 0.0)
                nc.gpsimd.memset(l[:], 0.0)
                nc.gpsimd.memset(m[:], NEG).then_inc(cleared, 1)
                pool.wait_ge(setup, 1)
                for r in range(4):
                    pool.dma_start(qr4[32 * r:32 * r + 32, :], qrp[NOPE:QK].rearrange("p b h -> p (b h)")).then_inc(repl, 16)

            @block.tensor
            def _(pe):
                pe.wait_ge(loaded, 16 * 7)
                for u in range(8):
                    if u >= 2:
                        pe.wait_ge(setup, u)
                    for x in range(4):
                        h, c = 2 * u + x // 2, x % 2
                        last = nc.tensor.transpose(tp[0:NOPE, u % 2, 0, x * P:(x + 1) * P], wuk[:, c, h * NOPE:(h + 1) * NOPE], k.ident[:])
                    last.then_inc(set_pe, 1)
                pe.wait_ge(setup, 9)
                for c in range(2):
                    for h in range(HEADS):
                        nc.tensor.matmul(vp[:, c * P + h:(c + 1) * P:W], wukT[:, h, c * P:(c + 1) * P], k.q0T[0:NOPE, h, :], start=True, stop=True)
                nc.tensor.transpose(vp[:, 256:256 + NS], k.new_row[:, 0:P], k.ident[0:NS, 0:NS])
                nc.tensor.transpose(vp[:, 264:264 + NS], k.new_row[:, P:2 * P], k.ident[0:NS, 0:NS])
                nc.tensor.transpose(vp[0:ROPE, 272:272 + NS], k.new_row[:, CL:CK], k.ident[0:NS, 0:NS]).then_inc(set_pe, 1)
                pe.wait_ge(setup, 11)

                def finish(j):
                    pe.wait_ge(expd, j * 2 + 2)
                    pe.wait_ge(acc_kept, j)
                    for r in range(4):
                        last = nc.tensor.transpose(vp[:, r * P:(r + 1) * P], pr[:, r * P:(r + 1) * P], k.ident[:])
                    last.then_inc(p_turned, 1)

                def products(j, x):
                    pe.wait_ge(pz_kept, j + 1)
                    for b in range(NS):
                        for r in range(4):
                            last = nc.tensor.matmul(vp[:, 0:CL], pz[:, r, b * P:(b + 1) * P], lat[:, x, b, r * CL:(r + 1) * CL],
                                                    start=(b == 0 and r == 0), stop=(b == NS - 1 and r == 3))
                    last.then_inc(pv_done, 1)

                def group(j, x, first):
                    def turn(b):
                        if b >= 2 or not first:
                            pe.wait_ge(kept_a, j * 8 + (b - 1))
                            pe.wait_ge(kept_v, j * 8 + (b - 1))
                        bank = tp[:, b % 2]
                        for c in range(2):
                            for r in range(4):
                                nc.tensor.transpose(bank[:, c, r * P:(r + 1) * P], lat[:, x, b, r * CL + c * P:r * CL + (c + 1) * P], k.ident[:])
                        nc.tensor.transpose(bank[:, 2, 0:P], rop[:, x, b, :], k.ident[:]).then_inc(turned, 1)

                    def score(b):
                        pe.wait_ge(kept_a, j * 8 + (b + 1))
                        pe.wait_ge(kept_v, j * 8 + (b + 1))
                        if b == 0 and not first:
                            pe.wait_ge(expd, j * 2)
                        for c in range(2):
                            nc.tensor.matmul(sp_[:], qz[:, c, b * P:(b + 1) * P], cT[:, b % 2, c, :],
                                             start=(b == 0 and c == 0), stop=False, skip_group_check=True)
                        for r in range(4):
                            last = nc.tensor.matmul(sp_[:, r * P:(r + 1) * P], qzr[:, r, b * P:(b + 1) * P], rT[:, b % 2, :], start=False,
                                                    stop=(b == NS - 1), skip_group_check=True)
                        last.then_inc(unit_done, 1)

                    pe.wait_ge(pages[x], (j - x) * (1024 // 2) + 1024)
                    turn(0)
                    for b in range(NS):
                        if b < NS - 1:
                            turn(b + 1)
                        score(b)
                        if b == 1 and not first:
                            finish(j - 1)
                        if b == 2 and not first:
                            products(j - 1, 1 - x)

                turns(pe, group)
                finish(G - 1)
                products(G - 1, (G - 1) % 2)
                pe.wait_ge(acc_kept, G)
                for c in range(2):
                    nc.tensor.matmul(vp[:, 0:NS], qlat[:, c, :], newT[:, c, :], start=(c == 0), stop=False)
                nc.tensor.matmul(vp[:, 0:NS], qr4[0:ROPE, :], newT[0:ROPE, 2, :], start=False, stop=True)
                nc.tensor.matmul(sp_[:, 0:CL], rep[:], k.new_row[:, 0:CL], start=True, stop=True).then_inc(fin_p, 1)
                pe.wait_ge(fin_v, 10)
                for c in range(2):
                    last = nc.tensor.transpose(vp[:, c * P:(c + 1) * P], acc[:, c * P:(c + 1) * P], k.ident[:])
                last.then_inc(fin_p, 1)
                pe.wait_ge(fin_v, 11)
                for h in range(HEADS):
                    for c in range(2):
                        last = nc.tensor.matmul(sp_[:, h * NS:(h + 1) * NS], wuv[:, c, (h // 2) * P:(h // 2 + 1) * P],
                                                accT[:, c, h::W], start=(c == 0), stop=(c == 1))
                last.then_inc(fin_p, 1)

            @block.vector
            def _(dve):
                nc.vector.tensor_copy(qrp[NOPE:QK].rearrange("p b h -> p h b"), k.q0T[NOPE:QK]).then_inc(setup, 1)
                for u in range(8):
                    dve.wait_ge(set_pe, u + 1)
                    nc.vector.tensor_copy(wukT[:, 2 * u:2 * u + 2, :], tp[0:NOPE, u % 2, 0, :].rearrange("p (h c) -> p h c", h=2)).then_inc(setup, 1)
                dve.wait_ge(set_pe, 9)
                dve.wait_ge(cleared, 1)
                dve.wait_ge(repl, 64)
                nc.vector.tensor_copy(qlat[:], vp[:, 0:2 * P].rearrange("p (c x) -> p c x", c=2)).then_inc(setup, 1)
                nc.vector.tensor_copy(newT[:, 0:2, :], vp[:, 256:272].rearrange("p (c x) -> p c x", c=2))
                nc.vector.tensor_copy(newT[0:ROPE, 2, :], vp[0:ROPE, 272:280])
                for c in range(2):
                    nc.vector.tensor_copy(strips(qz[:, c, :]), vp[:, c * P:(c + 1) * P].rearrange("p (b h) -> p b h", h=W))
                for r in range(4):
                    rows = slice(32 * r, 32 * r + 32)
                    last = nc.vector.tensor_copy(strips(qzr[rows, r, :]), qr4[rows].rearrange("p (b h) -> p b h", h=W))
                last.then_inc(setup, 1)

                def finish(j, x):
                    dve.wait_ge(p_turned, j + 1)
                    for r in range(4):
                        last = nc.vector.tensor_copy(strips(pz[:, r, :]), vp[:, r * P:(r + 1) * P].rearrange("p (b h) -> p b h", h=W))
                    last.then_inc(pz_kept, 1)
                    nc.vector.scalar_tensor_tensor(out=l[:], in0=l[:], scalar=corr[:, x:x + 1], in1=rs[:, x:x + 1], op0=ALU.mult, op1=ALU.add)

                def collect(j, x):
                    dve.wait_ge(pv_done, j + 1)
                    nc.vector.scalar_tensor_tensor(out=acc[:], in0=acc[:], scalar=corr[:, x:x + 1], in1=vp[:, 0:CL],
                                                   op0=ALU.mult, op1=ALU.add).then_inc(acc_kept, 1)

                def group(j, x, first):
                    for b in range(NS):
                        dve.wait_ge(turned, j * 8 + (b + 1))
                        if b >= 2 or not first:
                            dve.wait_ge(unit_done, j * 8 + (b - 1))
                        nc.vector.tensor_copy(cT[:, b % 2, 1, :], tp[:, b % 2, 1, :])
                        nc.vector.tensor_copy(rT[:, b % 2, :], tp[:, b % 2, 2, 0:P]).then_inc(kept_v, 1)
                        if b == 2 and not first:
                            finish(j - 1, 1 - x)
                        if b == 3 and not first:
                            collect(j - 1, 1 - x)
                    dve.wait_ge(unit_done, j * 8 + 8)
                    nc.vector.reduce_max(smax[:], sp_[:], AX_X).then_inc(maxed, 1)
                    dve.wait_ge(maxed, j * 2 + 1)
                    nc.vector.tensor_tensor(m[:, 1 - x:2 - x], m[:, x:x + 1], smax[:], ALU.max).then_inc(maxed, 1)
                    dve.wait_ge(maxed, j * 2 + 2)
                    nc.vector.tensor_scalar(nm[:, x:x + 1], m[:, 1 - x:2 - x], -MLA_SCALE, None, ALU.mult).then_inc(negated, 1)

                turns(dve, group)
                finish(G - 1, 1)
                collect(G - 1, 1)
                link = chained(dve, fin_v)
                dve.wait_ge(fin_p, 1)
                link(nc.vector.tensor_tensor(picked[:], vp[:, 0:NS], pick[:], ALU.mult))
                link(nc.vector.reduce_sum(snew[:], picked[:], AX_X))
                link(nc.vector.tensor_tensor(m[:, 1:2], m[:, 0:1], snew[:], ALU.max))
                link(nc.vector.tensor_scalar(nm[:, 0:1], m[:, 1:2], -MLA_SCALE, None, ALU.mult))
                dve.wait_ge(fin_a, 2)
                dve.wait_ge(acc_kept, G)
                link(nc.vector.tensor_scalar(acc[:], acc[:], corr[:, 0:1], None, ALU.mult))
                link(nc.vector.scalar_tensor_tensor(out=acc[:], in0=sp_[:, 0:CL], scalar=pnew[:], in1=acc[:], op0=ALU.mult, op1=ALU.add))
                link(nc.vector.tensor_tensor(l[:], l[:], corr[:, 0:1], ALU.mult))
                link(nc.vector.tensor_tensor(l[:], l[:], pnew[:], ALU.add))
                link(nc.vector.reciprocal(l[:], l[:]))
                link(nc.vector.tensor_scalar(acc[:], acc[:], l[:], None, ALU.mult))
                dve.wait_ge(fin_p, 2)
                link(nc.vector.tensor_copy(accT[:], vp[:, 0:2 * P].rearrange("p (c x) -> p c x", c=2)))
                dve.wait_ge(fin_p, 3)
                for half in (slice(0, NOPE), slice(NOPE, P)):
                    par = 0 if half.start == 0 else 1
                    last = nc.vector.tensor_tensor(og[half], sp_[half, 0:P].rearrange("p (c y b) -> p c y b", y=2, b=NS)[:, :, par, :],
                                                   gm[half], ALU.mult)
                link(last)
                link(nc.vector.tensor_tensor(mix[:], mix[:], og[:], ALU.add))

            @block.scalar
            def _(act):
                def group(j, x, first):
                    for b in range(NS):
                        act.wait_ge(turned, j * 8 + (b + 1))
                        if b >= 2 or not first:
                            act.wait_ge(unit_done, j * 8 + (b - 1))
                        nc.scalar.copy(cT[:, b % 2, 0, :], tp[:, b % 2, 0, :]).then_inc(kept_a, 1)
                    act.wait_ge(negated, j + 1)
                    if not first:
                        act.wait_ge(p_turned, j)
                    nc.scalar.activation(corr[:, x:x + 1], m[:, x:x + 1], ACT.Exp, bias=nm[:, x:x + 1], scale=MLA_SCALE).then_inc(expd, 1)
                    nc.scalar.activation(pr[:], sp_[:], ACT.Exp, bias=nm[:, x:x + 1], scale=MLA_SCALE, accum_out=rs[:, x:x + 1]).then_inc(expd, 1)

                turns(act, group)
                act.wait_ge(fin_v, 4)
                nc.scalar.activation(corr[:, 0:1], m[:, 0:1], ACT.Exp, bias=nm[:, 0:1], scale=MLA_SCALE).then_inc(fin_a, 1)
                nc.scalar.activation(pnew[:], snew[:], ACT.Exp, bias=nm[:, 0:1], scale=MLA_SCALE).then_inc(fin_a, 1)


def project_output(k):
    nc, d = k.nc, k.dram
    NL = GROUPS + EXPERTS
    with k.scope() as s:
        w = s.sb("po_w", [P, KD, D])
        mix = s.sb("po_mix", [P, KD, ROWS])
        wr = s.sb("po_wr", [P, KD, NL])
        br = s.sb("po_br", [P, NL])
        nf = s.sb("po_nf", [P, D])
        x, h = s.sb("po_x", [P, 2, D]), s.sb("po_h", [P, 2, D])
        square = s.sb("po_square", [P, D])
        hT = s.sb("po_hT", [P, KD, P])
        ss, mean, inv, rstd = (s.sb(f"po_{n}", [P, NT]) for n in ("ss", "mean", "inv", "rstd"))
        acc = s.ps("po_acc", [P, 2, 2, BANK])
        turned = s.ps("po_turned", [P, KD, P])
        lps = s.ps("po_lps", [P, BANK])
        loaded = s.sem("po_loaded")
        x_loaded = [s.sem(f"po_x_loaded{i}") for i in range(2)]
        stored = [s.sem(f"po_stored{i}") for i in range(2)]
        made, added, squared, meaned, inverted, rooted, normed, turn_done, hT_kept, routed, logits_kept = (
            s.sem(f"po_{n}") for n in ("made", "added", "squared", "meaned", "inverted", "rooted", "normed", "turned",
                                       "hT_kept", "routed", "logits_kept"))
        with nc.Block() as block:
            @block.sync
            def _(sp):
                sp.dma_start(w[:], d["w_out"][0].rearrange("(c p) n -> p c n", p=P)).then_inc(loaded, 16)
                sp.dma_start(mix[:], d["mixT"].rearrange("c p r -> p c r")).then_inc(loaded, 16)
                sp.dma_start(wr[:, :, 0:GROUPS], d["w_group"][0].rearrange("(c p) n -> p c n", p=P)).then_inc(loaded, 16)
                sp.dma_start(wr[:, :, GROUPS:NL], d["w_router"][0].rearrange("(c p) n -> p c n", p=P)).then_inc(loaded, 16)
                sp.dma_start(br[:, 0:GROUPS], d["b_group"][0].partition_broadcast(P)).then_inc(loaded, 16)
                sp.dma_start(br[:, GROUPS:NL], d["b_router"][0].partition_broadcast(P)).then_inc(loaded, 16)
                sp.dma_start(nf[:], d["norm_ffn"][0].partition_broadcast(P)).then_inc(loaded, 16)
                for t in range(NT):
                    if t >= 2:
                        sp.wait_ge(stored[t % 2], 32 * (t // 2))
                    if t == 0:
                        sp.dma_start(x[0:NS, 0, :], d["x_sample"].rearrange("b t d -> (b t) d")).then_inc(x_loaded[0], 16)
                        sp.dma_start(x[NS:HEAD_ROWS, 0, :], d["meta_tokens"]).then_inc(x_loaded[0], 16)
                    else:
                        sp.dma_start(x[:, t % 2, :], d["x_prompt"][0, (t - 1) * P:t * P, :]).then_inc(x_loaded[t % 2], 16)

            @block.gpsimd
            def _(pool):
                for t, (r0, n) in enumerate(TILES):
                    pool.wait_ge(added, t + 1)
                    pool.wait_ge(normed, t + 1)
                    pool.dma_start(d["resid"][r0:r0 + n, :], x[0:n, t % 2, :]).then_inc(stored[t % 2], 16)
                    pool.dma_start(d["ffn_in"][r0:r0 + n, :], h[0:n, t % 2, :]).then_inc(stored[t % 2], 16)
                pool.wait_ge(stored[0], 32 * 5)
                pool.wait_ge(stored[1], 32 * 4)

            @block.tensor
            def _(pe):
                def route(t):
                    n = TILES[t][1]
                    pe.wait_ge(normed, t + 1)
                    if t:
                        pe.wait_ge(hT_kept, t)
                    for c in range(KD):
                        last = nc.tensor.transpose(turned[:, c, 0:n], h[0:n, t % 2, c * P:(c + 1) * P], k.ident[0:n, 0:n])
                    last.then_inc(turn_done, 1)
                    pe.wait_ge(hT_kept, t + 1)
                    if t:
                        pe.wait_ge(logits_kept, t)
                    for c in range(KD):
                        last = nc.tensor.matmul(lps[0:n, 0:NL], hT[:, c, 0:n], wr[:, c, :], start=(c == 0), stop=(c == KD - 1))
                    last.then_inc(routed, 1)

                pe.wait_ge(loaded, 16 * 7)
                for t, (r0, n) in enumerate(TILES):
                    if t >= 2:
                        pe.wait_ge(added, t - 1)
                    for b in range(2):
                        for c in range(KD):
                            last = nc.tensor.matmul(acc[0:n, t % 2, b, :], mix[:, c, r0:r0 + n], w[:, c, b * BANK:(b + 1) * BANK],
                                                    start=(c == 0), stop=(c == KD - 1))
                    last.then_inc(made, 1)
                    if t:
                        route(t - 1)
                route(NT - 1)

            @block.vector
            def _(dve):
                nc.vector.memset(k.logits[:], 0.0)
                dve.wait_ge(loaded, 16 * 7)

                def keep_logits(t):
                    n = TILES[t][1]
                    dve.wait_ge(routed, t + 1)
                    nc.vector.tensor_tensor(k.logits[0:n, t, :], lps[0:n, 0:NL], br[0:n, :], ALU.add).then_inc(logits_kept, 1)

                for t, (r0, n) in enumerate(TILES):
                    i = t % 2
                    dve.wait_ge(x_loaded[i], 16 * (t // 2 + 1) + (16 if i == 0 else 0))
                    dve.wait_ge(made, t + 1)
                    nc.vector.tensor_tensor(x[0:n, i, :].rearrange("p (b n) -> p b n", b=2), x[0:n, i, :].rearrange("p (b n) -> p b n", b=2),
                                            acc[0:n, i], ALU.add).then_inc(added, 1)
                    dve.wait_ge(squared, t + 1)
                    nc.vector.tensor_scalar(mean[0:n, t:t + 1], ss[0:n, t:t + 1], 1.0 / D, EPS, ALU.mult, ALU.add).then_inc(meaned, 1)
                    dve.wait_ge(meaned, t + 1)
                    nc.vector.reciprocal(inv[0:n, t:t + 1], mean[0:n, t:t + 1]).then_inc(inverted, 1)
                    dve.wait_ge(rooted, t + 1)
                    if t >= 2:
                        dve.wait_ge(stored[i], 32 * (t // 2))
                        dve.wait_ge(turn_done, t - 1)
                    nc.vector.scalar_tensor_tensor(out=h[0:n, i, :], in0=x[0:n, i, :], scalar=rstd[0:n, t:t + 1], in1=nf[0:n, :],
                                                   op0=ALU.mult, op1=ALU.mult).then_inc(normed, 1)
                    if t:
                        keep_logits(t - 1)
                keep_logits(NT - 1)

            @block.scalar
            def _(act):
                def keep(t):
                    n = TILES[t][1]
                    act.wait_ge(turn_done, t + 1)
                    if t:
                        act.wait_ge(routed, t)
                    nc.scalar.copy(hT[:, :, 0:n], turned[:, :, 0:n]).then_inc(hT_kept, 1)

                for t, (r0, n) in enumerate(TILES):
                    act.wait_ge(added, t + 1)
                    if t:
                        act.wait_ge(squared, t)
                    nc.scalar.activation(square[0:n, :], x[0:n, t % 2, :], ACT.Square, accum_out=ss[0:n, t:t + 1]).then_inc(squared, 1)
                    act.wait_ge(inverted, t + 1)
                    nc.scalar.activation(rstd[0:n, t:t + 1], inv[0:n, t:t + 1], ACT.Sqrt).then_inc(rooted, 1)
                    if t:
                        keep(t - 1)
                keep(NT - 1)


def route(k):
    nc, d = k.nc, k.dram
    with k.scope() as s:
        before = s.sb("ro_before", [P, P])
        iota = s.sb("ro_iota", [P, 64])
        valid = s.sb("ro_valid", [P, NT])
        token = s.sb("ro_token", [P, NT], I32)
        zero = s.sb("ro_zero", [P, BLOCKS], I32)
        gmax, gsum, gate, vmin, m1, m2, dd, ed, rec = (s.sb(f"ro_{n}", [P, NT]) for n in (
            "gmax", "gsum", "gate", "vmin", "m1", "m2", "dd", "ed", "rec"))
        gd, eq4, og, pen = (s.sb(f"ro_{n}", [P, NT, GROUPS]) for n in ("gd", "eq4", "og", "pen"))
        lem, eq, A1, A2, M, pos, tmp = (s.sb(f"ro_{n}", [P, NT, EXPERTS]) for n in ("lem", "eq", "a1", "a2", "m", "pos", "tmp"))
        base = s.sb("ro_base", [P, NT + 1, EXPERTS])
        nbi = s.sb("ro_nbi", [P, EXPERTS], I32)
        nb, incl, start, zeros = (s.sb(f"ro_{n}", [P, EXPERTS]) for n in ("nb", "incl", "start", "zeros"))
        destf = s.sb("ro_destf", [P, 2, NT])
        cmp = s.sb("ro_cmp", [1, BLOCKS, EXPERTS])
        bef = s.sb("ro_bef", [1, BLOCKS])
        rank_ps = s.ps("ro_rank", [P, NT, EXPERTS])
        tot_ps = s.ps("ro_tot", [P, NT, EXPERTS])
        loaded, step, acted, summed = s.sem("ro_loaded"), s.sem("ro_step"), s.sem("ro_acted"), s.sem("ro_summed")
        exps_asked, weights_asked, counted, placed = (s.sem(f"ro_{n}") for n in ("exps_asked", "weights_asked", "counted", "placed"))
        cleared, zeroed, scattered = s.sem("ro_cleared"), s.sem("ro_zeroed"), s.sem("ro_scattered")
        lg = k.logits[:, :, 0:GROUPS]
        le = k.logits[:, :, GROUPS:]

        def per_tile(ap, w):
            return ap.unsqueeze(2).to_broadcast([P, NT, w])

        with nc.Block() as block:
            @block.sync
            def _(sp):
                sp.dma_start(before[:], d["c_before"]).then_inc(loaded, 16)
                sp.dma_start(iota[:], d["c_iota"]).then_inc(loaded, 16)
                sp.dma_start(valid[:], d["c_valid"]).then_inc(loaded, 16)
                sp.dma_start(token[:], d["c_token"]).then_inc(loaded, 16)

            @block.gpsimd
            def _(pool):
                nc.gpsimd.memset(zero[:], 0).then_inc(cleared, 1)
                pool.wait_ge(cleared, 1)
                pool.dma_start(d["slot_token"].rearrange("(p b) o -> p (b o)", p=P), zero[:]).then_inc(zeroed, 16)
                pool.wait_ge(zeroed, 16)
                pool.wait_ge(loaded, 64)
                pool.wait_ge(placed, 1)
                for t, (r0, n) in enumerate(TILES):
                    for i in range(2):
                        nc.gpsimd.indirect_dma_start(
                            out=d["slot_token"], out_offset=bass.IndirectOffsetOnAxis(ap=k.dest[0:n, i, t:t + 1], axis=0),
                            in_=token[0:n, t:t + 1], in_offset=None).then_inc(scattered, 16)
                pool.wait_ge(scattered, 16 * 2 * NT)

            @block.tensor
            def _(pe):
                pe.wait_ge(counted, 1)
                nc.tensor.matmul(rank_ps[:], before[:], M[:], start=True, stop=True)
                nc.tensor.matmul(tot_ps[:], k.ones[:], M[:], start=True, stop=True).then_inc(summed, 1)

            @block.scalar
            def _(act):
                act.wait_ge(exps_asked, 1)
                nc.scalar.activation(gd[:], gd[:], ACT.Exp).then_inc(acted, 1)
                act.wait_ge(weights_asked, 1)
                nc.scalar.activation(ed[:], dd[:], ACT.Exp).then_inc(acted, 1)

            @block.vector
            def _(dve):
                link = chained(dve, step)
                V = nc.vector

                def first_of(out, x, top, width, scratch):
                    link(V.tensor_tensor(scratch, x, per_tile(top, width), ALU.is_equal))
                    link(V.scalar_tensor_tensor(out=scratch, in0=scratch, scalar=-64.0,
                                                in1=iota[:, 0:width].unsqueeze(1).to_broadcast([P, NT, width]), op0=ALU.mult, op1=ALU.add))
                    link(V.tensor_reduce(vmin[:], scratch, AX_X, ALU.min))
                    link(V.tensor_tensor(out, scratch, per_tile(vmin[:], width), ALU.is_equal))

                dve.wait_ge(loaded, 64)
                V.memset(zeros[:], 0.0)
                V.memset(base[:, 0, :], 0.0)
                link(V.reduce_max(gmax[:], lg, AX_X))
                V.tensor_tensor(gd[:], lg, per_tile(gmax[:], GROUPS), ALU.subtract).then_inc(exps_asked, 1)
                first_of(og[:], lg, gmax[:], GROUPS, eq4[:])
                link(V.tensor_scalar(pen[:], og[:], 1.0, -NEG, ALU.subtract, ALU.mult))
                for t in range(NT):
                    last = V.tensor_tensor(lem[:, t, :].rearrange("p (g e) -> p g e", g=GROUPS), le[:, t, :].rearrange("p (g e) -> p g e", g=GROUPS),
                                           pen[:, t, :].unsqueeze(2).to_broadcast([P, GROUPS, PER_GROUP]), ALU.add)
                link(last)
                link(V.reduce_max(m1[:], lem[:], AX_X))
                first_of(A1[:], lem[:], m1[:], EXPERTS, eq[:])
                link(V.scalar_tensor_tensor(out=lem[:], in0=A1[:], scalar=3 * NEG, in1=lem[:], op0=ALU.mult, op1=ALU.add))
                link(V.reduce_max(m2[:], lem[:], AX_X))
                first_of(A2[:], lem[:], m2[:], EXPERTS, eq[:])
                V.tensor_tensor(dd[:], m2[:], m1[:], ALU.subtract).then_inc(weights_asked, 1)
                link(V.tensor_tensor(M[:], A1[:], A2[:], ALU.add))
                link(V.tensor_tensor(M[:], M[:], per_tile(valid[:], EXPERTS), ALU.mult))
                V.memset(incl[:], 0.0).then_inc(counted, 1)
                dve.wait_ge(acted, 2)
                link(V.reduce_sum(gsum[:], gd[:], AX_X))
                link(V.reciprocal(gate[:], gsum[:]))
                link(V.tensor_scalar(rec[:], ed[:], 1.0, None, ALU.add))
                link(V.reciprocal(rec[:], rec[:]))
                link(V.tensor_tensor(k.weight[:, 0, :], rec[:], gate[:], ALU.mult))
                link(V.tensor_tensor(k.weight[:, 1, :], k.weight[:, 0, :], ed[:], ALU.mult))
                dve.wait_ge(summed, 1)
                for t in range(NT):
                    link(V.tensor_tensor(base[:, t + 1, :], base[:, t, :], tot_ps[:, t, :], ALU.add))
                link(V.tensor_scalar(nbi[:], base[:, NT, :], float(P - 1), None, ALU.add))
                link(V.tensor_scalar(nbi[:], nbi[:], 7, None, ALU.logical_shift_right))
                link(V.tensor_copy(nb[:], nbi[:]))
                link(V.tensor_tensor_scan(incl[:], nb[:], zeros[:], 0.0, ALU.add, ALU.add))
                link(V.tensor_tensor(start[:], incl[:], nb[:], ALU.subtract))
                link(V.tensor_scalar(start[:], start[:], float(P), None, ALU.mult))
                link(V.tensor_tensor(pos[:], rank_ps[:], base[:, 0:NT, :], ALU.add))
                link(V.tensor_tensor(pos[:], pos[:], start[:].unsqueeze(1).to_broadcast([P, NT, EXPERTS]), ALU.add))
                for i, A in enumerate((A1, A2)):
                    link(V.tensor_tensor(tmp[:], A[:], pos[:], ALU.mult))
                    link(V.reduce_sum(destf[:, i, :], tmp[:], AX_X))
                link(V.tensor_copy(k.dest[:], destf[:]))
                V.tensor_scalar(dd[:], dd[:], 0.0, None, ALU.mult).then_inc(placed, 1)
                link(V.tensor_tensor(cmp[:], incl[0:1, :].unsqueeze(1).to_broadcast([1, BLOCKS, EXPERTS]),
                                     iota[0:1, 0:BLOCKS].unsqueeze(2).to_broadcast([1, BLOCKS, EXPERTS]), ALU.is_le))
                link(V.reduce_sum(bef[:], cmp[:], AX_X))
                link(V.tensor_scalar(k.block_expert[:], bef[:], float(EXPERTS - 1), None, ALU.min))
                link(V.tensor_scalar(k.turns[:], incl[0:1, EXPERTS - 1:EXPERTS], -2.0, None, ALU.add))
                link(V.tensor_scalar(k.turns[:], k.turns[:], 1, None, ALU.logical_shift_right))


def experts(k):
    nc, d = k.nc, k.dram
    KE = DE // P
    wg_d = d["w_gate"][0].rearrange("e (p c) f -> e p (c f)", p=P)
    wu_d = d["w_up"][0].rearrange("e (p c) f -> e p (c f)", p=P)
    wd_d = d["w_down"][0].rearrange("e (p c) n -> e p (c n)", p=P)
    with k.scope() as s:
        wg, wu = (s.sb(f"ex_{n}", [P, 2, KD * DE]) for n in ("wg", "wu"))
        wd = s.sb("ex_wd", [P, 2, KE * D])
        idx = [s.sb(f"ex_idx{i}", [P, 1], I32) for i in range(2)]
        slots, slots_f = s.sb("ex_slots", [BLOCKS, P], I32), s.sb("ex_slots_f", [BLOCKS, P])
        idx_all = s.sb("ex_idx_all", [P, BLOCKS], I32)
        x = [s.sb(f"ex_x{i}", [P, D]) for i in range(2)]
        xT = s.sb("ex_xT", [P, 2, KD, P])
        act_g, h = s.sb("ex_act_g", [P, 2, DE]), s.sb("ex_h", [P, 2, DE])
        hT = s.sb("ex_hT", [P, 2, KE, P])
        y = s.sb("ex_y", [P, 2, 2, BANK])
        xps = s.ps("ex_xps", [P, 2, KD // 2, P])
        gu = s.ps("ex_gu", [P, 2, 2, DE])
        hps = s.ps("ex_hps", [P, KE, P])
        yps = s.ps("ex_yps", [P, 2, BANK])
        w_loaded = [s.sem(f"ex_w_loaded{i}") for i in range(2)]
        slots_loaded, slots_kept, slots_turned, idx_ready = (s.sem(f"ex_{n}") for n in ("slots_loaded", "slots_kept", "slots_turned", "idx_ready"))
        gathered = [s.sem(f"ex_gathered{i}") for i in range(2)]
        stored = [s.sem(f"ex_stored{i}") for i in range(2)]
        gather_due, load_due = s.sem("ex_gather_due"), s.sem("ex_load_due")
        x_turned, x_kept_a, x_kept_v, gu_done, silu_done, h_done, h_turned, h_kept, y_done, y_kept_a, y_kept_v = (
            s.sem(f"ex_{n}") for n in ("x_turned", "x_kept_a", "x_kept_v", "gu_done", "silu_done", "h_done", "h_turned",
                                       "h_kept", "y_done", "y_kept_a", "y_kept_v"))

        TURNS = (BLOCKS - 3) // 2

        def turns(eng, body):
            busy = eng.value_load(k.turns[0:1, 0:1], min_val=(2 * ROWS // P - 2) // 2, max_val=TURNS)
            body(0, 0, False)
            body(1, 1, False)
            with eng.Fori(0, TURNS) as i:
                with eng.If(i < busy):
                    body(i * 2 + 2, 0, False)
                    body(i * 2 + 3, 1, False)
            body(busy * 2 + 2, 0, True)
            return busy

        def fixed(b):
            return isinstance(b, int)

        with nc.Block() as block:
            @block.sync
            def _(sp):
                def load(b, i):
                    if not fixed(b) or b >= 2:
                        sp.wait_ge(y_done, b - 1)
                        sp.sem_inc(load_due, 1)
                    e = sp.value_load(k.block_expert[0:1, bass.ds(b, 1)], min_val=0, max_val=EXPERTS - 1)
                    sp.dma_start(wg[:, i, :], wg_d[bass.ds(e, 1)].rearrange("e p n -> p (e n)")).then_inc(w_loaded[i], 16)
                    sp.dma_start(wu[:, i, :], wu_d[bass.ds(e, 1)].rearrange("e p n -> p (e n)")).then_inc(w_loaded[i], 16)
                    sp.dma_start(wd[:, i, :], wd_d[bass.ds(e, 1)].rearrange("e p n -> p (e n)")).then_inc(w_loaded[i], 16)

                def body(b, i, last_one):
                    if not last_one:
                        load(b + 1, 1 - i)
                    sp.wait_ge(y_kept_a, b + 1)
                    sp.wait_ge(y_kept_v, b + 1)
                    sp.dma_start(d["expert_out"][bass.ds(b * P, P), :], y[:, i].rearrange("p b n -> p (b n)")).then_inc(stored[i], 16)

                sp.dma_start(slots[:], d["slot_token"].rearrange("(b p) o -> b (p o)", p=P)).then_inc(slots_loaded, 16)
                load(0, 0)
                busy = turns(sp, body)
                sp.wait_ge(stored[0], busy * 16 + 32)
                sp.sem_inc(load_due, 1)
                sp.wait_ge(stored[1], busy * 16 + 16)
                sp.sem_inc(load_due, 1)

            @block.gpsimd
            def _(pool):
                def gather(b, i):
                    if not fixed(b) or b >= 2:
                        pool.wait_ge(x_turned, b - 1)
                    pool.sem_inc(gather_due, 1)
                    nc.gpsimd.tensor_copy(idx[i][:], idx_all[:, bass.ds(b, 1)]).then_inc(idx_ready, 1)
                    pool.wait_ge(idx_ready, b + 1)
                    pool.sem_inc(gather_due, 1)
                    nc.gpsimd.indirect_dma_start(out=x[i][:], out_offset=None, in_=d["ffn_in"],
                                                 in_offset=bass.IndirectOffsetOnAxis(ap=idx[i][:, 0:1], axis=0)).then_inc(gathered[i], 16)

                def body(b, i, last_one):
                    if not last_one:
                        gather(b + 1, 1 - i)

                pool.wait_ge(slots_kept, 2)
                gather(0, 0)
                turns(pool, body)

            @block.tensor
            def _(pe):
                def turn(b, i):
                    pe.wait_ge(gathered[i], (b - i) * 8 + 16)
                    if not fixed(b) or b >= 1:
                        pe.wait_ge(x_kept_a, b)
                        pe.wait_ge(x_kept_v, b)
                    for c in range(KD):
                        last = nc.tensor.transpose(xps[:, c // 4, c % 4, :], x[i][:, c:D:KD], k.ident[:])
                    last.then_inc(x_turned, 1)

                def body(b, i, last_one):
                    pe.wait_ge(w_loaded[i], (b - i) * 24 + 48)
                    pe.wait_ge(x_kept_a, b + 1)
                    pe.wait_ge(x_kept_v, b + 1)
                    if not fixed(b) or b >= 2:
                        pe.wait_ge(h_done, b - 1)
                    for j, w in enumerate((wg, wu)):
                        for c in range(KD):
                            last = nc.tensor.matmul(gu[:, i, j, :], xT[:, i, c, :], w[:, i, c * DE:(c + 1) * DE], start=(c == 0), stop=(c == KD - 1))
                    last.then_inc(gu_done, 1)
                    if not last_one:
                        turn(b + 1, 1 - i)
                    pe.wait_ge(h_done, b + 1)
                    if not fixed(b) or b >= 1:
                        pe.wait_ge(h_kept, b)
                    for c in range(KE):
                        last = nc.tensor.transpose(hps[:, c, :], h[:, i, c:DE:KE], k.ident[:])
                    last.then_inc(h_turned, 1)
                    pe.wait_ge(h_kept, b + 1)
                    if not fixed(b) or b >= 1:
                        pe.wait_ge(y_kept_a, b)
                        pe.wait_ge(y_kept_v, b)
                    for n in range(2):
                        for c in range(KE):
                            last = nc.tensor.matmul(yps[:, n, :], hT[:, i, c, :], wd[:, i, c * D + n * BANK:c * D + (n + 1) * BANK], start=(c == 0), stop=(c == KE - 1))
                    last.then_inc(y_done, 1)

                pe.wait_ge(slots_kept, 1)
                nc.tensor.transpose(hps[:, 0, 0:BLOCKS], slots_f[:], k.ident[0:BLOCKS, 0:BLOCKS]).then_inc(slots_turned, 1)
                pe.wait_ge(slots_kept, 2)
                turn(0, 0)
                turns(pe, body)

            def keep_x(eng, copy, half, kept, b, i):
                eng.wait_ge(x_turned, b + 1)
                if not fixed(b) or b >= 2:
                    eng.wait_ge(gu_done, b - 1)
                copy(xT[:, i, half * 4:half * 4 + 4, :], xps[:, half]).then_inc(kept, 1)

            def keep_y(eng, copy, half, kept, b, i):
                eng.wait_ge(y_done, b + 1)
                if not fixed(b) or b >= 2:
                    eng.wait_ge(stored[i], (b - i) * 8)
                copy(y[:, i, half, :], yps[:, half, :]).then_inc(kept, 1)

            @block.scalar
            def _(act):
                def body(b, i, last_one):
                    act.wait_ge(gu_done, b + 1)
                    if not fixed(b) or b >= 2:
                        act.wait_ge(h_done, b - 1)
                    nc.scalar.activation(act_g[:, i, :], gu[:, i, 0, :], ACT.Silu).then_inc(silu_done, 1)
                    if not last_one:
                        keep_x(act, nc.scalar.copy, 0, x_kept_a, b + 1, 1 - i)
                    act.wait_ge(h_turned, b + 1)
                    if not fixed(b) or b >= 2:
                        act.wait_ge(y_done, b - 1)
                    nc.scalar.copy(hT[:, i], hps[:]).then_inc(h_kept, 1)
                    keep_y(act, nc.scalar.copy, 0, y_kept_a, b, i)

                keep_x(act, nc.scalar.copy, 0, x_kept_a, 0, 0)
                turns(act, body)

            @block.vector
            def _(dve):
                def body(b, i, last_one):
                    dve.wait_ge(silu_done, b + 1)
                    if not fixed(b) or b >= 2:
                        dve.wait_ge(h_turned, b - 1)
                    nc.vector.tensor_tensor(h[:, i, :], act_g[:, i, :], gu[:, i, 1, :], ALU.mult).then_inc(h_done, 1)
                    if not last_one:
                        keep_x(dve, nc.vector.tensor_copy, 1, x_kept_v, b + 1, 1 - i)
                    keep_y(dve, nc.vector.tensor_copy, 1, y_kept_v, b, i)

                dve.wait_ge(slots_loaded, 16)
                nc.vector.tensor_copy(slots_f[:], slots[:]).then_inc(slots_kept, 1)
                dve.wait_ge(slots_turned, 1)
                nc.vector.tensor_copy(idx_all[:], hps[:, 0, 0:BLOCKS]).then_inc(slots_kept, 1)
                keep_x(dve, nc.vector.tensor_copy, 1, x_kept_v, 0, 0)
                turns(dve, body)


def combine(k):
    nc, d = k.nc, k.dram
    with k.scope() as s:
        nf = s.sb("co_nf", [P, D])
        y = [[s.sb(f"co_y{j}{i}", [P, D]) for i in range(2)] for j in range(2)]
        r, out = s.sb("co_r", [P, 2, D]), s.sb("co_out", [P, 2, D])
        square = s.sb("co_square", [P, D])
        ss, mean, inv, rstd = (s.sb(f"co_{n}", [P, NT]) for n in ("ss", "mean", "inv", "rstd"))
        nf_loaded = s.sem("co_nf_loaded")
        r_loaded, gathered, stored = ([s.sem(f"co_{n}{i}") for i in range(2)] for n in ("r_loaded", "gathered", "stored"))
        half, added, squared, meaned, inverted, rooted, normed = (s.sem(f"co_{n}") for n in (
            "half", "added", "squared", "meaned", "inverted", "rooted", "normed"))
        with nc.Block() as block:
            @block.sync
            def _(sp):
                sp.dma_start(nf[:], d["norm_final"].partition_broadcast(P)).then_inc(nf_loaded, 16)

                def load(t):
                    r0, n = TILES[t]
                    sp.dma_start(r[0:n, t % 2, :], d["resid"][r0:r0 + n, :]).then_inc(r_loaded[t % 2], 16)

                load(0)
                load(1)
                for t in range(NT):
                    sp.wait_ge(normed, t + 1)
                    if t == 0:
                        sp.dma_start(d["y_sample"].rearrange("b t d -> (b t) d"), out[0:NS, 0, :]).then_inc(stored[0], 16)
                    else:
                        sp.dma_start(d["y_prompt"][0, (t - 1) * P:t * P, :], out[:, t % 2, :]).then_inc(stored[t % 2], 16)
                    if t + 2 < NT:
                        load(t + 2)
                sp.wait_ge(stored[0], 16 * 5)
                sp.wait_ge(stored[1], 16 * 4)

            @block.gpsimd
            def _(pool):
                for t, (r0, n) in enumerate(TILES):
                    if t >= 2:
                        pool.wait_ge(added, t - 1)
                    for j in range(2):
                        nc.gpsimd.indirect_dma_start(out=y[j][t % 2][0:n, :], out_offset=None, in_=d["expert_out"],
                                                     in_offset=bass.IndirectOffsetOnAxis(ap=k.dest[0:n, j, t:t + 1], axis=0)).then_inc(gathered[t % 2], 16)

            @block.vector
            def _(dve):
                dve.wait_ge(nf_loaded, 16)
                for t, (r0, n) in enumerate(TILES):
                    i = t % 2
                    dve.wait_ge(r_loaded[i], 16 * (t // 2 + 1))
                    dve.wait_ge(gathered[i], 32 * (t // 2 + 1))
                    rt = r[0:n, i, :]
                    nc.vector.scalar_tensor_tensor(out=rt, in0=y[0][i][0:n, :], scalar=k.weight[0:n, 0, t:t + 1], in1=rt, op0=ALU.mult, op1=ALU.add).then_inc(half, 1)
                    dve.wait_ge(half, t + 1)
                    nc.vector.scalar_tensor_tensor(out=rt, in0=y[1][i][0:n, :], scalar=k.weight[0:n, 1, t:t + 1], in1=rt, op0=ALU.mult, op1=ALU.add).then_inc(added, 1)
                    dve.wait_ge(squared, t + 1)
                    nc.vector.tensor_scalar(mean[0:n, t:t + 1], ss[0:n, t:t + 1], 1.0 / D, EPS, ALU.mult, ALU.add).then_inc(meaned, 1)
                    dve.wait_ge(meaned, t + 1)
                    nc.vector.reciprocal(inv[0:n, t:t + 1], mean[0:n, t:t + 1]).then_inc(inverted, 1)
                    dve.wait_ge(rooted, t + 1)
                    if t >= 2:
                        dve.wait_ge(stored[i], 16 * (t // 2))
                    nc.vector.scalar_tensor_tensor(out=out[0:n, i, :], in0=rt, scalar=rstd[0:n, t:t + 1], in1=nf[0:n, :], op0=ALU.mult, op1=ALU.mult).then_inc(normed, 1)

            @block.scalar
            def _(act):
                for t, (r0, n) in enumerate(TILES):
                    act.wait_ge(added, t + 1)
                    if t:
                        act.wait_ge(squared, t)
                    nc.scalar.activation(square[0:n, :], r[0:n, t % 2, :], ACT.Square, accum_out=ss[0:n, t:t + 1]).then_inc(squared, 1)
                    act.wait_ge(inverted, t + 1)
                    nc.scalar.activation(rstd[0:n, t:t + 1], inv[0:n, t:t + 1], ACT.Sqrt).then_inc(rooted, 1)


def decoder_step(nc, dram):
    k = Core(nc, dram)
    with k:
        load_constants(k)
        with k.scope() as s:
            k.qd, k.kvd = s.sb("qd", [P, NT, QL]), s.sb("kvd", [P, NT, CK])
            k.hT = s.sb("hT", [P, KD, ROWS])
            normalise_input(k)
            project_input(k)
        with k.scope() as s:
            k.g, k.beta = s.sb("g", [P, NT + 1, GH]), s.sb("beta", [P, NT + 1, GH])
            k.G, k.left, k.total_exp = (s.sb(n, [P, NT, GH]) for n in ("G", "left", "total_exp"))
            k.g_exp = s.sb("g_exp", [P, GH])
            gdn_gates(k)
            k.convT = s.sb("convT", [P, GC, ROWS])
            convolve(k)
            gdn_prompt(k)
            gdn_sample(k)
        gate_gdn(k)
        k.q0T = k.sb("q0T", [QK, HEADS, NS])
        k.new_row = k.sb("new_row", [NS, CK])
        with k.scope() as s:
            k.rope = s.sb("rope", [P, NT, ROPE])
            k.keyT = s.sb("keyT", [QK, HEADS, PROMPT])
            k.qlT = s.sb("qlT", [P, KQ, ROWS])
            k.val = s.sb("val", [P, NT, D])
            with k.scope() as s2:
                k.latT = s2.sb("latT", [P, 2, ROWS])
                mla_latents(k)
                mla_keys_values(k)
            attend_prompt(k)
        attend_sample(k)
        k.logits = k.sb("logits", [P, NT, GROUPS + EXPERTS])
        k.dest = k.sb("dest", [P, 2, NT], I32)
        k.weight = k.sb("weight", [P, 2, NT])
        k.block_expert = k.sb("block_expert", [1, BLOCKS], I32)
        k.turns = k.sb("turns", [1, 1], I32)
        project_output(k)
        route(k)
        experts(k)
        combine(k)


_INPUTS = ["x_prompt", "x_sample", "cache_kv_latent", "cache_k_rope", "page_table", "state_conv", "state_gdn",
           "meta_tokens", "norm_mix", "w_in", "q_norm", "w_uq", "kv_norm", "w_uk", "w_uv", "conv_w", "a_log",
           "dt_bias", "gdn_norm", "w_out", "norm_ffn", "w_group", "b_group", "w_router", "b_router", "w_gate",
           "w_up", "w_down", "norm_final"]
_OUTPUTS = [("y_prompt", (1, SEQ, D)), ("y_sample", (NS, 1, D)),
            ("new_latent_prompt", (1, 1, PROMPT, CL)), ("new_rope_prompt", (1, 1, PROMPT, ROPE)),
            ("new_latent_sample", (1, NS, 1, CL)), ("new_rope_sample", (1, NS, 1, ROPE)),
            ("new_conv_prompt", (1, 1, 3, 3 * D)), ("new_conv_sample", (1, NS, 3, 3 * D)),
            ("new_gdn_prompt", (1, 1, GH, DK, DK)), ("new_gdn_sample", (1, NS, GH, DK, DK))]
_SCRATCH = [("projT", (GC + 3 * GH, P, ROWS), F32), ("gdnT", (GH, P, ROWS), F32),
            ("latents", (P, NT, QL + CK), F32), ("mixT", (GH, P, ROWS), F32), ("ffn_in", (ROWS, D), F32),
            ("slot_token", (SLOTS, 1), I32), ("expert_out", (SLOTS, D), F32), ("resid", (ROWS, D), F32)]


def shape_constants():
    import numpy as np

    i = np.arange(P)
    f = np.float32
    levels = np.stack([((i[None, :] >> l) == (i[:, None] >> l) + 1) & (((i[None, :] >> l) & 1) == 1)
                       for l in range(7)], 1)
    inv_freq = np.float32(10000.0) ** (-np.arange(0, ROPE, 2, dtype=f) / f(ROPE))
    pos = np.concatenate([np.full(NS, PAGES * PAGE), np.arange(PROMPT)]).astype(f)
    ang = (pos[:, None] * inv_freq[None, :]).astype(f)
    rope = np.concatenate([np.cos(ang), np.sin(ang)], 1).astype(f)
    table = np.zeros((NT, P, ROPE), f)
    for t, (r0, n) in enumerate(TILES):
        table[t, :n] = rope[r0:r0 + n]
    valid = np.zeros((P, NT), f)
    for t, (_, n) in enumerate(TILES):
        valid[:n, t] = 1
    token = np.stack([np.arange(P) + r0 for r0, _ in TILES], 1)
    return {
        "c_ident": np.eye(P, dtype=f),
        "c_upto": (i[:, None] <= i[None, :]).astype(f),
        "c_before": (i[:, None] < i[None, :]).astype(f),
        "c_levels": levels.astype(f),
        "c_rope": np.ascontiguousarray(table.transpose(1, 0, 2)),
        "c_future": np.where(i[None, :] > i[:, None], f(NEG), f(0)).astype(f),
        "c_diag8": np.repeat(np.eye(NS, dtype=f)[:, :, None], P, 2),
        "c_rep16": np.repeat(np.eye(NS, dtype=f), HEADS, 1),
        "c_pick16": np.repeat(np.eye(NS, dtype=f), HEADS, 0),
        "c_iota": np.broadcast_to(np.arange(64, dtype=f), (P, 64)).copy(),
        "c_valid": valid,
        "c_token": token.astype(np.int32),
    }


def kernel(**inputs):
    import concourse.bacc as _bacc
    import numpy as _np
    from concourse.bass_utils import run_bass_kernel_spmd as _run

    nc = _bacc.Bacc("TRN2", target_bir_lowering=False, num_devices=1)
    arrays = {name: _np.ascontiguousarray(inputs[name]) for name in _INPUTS}
    arrays.update(shape_constants())
    dram = {}
    for name, a in arrays.items():
        dram[name] = nc.dram_tensor(name, a.shape, mybir.dt.from_np(a.dtype), kind="ExternalInput").ap()
    for name, shape in _OUTPUTS:
        dram[name] = nc.dram_tensor(name, shape, F32, kind="ExternalOutput").ap()
    for name, shape, dt in _SCRATCH:
        dram[name] = nc.dram_tensor(name, shape, dt).ap()
    decoder_step(nc, dram)
    r = _run(nc, [arrays], core_ids=[0])
    return tuple(r.results[0][name] for name, _ in _OUTPUTS)
```

```python
from contextlib import ExitStack

import concourse.bass as bass
from concourse import mybir

F32 = mybir.dt.float32
I32 = mybir.dt.int32
F32R = mybir.dt.float32r
ALU = mybir.AluOpType
ACT = mybir.ActivationFunctionType
AX_X = mybir.AxisListType.X

P = 128
D = 1024
KD = D // P
NS = 8
META = 16
SEQ = 1024
PROMPT = META + SEQ
ROWS = NS + PROMPT
HEAD_ROWS = NS + META
NT = 1 + SEQ // P
TILES = [(0, HEAD_ROWS)] + [(HEAD_ROWS + P * i, P) for i in range(NT - 1)]
CHUNKS = [(NS, META)] + TILES[1:]
EPS = 1e-6
HEADS = 16
QL = 384
KQ = QL // P
CL = 256
NOPE = 64
ROPE = 32
HALF = ROPE // 2
QK = NOPE + ROPE
CK = CL + ROPE
MLA_SCALE = QK ** -0.5
NEG = -1e30
PAGES = 64
PAGE = 128
GH = 8
DK = 128
GC = 3 * GH
OFF_QKV = QL + CK
OFF_BA = OFF_QKV + 4 * D
OFF_G = OFF_BA + 2 * GH
GROUPS = 4
PER_GROUP = 8
EXPERTS = GROUPS * PER_GROUP
DE = 256
BLOCKS = (2 * ROWS + EXPERTS * (P - 1) + P - 1) // P
SLOTS = BLOCKS * P
BANK = 512
SPANS = [(0, 352), (352, 704), (704, ROWS)]
Z0, GM0, GG0 = GC, GC + GH, GC + 2 * GH
V_CONV, V_MIX, V_Q, V_GDN = 0, 96, 104, 107


class Scope:

    def __init__(self, nc):
        self.nc = nc
        self.stack = ExitStack()
        self.sems = []

    def __enter__(self):
        return self

    def __exit__(self, *a):
        self.stack.close()
        if self.sems:
            self.nc.clear_and_free_semaphores(self.sems)
            self.nc.all_engine_barrier()

    def sb(self, name, shape, dt=F32):
        return self.stack.enter_context(self.nc.sbuf_tensor(name, shape, dt))

    def ps(self, name, shape):
        return self.stack.enter_context(self.nc.psum_tensor(name, shape, F32))

    def sem(self, name):
        self.sems.append(self.nc.alloc_semaphore(name=name))
        return self.sems[-1]


class Core(Scope):

    def __init__(self, nc, dram):
        super().__init__(nc)
        self.dram = dram

    def scope(self):
        return Scope(self.nc)


def chained(eng, sem):
    count = [0]

    def link(ins):
        count[0] += 1
        ins.then_inc(sem, 1)
        eng.wait_ge(sem, count[0])

    return link


def masked_hi(nc, out, x):
    return nc.vector.tensor_scalar(out.bitcast(I32), x.bitcast(I32), -4096, None, ALU.bitwise_and)


def split_matmul(nc, out, lhs, rhs, start, stop):
    for i, (a, b) in enumerate(((0, 0), (0, 1), (1, 0))):
        last = nc.tensor.matmul(out, lhs[a], rhs[b], start=(start and i == 0), stop=(stop and i == 2))
    return last


def load_constants(k):
    nc, d = k.nc, k.dram
    k.ident = k.sb("ident", [P, P])
    k.ones = k.sb("ones", [P, P])
    k.upto = k.sb("upto", [P, P])
    k.vecT = k.sb("vecT", [P, P])
    k.eps = k.sb("eps", [P, 1])
    k.ba = k.sb("ba", [P, NT + 1, 2 * GH])
    with k.scope() as s:
        rows = s.sb("vec_rows", [P, P])
        turned = s.ps("vec_ps", [P, P])
        c_loaded, c_turned, c_kept = s.sem("c_loaded"), s.sem("c_turned"), s.sem("c_kept")
        c_zero = s.sem("c_zero")
        with nc.Block() as block:
            @block.sync
            def _(sp):
                sp.dma_start(k.ident[:], d["c_ident"]).then_inc(c_loaded, 16)
                sp.dma_start(k.upto[:], d["c_upto"]).then_inc(c_loaded, 16)
                sp.wait_ge(c_zero, 1)
                sp.dma_start(rows[V_CONV:V_MIX, :], d["conv_w"].rearrange("a w (j p) -> (a w j) p", p=P)).then_inc(c_loaded, 16)
                sp.dma_start(rows[V_MIX:V_Q, :], d["norm_mix"].rearrange("a (j p) -> (a j) p", p=P)).then_inc(c_loaded, 16)
                sp.dma_start(rows[V_Q:V_GDN, :], d["q_norm"].rearrange("a (j p) -> (a j) p", p=P)).then_inc(c_loaded, 16)
                sp.dma_start(rows[V_GDN:V_GDN + 1, :], d["gdn_norm"]).then_inc(c_loaded, 16)

            @block.vector
            def _(dve):
                nc.vector.memset(k.ones[:], 1.0)
                nc.vector.memset(k.eps[:], EPS)
                nc.vector.memset(k.ba[:], 0.0)
                nc.vector.memset(rows[:], 0.0).then_inc(c_zero, 1)
                dve.wait_ge(c_turned, 1)
                nc.vector.tensor_copy(k.vecT[:], turned[:]).then_inc(c_kept, 1)

            @block.tensor
            def _(pe):
                pe.wait_ge(c_loaded, 6 * 16)
                nc.tensor.transpose(turned[:], rows[:], k.ident[:]).then_inc(c_turned, 1)


def normalise_input(k):
    nc, d = k.nc, k.dram
    with k.scope() as s:
        x = s.sb("na_x", [P, 2, D])
        xn = s.sb("na_xn", [P, 2, D])
        square = s.sb("na_square", [P, D])
        h, m = s.sb("na_h", [P, KD, P]), s.sb("na_m", [P, KD, P])
        ss, mean, inv, rstd = (s.sb(f"na_{n}", [P, NT]) for n in ("ss", "mean", "inv", "rstd"))
        turned = s.ps("na_ps", [P, 2, KD, P])
        loaded = [s.sem(f"na_loaded{i}") for i in range(2)]
        zeroed, masked, hi_kept, lo_made = (s.sem(f"na_{n}") for n in ("zeroed", "masked", "hi_kept", "lo_made"))
        squared, meaned, inverted, rooted, scaled, turn_done, kept = (s.sem(f"na_{n}") for n in (
            "squared", "meaned", "inverted", "rooted", "scaled", "turned", "kept"))
        with nc.Block() as block:
            @block.sync
            def _(sp):
                for t, (r0, n) in enumerate(TILES):
                    if t >= 2:
                        sp.wait_ge(scaled, t - 1)
                        sp.wait_ge(squared, t - 1)
                    if t == 0:
                        sp.dma_start(x[0:NS, 0, :], d["x_sample"].rearrange("b t d -> (b t) d")).then_inc(loaded[0], 16)
                        sp.dma_start(x[NS:HEAD_ROWS, 0, :], d["meta_tokens"]).then_inc(loaded[0], 16)
                    else:
                        sp.dma_start(x[:, t % 2, :], d["x_prompt"][0, (t - 1) * P:t * P, :]).then_inc(loaded[t % 2], 16)

            @block.gpsimd
            def _(pool):
                nc.gpsimd.memset(k.qd[:, 0, :], 0.0)
                nc.gpsimd.memset(k.kvd[:, 0, :], 0.0).then_inc(zeroed, 1)

            @block.scalar
            def _(act):
                def root(t):
                    act.wait_ge(inverted, t + 1)
                    n = TILES[t][1]
                    nc.scalar.activation(rstd[0:n, t:t + 1], inv[0:n, t:t + 1], ACT.Sqrt).then_inc(rooted, 1)

                def keep_hi(t):
                    r0, n = TILES[t]
                    act.wait_ge(masked, t + 1)
                    nc.scalar.copy(k.hT_hi[:, :, r0:r0 + n], m[:, :, 0:n]).then_inc(hi_kept, 1)

                for t, (r0, n) in enumerate(TILES):
                    act.wait_ge(loaded[t % 2], 16 * (t // 2 + 1) + (16 if t % 2 == 0 else 0))
                    if t:
                        act.wait_ge(squared, t)
                    nc.scalar.activation(square[0:n, :], x[0:n, t % 2, :], ACT.Square,
                                         accum_out=ss[0:n, t:t + 1]).then_inc(squared, 1)
                    root(t)
                    if t:
                        keep_hi(t - 1)
                keep_hi(NT - 1)

            @block.vector
            def _(dve):
                def keep(t):
                    r0, n = TILES[t]
                    dve.wait_ge(turn_done, t + 1)
                    nc.vector.tensor_tensor(h[:, :, 0:n], turned[:, t % 2, :, 0:n],
                                            k.vecT[:, V_MIX:V_Q].unsqueeze(2).to_broadcast([P, KD, n]),
                                            ALU.mult).then_inc(kept, 1)
                    dve.wait_ge(kept, t + 1)
                    if t:
                        dve.wait_ge(hi_kept, t)
                    masked_hi(nc, m[:, :, 0:n], h[:, :, 0:n]).then_inc(masked, 1)
                    dve.wait_ge(masked, t + 1)
                    nc.vector.tensor_tensor(k.hT_lo[:, :, r0:r0 + n], h[:, :, 0:n], m[:, :, 0:n], ALU.subtract).then_inc(lo_made, 1)
                    dve.wait_ge(lo_made, t + 1)

                for t, (r0, n) in enumerate(TILES):
                    dve.wait_ge(squared, t + 1)
                    nc.vector.tensor_scalar(mean[0:n, t:t + 1], ss[0:n, t:t + 1], 1.0 / D, EPS,
                                            ALU.mult, ALU.add).then_inc(meaned, 1)
                    dve.wait_ge(meaned, t + 1)
                    nc.vector.reciprocal(inv[0:n, t:t + 1], mean[0:n, t:t + 1]).then_inc(inverted, 1)
                    dve.wait_ge(rooted, t + 1)
                    if t >= 2:
                        dve.wait_ge(turn_done, t - 1)
                    nc.vector.tensor_scalar(xn[0:n, t % 2, :], x[0:n, t % 2, :], rstd[0:n, t:t + 1], None,
                                            ALU.mult).then_inc(scaled, 1)
                    if t:
                        keep(t - 1)
                keep(NT - 1)

            @block.tensor
            def _(pe):
                for t, (r0, n) in enumerate(TILES):
                    pe.wait_ge(scaled, t + 1)
                    if t >= 2:
                        pe.wait_ge(kept, t - 1)
                    for c in range(KD):
                        last = nc.tensor.transpose(turned[:, t % 2, c, 0:n], xn[0:n, t % 2, c * P:(c + 1) * P],
                                                   k.ident[0:n, 0:n])
                    last.then_inc(turn_done, 1)


def project_input(k):
    nc, d = k.nc, k.dram
    w_in = d["w_in"][0].rearrange("(c p) n -> p c n", p=P)
    projT = d["projT"].rearrange("(g c) p t -> g p c t", c=4)
    with k.scope() as s:
        w_hi, w_lo = (s.sb(f"pi_w_{n}", [P, 2, KD, BANK], F32R) for n in ("hi", "lo"))
        piece, m = s.sb("pi_piece", [P, 2, 2, BANK]), s.sb("pi_m", [P, 2, BANK])
        out = s.sb("pi_out", [P, 2, 4, ROWS])
        acc = s.ps("pi_acc", [P, 2, 3, BANK])
        piece_loaded = [s.sem(f"pi_piece_loaded{i}") for i in range(2)]
        acc_ready, acc_kept = s.sem("pi_acc_ready"), s.sem("pi_acc_kept")
        stored = [s.sem(f"pi_stored{i}") for i in range(2)]
        latents_out, masked, w_split = s.sem("pi_latents_out"), s.sem("pi_masked"), s.sem("pi_w_split")
        whole = [(r0, n, t) for t, (r0, n) in enumerate(TILES)]
        jobs = [(0, QL, whole, lambda n, t: k.qd[0:n, t, :]),
                (QL, CK, whole, lambda n, t: k.kvd[0:n, t, :]),
                (OFF_BA, 2 * GH, [(r0, n, t) for t, (r0, n) in enumerate(CHUNKS)] + [(0, NS, NT)],
                 lambda n, t: k.ba[0:n, t, :])]
        token_units = sum(len(j[2]) for j in jobs)
        assert token_units % 2 == 0
        J = len(jobs)
        runs = [(OFF_QKV, 0, 2, ACT.Copy), (OFF_QKV + 2 * BANK, 2, 4, ACT.Copy), (OFF_QKV + 6 * BANK, 6, 2, ACT.Silu), (OFF_G, 8, 4, ACT.Sigmoid)]

        with nc.Block() as block:
            @block.sync
            def _(sp):
                def load(before, c0, n, first):
                    for x in range(4):
                        if not first or x >= 2:
                            sp.wait_ge(w_split, before * 4 + (x - 1))
                        sp.dma_start(piece[:, x % 2, :, 0:n], w_in[:, 2 * x:2 * x + 2, bass.ds(c0, n)]).then_inc(piece_loaded[x % 2], 16)

                for i, (c0, n, tiles, _) in enumerate(jobs):
                    load(i, c0, n, i == 0)
                for c0, g0, ng, _ in runs:
                    with sp.Fori(0, ng // 2) as i:
                        for h in range(2):
                            load(i * 2 + (J + g0 + h), i * (2 * BANK) + (c0 + h * BANK), BANK, False)

            @block.tensor
            def _(pe):
                unit = 0
                for i, (c0, n, tiles, _) in enumerate(jobs):
                    pe.wait_ge(w_split, 4 * (i + 1))
                    for r0, m, t in tiles:
                        if unit >= 2:
                            pe.wait_ge(acc_kept, unit - 1)
                        for c in range(KD):
                            last = split_matmul(nc, acc[0:m, unit % 2, 0, 0:n], [x[:, c, r0:r0 + m] for x in (k.hT_hi, k.hT_lo)],
                                                [x[:, i % 2, c, 0:n] for x in (w_hi, w_lo)], start=(c == 0), stop=(c == KD - 1))
                        last.then_inc(acc_ready, 1)
                        unit += 1
                for _, g0, ng, _ in runs:
                    with pe.Fori(0, ng // 2) as i:
                        for h in range(2):
                            slot = (J + h) % 2
                            pe.wait_ge(w_split, i * 8 + 4 * (J + g0 + h + 1))
                            for c4 in range(4):
                                u = 4 * (g0 + h) + c4
                                pe.wait_ge(acc_kept, i * 8 + (token_units + u - 1))
                                for c in range(KD):
                                    for b, (a0, a1) in enumerate(SPANS):
                                        last = split_matmul(nc, acc[:, u % 2, b, 0:a1 - a0], [x[:, slot, c, c4 * P:(c4 + 1) * P] for x in (w_hi, w_lo)],
                                                            [x[:, c, a0:a1] for x in (k.hT_hi, k.hT_lo)], start=(c == 0), stop=(c == KD - 1))
                                last.then_inc(acc_ready, 1)

            @block.vector
            def _(dve):
                def split_weights(slot, n, before):
                    for x in range(4):
                        mine = piece[:, x % 2, :, 0:n]
                        dve.wait_ge(piece_loaded[x % 2], before * 32 + (16 * (x // 2) + 16))
                        if x or not isinstance(before, int) or before:
                            dve.wait_ge(w_split, before * 4 + x)
                        masked_hi(nc, m[:, :, 0:n], mine).then_inc(masked, 1)
                        dve.wait_ge(masked, before * 4 + (x + 1))
                        nc.vector.tensor_copy(w_hi[:, slot, 2 * x:2 * x + 2, 0:n], m[:, :, 0:n])
                        nc.vector.tensor_tensor(w_lo[:, slot, 2 * x:2 * x + 2, 0:n], mine, m[:, :, 0:n], ALU.subtract).then_inc(w_split, 1)

                for i, (c0, n, tiles, to) in enumerate(jobs):
                    if i >= 2:
                        dve.wait_ge(acc_ready, NT * (i - 1))
                    split_weights(i % 2, n, i)
                for _, g0, ng, _ in runs:
                    with dve.Fori(0, ng // 2) as i:
                        for h in range(2):
                            dve.wait_ge(acc_ready, i * 8 + (token_units + 4 * (g0 + h - 1)))
                            split_weights((J + h) % 2, BANK, i * 2 + (J + g0 + h))

            @block.scalar
            def _(act):
                unit = 0
                for i, (c0, n, tiles, to) in enumerate(jobs):
                    for r0, m, t in tiles:
                        act.wait_ge(acc_ready, unit + 1)
                        nc.scalar.activation(to(m, t), acc[0:m, unit % 2, 0, 0:n], ACT.Copy).then_inc(acc_kept, 1)
                        unit += 1
                for _, g0, ng, func in runs:
                    with act.Fori(0, ng // 2) as i:
                        for h in range(2):
                            if g0:
                                act.wait_ge(stored[h], i * 16 + 16 * (g0 // 2))
                            for c4 in range(4):
                                u = 4 * (g0 + h) + c4
                                act.wait_ge(acc_ready, i * 8 + (token_units + u + 1))
                                for b, (a0, a1) in enumerate(SPANS):
                                    last = nc.scalar.activation(out[:, h, c4, a0:a1], acc[:, u % 2, b, 0:a1 - a0], func)
                                last.then_inc(acc_kept, 1)

            @block.gpsimd
            def _(pool):
                for _, g0, ng, _ in runs:
                    with pool.Fori(0, ng // 2) as i:
                        for h in range(2):
                            pool.wait_ge(acc_kept, i * 8 + (token_units + 4 * (g0 + h) + 4))
                            pool.dma_start(projT[bass.ds(i * 2 + (g0 + h), 1)].rearrange("g p c t -> p (g c) t"),
                                           out[:, h]).then_inc(stored[h], 16)
                for h in range(2):
                    pool.wait_ge(stored[h], 16 * 6)
                pool.dma_start(d["latents"][:, :, 0:QL], k.qd[:]).then_inc(latents_out, 16)
                pool.dma_start(d["latents"][:, :, QL:], k.kvd[:]).then_inc(latents_out, 16)
                pool.wait_ge(latents_out, 32)


def convolve(k):
    nc, d = k.nc, k.dram
    with k.scope() as s:
        state_rows = s.sb("cv_state_rows", [3 * NS, 3 * D])
        stateT = s.sb("cv_stateT", [P, GC, 3 * NS])
        x = s.sb("cv_x", [P, 2, ROWS])
        y = s.sb("cv_y", [P, 2, ROWS])
        tail = s.sb("cv_tail", [NS, 3 * D])
        tail_p = s.sb("cv_tail_p", [3, 3 * D])
        norm = s.sb("cv_norm", [P, 2, ROWS])
        tail_ps = s.ps("cv_tail_ps", [NS, 2, BANK])
        sum_ps = s.ps("cv_sum_ps", [P, 2, 3, BANK])
        state_ps = sum_ps[:, 0]
        state_loaded, state_turned, state_kept = s.sem("cv_state_loaded"), s.sem("cv_state_turned"), s.sem("cv_state_kept")
        x_loaded = [s.sem(f"cv_x_loaded{i}") for i in range(2)]
        tap, conv_done, silu_done = s.sem("cv_tap"), s.sem("cv_conv_done"), s.sem("cv_silu_done")
        tail_turned, tail_kept, tails_out = s.sem("cv_tail_turned"), s.sem("cv_tail_kept"), s.sem("cv_tails_out")
        squared, summed, logged, rooted, normed = (s.sem(f"cv_{n}") for n in (
            "squared", "summed", "logged", "rooted", "normed"))
        HB = GC // 2

        def w(j, i):
            return k.vecT[:, V_CONV + i * GC + j:V_CONV + i * GC + j + 1]

        def earlier(j, i):
            return stateT[:, j, :].rearrange("p (b r) -> p r b", r=3)[:, i, :]

        with nc.Block() as block:
            @block.sync
            def _(sp):
                sp.dma_start(state_rows[:], d["state_conv"].rearrange("a b r c -> (a b r) c")).then_inc(state_loaded, 16)
                for j in range(GC):
                    if j >= 2:
                        sp.wait_ge(conv_done, j - 1)
                        sp.wait_ge(tail_turned, j - 1)
                    sp.dma_start(x[:, j % 2, :], d["projT"][j]).then_inc(x_loaded[j % 2], 16)
                sp.dma_start(d["new_conv_sample"][0, :, 0:2, :], d["state_conv"][0, :, 1:3, :]).then_inc(tails_out, 16)
                sp.wait_ge(tail_kept, 2 * GC)
                sp.dma_start(d["new_conv_sample"][0, :, 2, :], tail[:]).then_inc(tails_out, 16)
                sp.dma_start(d["new_conv_prompt"][0, 0], tail_p[:]).then_inc(tails_out, 16)
                sp.wait_ge(tails_out, 3 * 16)

            @block.vector
            def _(dve):
                for b in range(2):
                    dve.wait_ge(state_turned, b + 1)
                    nc.vector.tensor_copy(stateT[:, b * HB:(b + 1) * HB, :],
                                          state_ps[:, b, 0:HB * 3 * NS].rearrange("p (j r) -> p j r", j=HB)).then_inc(state_kept, 1)
                dve.wait_ge(state_kept, 2)
                for j in range(GC):
                    xj, yj = x[:, j % 2, :], y[:, j % 2, :]
                    dve.wait_ge(x_loaded[j % 2], 16 * (j // 2 + 1))
                    if j >= 2:
                        dve.wait_ge(silu_done, j - 1)
                    nc.vector.tensor_scalar(yj, xj, w(j, 3), None, ALU.mult).then_inc(tap, 1)
                    for i in range(3):
                        dve.wait_ge(tap, 3 * j + i + 1)
                        back = i + 1
                        nc.vector.scalar_tensor_tensor(out=yj[:, NS + back:], in0=xj[:, NS:ROWS - back], scalar=w(j, 2 - i),
                                                       in1=yj[:, NS + back:], op0=ALU.mult, op1=ALU.add)
                        nc.vector.scalar_tensor_tensor(out=yj[:, 0:NS], in0=earlier(j, 2 - i), scalar=w(j, 2 - i),
                                                       in1=yj[:, 0:NS], op0=ALU.mult, op1=ALU.add).then_inc(
                                                           tap if i < 2 else conv_done, 1)
                for j in range(2 * GH):
                    dve.wait_ge(rooted, j + 1)
                    nc.vector.scalar_tensor_tensor(out=k.convT[:, j, :], in0=norm[:, j % 2, :],
                                                   scalar=DK ** -0.5 if j < GH else 1.0, in1=k.convT[:, j, :],
                                                   op0=ALU.mult, op1=ALU.mult).then_inc(normed, 1)

            @block.scalar
            def _(act):
                for j in range(GC):
                    act.wait_ge(conv_done, j + 1)
                    nc.scalar.activation(k.convT[:, j, :], y[:, j % 2, :], ACT.Silu).then_inc(silu_done, 1)
                    act.wait_ge(tail_turned, j + 1)
                    nc.scalar.activation(tail[:, j * P:(j + 1) * P], tail_ps[:, j % 2, 0:P], ACT.Copy).then_inc(tail_kept, 1)
                    nc.scalar.activation(tail_p[:, j * P:(j + 1) * P], tail_ps[0:3, j % 2, P:2 * P], ACT.Copy).then_inc(tail_kept, 1)
                act.wait_ge(silu_done, GC)

                def root(j):
                    act.wait_ge(summed, j + 1)
                    if j >= 2:
                        act.wait_ge(normed, j - 1)
                    for b, (a0, a1) in enumerate(SPANS):
                        last = nc.scalar.activation(norm[:, j % 2, a0:a1], sum_ps[:, j % 2, b, 0:a1 - a0], ACT.Ln, bias=k.eps[:])
                    last.then_inc(logged, 1)
                    act.wait_ge(logged, j + 1)
                    nc.scalar.activation(norm[:, j % 2, :], norm[:, j % 2, :], ACT.Exp, scale=-0.5).then_inc(rooted, 1)

                for j in range(2 * GH):
                    if j >= 2:
                        act.wait_ge(summed, j - 1)
                    nc.scalar.activation(y[:, j % 2, :], k.convT[:, j, :], ACT.Square).then_inc(squared, 1)
                    if j:
                        root(j - 1)
                root(2 * GH - 1)

            @block.tensor
            def _(pe):
                pe.wait_ge(state_loaded, 16)
                for b in range(2):
                    for j in range(HB):
                        last = nc.tensor.transpose(state_ps[:, b, j * 3 * NS:(j + 1) * 3 * NS],
                                                   state_rows[:, (b * HB + j) * P:(b * HB + j + 1) * P],
                                                   k.ident[0:3 * NS, 0:3 * NS])
                    last.then_inc(state_turned, 1)
                pe.wait_ge(state_kept, 2)
                for j in range(GC):
                    pe.wait_ge(x_loaded[j % 2], 16 * (j // 2 + 1))
                    if j >= 2:
                        pe.wait_ge(tail_kept, 2 * (j - 1))
                    nc.tensor.transpose(tail_ps[:, j % 2, 0:P], x[:, j % 2, 0:NS], k.ident[:])
                    nc.tensor.transpose(tail_ps[0:3, j % 2, P:2 * P], x[:, j % 2, ROWS - 3:], k.ident[:]).then_inc(tail_turned, 1)
                for j in range(2 * GH):
                    pe.wait_ge(squared, j + 1)
                    if j >= 2:
                        pe.wait_ge(logged, j - 1)
                    for b, (a0, a1) in enumerate(SPANS):
                        last = nc.tensor.matmul(sum_ps[:, j % 2, b, 0:a1 - a0], k.ones[:], y[:, j % 2, a0:a1], start=True, stop=True)
                    last.then_inc(summed, 1)


def gdn_gates(k):
    nc, d = k.nc, k.dram
    NB = NT + 1
    with k.scope() as s:
        bias = s.sb("gg_bias", [P, GH])
        rate = s.sb("gg_rate", [P, GH])
        v, m, e, l = (s.sb(f"gg_{n}", [P, NB, GH]) for n in ("v", "neg_abs", "exp", "ln"))
        total = s.sb("gg_total", [P, NT, GH])
        g_ps = s.ps("gg_g_ps", [P, NT, GH])
        t_ps = s.ps("gg_t_ps", [P, NT, GH])
        loaded, step, acted = s.sem("gg_loaded"), s.sem("gg_step"), s.sem("gg_acted")
        sums = s.sem("gg_sums")
        sums_kept, diffed = s.sem("gg_sums_kept"), s.sem("gg_diffed")
        with nc.Block() as block:
            @block.sync
            def _(sp):
                sp.dma_start(bias[:], d["dt_bias"][0].partition_broadcast(P)).then_inc(loaded, 16)
                sp.dma_start(rate[:], d["a_log"][0].partition_broadcast(P)).then_inc(loaded, 16)

            @block.vector
            def _(dve):
                link = chained(dve, step)
                dve.wait_ge(loaded, 32)
                link(nc.vector.tensor_tensor(v[:], k.ba[:, :, GH:], bias[:].unsqueeze(1).to_broadcast([P, NB, GH]), ALU.add))
                link(nc.vector.scalar_tensor_tensor(out=m[:], in0=v[:], scalar=-1.0, in1=v[:], op0=ALU.mult, op1=ALU.min))
                link(nc.vector.tensor_scalar(v[:], v[:], 0.0, None, ALU.max))
                dve.wait_ge(acted, 3)
                link(nc.vector.tensor_tensor(v[:], v[:], l[:], ALU.add))
                link(nc.vector.tensor_scalar(rate[:], rate[:], -1.0, None, ALU.mult))
                link(nc.vector.tensor_tensor(k.g[:], v[:], rate[:].unsqueeze(1).to_broadcast([P, NB, GH]), ALU.mult))
                dve.wait_ge(sums, 1)
                nc.vector.tensor_copy(k.G[:], g_ps[:]).then_inc(sums_kept, 1)
                nc.vector.tensor_copy(total[:], t_ps[:]).then_inc(sums_kept, 1)
                dve.wait_ge(sums_kept, 2)
                nc.vector.tensor_tensor(k.left[:], total[:], k.G[:], ALU.subtract).then_inc(diffed, 1)

            @block.scalar
            def _(act):
                act.wait_ge(step, 2)
                nc.scalar.activation(e[:], m[:], ACT.Exp).then_inc(acted, 1)
                act.wait_ge(acted, 1)
                nc.scalar.activation(l[:], e[:], ACT.Ln, bias=k.ones[:, 0:1]).then_inc(acted, 1)
                act.wait_ge(loaded, 32)
                nc.scalar.activation(rate[:], rate[:], ACT.Exp).then_inc(acted, 1)
                act.wait_ge(diffed, 1)
                nc.scalar.activation(k.left[:], k.left[:], ACT.Exp).then_inc(acted, 1)
                nc.scalar.activation(k.total_exp[:], total[:], ACT.Exp).then_inc(acted, 1)
                nc.scalar.activation(k.g_exp[:], k.g[:, NT, :], ACT.Exp).then_inc(acted, 1)
                nc.scalar.activation(k.beta[:], k.ba[:, :, 0:GH], ACT.Sigmoid).then_inc(acted, 1)

            @block.tensor
            def _(pe):
                pe.wait_ge(step, 6)
                nc.tensor.matmul(g_ps[:], k.upto[:], k.g[:, 0:NT, :], start=True, stop=True)
                nc.tensor.matmul(t_ps[:], k.ones[:], k.g[:, 0:NT, :], start=True, stop=True)
                nc.tensor.matmul(g_ps[:, 0, :], k.upto[0:META, :], k.g[0:META, 0, :], start=True, stop=True)
                nc.tensor.matmul(t_ps[:, 0, :], k.ones[0:META, :], k.g[0:META, 0, :], start=True, stop=True).then_inc(sums, 1)


def gdn_prompt(k):
    nc, d = k.nc, k.dram
    with k.scope() as s:
        levels = s.sb("gp_levels", [P, 7, P])
        S = s.sb("gp_state", [P, GH, DK])
        decayed = s.sb("gp_decayed", [P, GH, DK])
        decay, row_exp, kg, qg, LT, attn, ktok, vtok, B, X, Y, M, r, vn, o = (s.sb(f"gp_{n}", [P, GH, P]) for n in (
            "decay", "row_exp", "kg", "qg", "LT", "attn", "ktok", "vtok", "B", "X", "Y", "M", "r", "vn", "o"))
        ps = [s.ps(f"gp_ps{i}", [P, GH, P]) for i in range(4)]
        consts, zeroed = s.sem("gp_consts"), s.sem("gp_zeroed")
        prods, exps, local, scaled_k = s.sem("gp_prods"), s.sem("gp_exps"), s.sem("gp_local"), s.sem("gp_scaled_k")
        turned, ktok_kept, vtok_kept = s.sem("gp_turned"), s.sem("gp_ktok_kept"), s.sem("gp_vtok_kept")
        masked, b_turned, m_done, m_kept, xy_done, x_kept, y_kept = (s.sem(f"gp_{n}") for n in (
            "masked", "b_turned", "m_done", "m_kept", "xy_done", "x_kept", "y_kept"))
        ks_done, r_ready, vn_done, vn_kept, out_done, out_kept, out_stored = (s.sem(f"gp_{n}") for n in (
            "ks_done", "r_ready", "vn_done", "vn_kept", "out_done", "out_kept", "out_stored"))
        upd_done, S_decayed, S_ready, dve_step = (s.sem(f"gp_{n}") for n in ("upd_done", "S_decayed", "S_ready", "dve_step"))
        H2 = GH // 2
        halves = [slice(0, H2), slice(H2, GH)]
        LV = [4] + [7] * (NT - 1)
        UP = [sum(LV[:c]) for c in range(NT + 1)]
        UM = [UP[c] - c for c in range(NT + 1)]

        def cols(c):
            r0, n = CHUNKS[c]
            return slice(r0, r0 + n), n

        with nc.Block() as block:
            @block.sync
            def _(sp):
                sp.dma_start(levels[:], d["c_levels"]).then_inc(consts, 16)
                for c in range(NT):
                    sl, n = cols(c)
                    sp.wait_ge(out_kept, c + 1)
                    sp.dma_start(d["gdnT"][:, :, sl].rearrange("h p t -> p h t"), o[:, :, 0:n]).then_inc(out_stored, 16)
                sp.wait_ge(S_ready, NT)
                sp.dma_start(d["new_gdn_prompt"][0, 0].rearrange("h p v -> p h v"), S[:]).then_inc(out_stored, 16)
                sp.wait_ge(out_stored, 16 * (NT + 1))

            @block.tensor
            def _(pe):
                pe.wait_ge(consts, 16)
                for c in range(NT):
                    sl, n = cols(c)
                    q, kk, v = (k.convT[:, i * GH:(i + 1) * GH, sl] for i in range(3))
                    if c:
                        pe.wait_ge(out_kept, c)
                        pe.wait_ge(S_ready, c)
                        pe.wait_ge(r_ready, c)
                        pe.wait_ge(vn_kept, c)
                    for h in range(GH):
                        nc.tensor.matmul(ps[0][:, h, 0:n], k.g[0:n, c, h:h + 1].to_broadcast([n, P]), k.upto[0:n, 0:n], start=True, stop=True)
                    for h in range(GH):
                        nc.tensor.matmul(ps[2][0:n, h, 0:n], kk[:, h, :], kk[:, h, :], start=True, stop=True)
                    for h in range(GH):
                        nc.tensor.matmul(ps[1][:, h, 0:n], k.beta[0:n, c, h:h + 1].to_broadcast([n, P]), k.ident[0:n, 0:n], start=True, stop=True)
                    for h in range(GH):
                        last = nc.tensor.matmul(ps[3][0:n, h, 0:n], kk[:, h, :], q[:, h, :], start=True, stop=True)
                    last.then_inc(prods, 1)
                    pe.wait_ge(exps, 2 * c + 1)
                    pe.wait_ge(local, 4 * c + 1)
                    for h in range(GH):
                        last = nc.tensor.transpose(ps[0][0:n, h, :], kk[:, h, :], k.ident[:])
                    last.then_inc(turned, 1)
                    pe.wait_ge(local, 4 * c + 4)
                    for h in range(GH):
                        last = nc.tensor.transpose(ps[1][0:n, h, :], v[:, h, :], k.ident[:])
                    last.then_inc(turned, 1)
                    for hv in range(2):
                        pe.wait_ge(masked, UP[c] + 1)
                        for h in range(hv * H2, hv * H2 + H2):
                            last = nc.tensor.transpose(ps[2][0:n, h, 0:n], B[0:n, h, 0:n], k.ident[0:n, 0:n])
                        last.then_inc(b_turned, 1)
                    pe.wait_ge(ktok_kept, c + 1)
                    pe.wait_ge(vtok_kept, c + 1)
                    for l in range(1, LV[c]):
                        u = UM[c] + l - 1
                        for hv in range(2):
                            pe.wait_ge(masked, UP[c] + l + 1)
                            pe.wait_ge(x_kept, 2 * (UP[c] + l - 1) + hv + 1)
                            for h in range(hv * H2, hv * H2 + H2):
                                last = nc.tensor.matmul(ps[3][0:n, h, 0:n], B[0:n, h, 0:n], X[0:n, h, 0:n], start=True, stop=True)
                            last.then_inc(m_done, 1)
                        for hv in range(2):
                            pe.wait_ge(m_kept, 2 * u + hv + 1)
                            pe.wait_ge(y_kept, 2 * (UP[c] + l - 1) + hv + 1)
                            for h in range(hv * H2, hv * H2 + H2):
                                nc.tensor.matmul(ps[2][0:n, h, 0:n], Y[0:n, h, 0:n], M[0:n, h, 0:n], start=True, stop=True)
                            for h in range(hv * H2, hv * H2 + H2):
                                last = nc.tensor.matmul(ps[0][0:n, h, 0:n], M[0:n, h, 0:n], Y[0:n, h, 0:n], start=True, stop=True)
                            last.then_inc(xy_done, 1)
                    pe.wait_ge(scaled_k, 2 * c + 2)
                    if c:
                        pe.wait_ge(S_ready, c)
                    else:
                        pe.wait_ge(zeroed, 1)
                    for h in range(GH):
                        last = nc.tensor.matmul(ps[1][0:n, h, :], kg[:, h, 0:n], S[:, h, :], start=True, stop=True)
                    last.then_inc(ks_done, 1)
                    pe.wait_ge(r_ready, c + 1)
                    pe.wait_ge(y_kept, 2 * UP[c + 1])
                    for h in range(GH):
                        last = nc.tensor.matmul(ps[3][0:n, h, :], Y[0:n, h, 0:n], r[0:n, h, :], start=True, stop=True)
                    last.then_inc(vn_done, 1)
                    pe.wait_ge(vn_kept, c + 1)
                    pe.wait_ge(x_kept, 2 * UP[c + 1])
                    for h in range(GH):
                        last = nc.tensor.matmul(ps[2][:, h, :], ktok[0:n, h, :], vn[0:n, h, :], start=True, stop=True)
                    last.then_inc(upd_done, 1)
                    for h in range(GH):
                        nc.tensor.matmul(ps[0][:, h, 0:n], S[:, h, :], qg[:, h, 0:n], start=True, stop=False)
                        last = nc.tensor.matmul(ps[0][:, h, 0:n], vn[0:n, h, :], attn[0:n, h, 0:n], start=False, stop=True)
                    last.then_inc(out_done, 1)

            @block.vector
            def _(dve):
                nc.vector.memset(S[:], 0.0).then_inc(zeroed, 1)
                dve.wait_ge(consts, 16)
                for c in range(NT):
                    sl, n = cols(c)

                    def bc(ap):
                        return ap.unsqueeze(2).to_broadcast([n, GH, n])

                    upto = k.upto[0:n, 0:n].unsqueeze(1).to_broadcast([n, GH, n])
                    step = 4 * c
                    dve.wait_ge(prods, c + 1)
                    nc.vector.tensor_tensor(decay[0:n, :, 0:n], ps[0][0:n, :, 0:n], bc(k.G[0:n, c, :]), ALU.subtract).then_inc(local, 1)
                    dve.wait_ge(local, step + 1)
                    nc.vector.tensor_scalar(decay[0:n, :, 0:n], decay[0:n, :, 0:n], 0.0, None, ALU.min).then_inc(local, 1)
                    dve.wait_ge(exps, 2 * c + 2)
                    nc.vector.tensor_tensor(LT[0:n, :, 0:n], ps[2][0:n, :, 0:n], decay[0:n, :, 0:n], ALU.mult)
                    nc.vector.tensor_tensor(decay[0:n, :, 0:n], decay[0:n, :, 0:n], upto, ALU.mult).then_inc(local, 1)
                    dve.wait_ge(local, step + 3)
                    nc.vector.tensor_tensor(LT[0:n, :, 0:n], LT[0:n, :, 0:n], ps[1][0:n, :, 0:n], ALU.mult)
                    nc.vector.tensor_tensor(attn[0:n, :, 0:n], decay[0:n, :, 0:n], ps[3][0:n, :, 0:n], ALU.mult).then_inc(local, 1)
                    dve.wait_ge(turned, 2 * c + 1)
                    nc.vector.tensor_tensor(ktok[0:n], ps[0][0:n], k.left[0:n, c, :].unsqueeze(2).to_broadcast([n, GH, P]), ALU.mult).then_inc(ktok_kept, 1)
                    ident = k.ident[0:n, 0:n].unsqueeze(1).to_broadcast([n, H2, n])
                    dve.wait_ge(masked, UP[c] + 1)
                    for hv in range(2):
                        hs = halves[hv]
                        nc.vector.tensor_tensor(Y[0:n, hs, 0:n], ident, B[0:n, hs, 0:n], ALU.subtract).then_inc(y_kept, 1)
                        dve.wait_ge(b_turned, 2 * c + hv + 1)
                        nc.vector.tensor_tensor(X[0:n, hs, 0:n], ident, ps[2][0:n, hs, 0:n], ALU.subtract).then_inc(x_kept, 1)
                    for l in range(1, LV[c]):
                        u = UM[c] + l - 1
                        for hv in range(2):
                            hs = halves[hv]
                            dve.wait_ge(xy_done, 2 * u + hv + 1)
                            nc.vector.tensor_tensor(X[0:n, hs, 0:n], X[0:n, hs, 0:n], ps[2][0:n, hs, 0:n], ALU.subtract).then_inc(x_kept, 1)
                            nc.vector.tensor_tensor(Y[0:n, hs, 0:n], Y[0:n, hs, 0:n], ps[0][0:n, hs, 0:n], ALU.subtract).then_inc(y_kept, 1)
                    dve.wait_ge(ks_done, c + 1)
                    dve.wait_ge(vtok_kept, c + 1)
                    nc.vector.tensor_tensor(r[0:n], vtok[0:n], ps[1][0:n], ALU.subtract).then_inc(dve_step, 1)
                    dve.wait_ge(dve_step, c + 1)
                    nc.vector.tensor_tensor(r[0:n], r[0:n], k.beta[0:n, c, :].unsqueeze(2).to_broadcast([n, GH, P]), ALU.mult).then_inc(r_ready, 1)
                    dve.wait_ge(upd_done, c + 1)
                    dve.wait_ge(out_done, c + 1)
                    dve.wait_ge(S_decayed, c + 1)
                    nc.vector.tensor_tensor(S[:], decayed[:], ps[2][:], ALU.add).then_inc(S_ready, 1)

            @block.gpsimd
            def _(pool):
                pool.wait_ge(consts, 16)
                pool.wait_ge(zeroed, 1)
                for c in range(NT):
                    sl, n = cols(c)
                    pool.wait_ge(local, 4 * c + 4)
                    for l in range(LV[c]):
                        if l == 1:
                            pool.wait_ge(y_kept, 2 * (UP[c] + 1))
                            pool.wait_ge(b_turned, 2 * (c + 1))
                        if l > 1:
                            pool.wait_ge(m_done, 2 * (UM[c] + l - 1))
                        nc.gpsimd.tensor_tensor(B[0:n, :, 0:n], LT[0:n, :, 0:n],
                                                levels[0:n, l, 0:n].unsqueeze(1).to_broadcast([n, GH, n]), ALU.mult).then_inc(masked, 1)
                        if l == 1:
                            pool.wait_ge(exps, 2 * c + 1)
                            for i, to in ((GH, kg), (0, qg)):
                                nc.gpsimd.tensor_tensor(to[:, :, 0:n], k.convT[:, i:i + GH, sl], row_exp[:, :, 0:n], ALU.mult).then_inc(scaled_k, 1)
                        if l == 2:
                            if c:
                                pool.wait_ge(S_ready, c)
                            nc.gpsimd.tensor_tensor(decayed[:], S[:], k.total_exp[:, c, :].unsqueeze(2).to_broadcast([P, GH, DK]), ALU.mult).then_inc(S_decayed, 1)

            @block.scalar
            def _(act):
                for c in range(NT):
                    sl, n = cols(c)
                    act.wait_ge(local, 4 * c + 1)
                    nc.scalar.activation(row_exp[:, :, 0:n], ps[0][:, :, 0:n], ACT.Exp).then_inc(exps, 1)
                    act.wait_ge(local, 4 * c + 2)
                    nc.scalar.activation(decay[0:n, :, 0:n], decay[0:n, :, 0:n], ACT.Exp).then_inc(exps, 1)
                    act.wait_ge(turned, 2 * c + 2)
                    nc.scalar.activation(vtok[0:n], ps[1][0:n], ACT.Copy).then_inc(vtok_kept, 1)
                    for l in range(1, LV[c]):
                        u = UM[c] + l - 1
                        for hv in range(2):
                            hs = halves[hv]
                            act.wait_ge(m_done, 2 * u + hv + 1)
                            nc.scalar.activation(M[0:n, hs, 0:n], ps[3][0:n, hs, 0:n], ACT.Copy).then_inc(m_kept, 1)
                    act.wait_ge(vn_done, c + 1)
                    nc.scalar.activation(vn[0:n], ps[3][0:n], ACT.Copy).then_inc(vn_kept, 1)
                    act.wait_ge(out_done, c + 1)
                    if c:
                        act.wait_ge(out_stored, 16 * c)
                    nc.scalar.activation(o[:, :, 0:n], ps[0][:, :, 0:n], ACT.Copy).then_inc(out_kept, 1)


def gdn_sample(k):
    nc, d = k.nc, k.dram
    pairs = GH * NS
    N4 = pairs // 4
    with k.scope() as s:
        S = s.sb("gs_state", [P, NS, GH, DK])
        diag = s.sb("gs_diag", [NS, NS, P])
        gates = s.sb("gs_gates", [NS, 2, GH, NS])
        gb = s.sb("gs_gb", [P, 2, GH, NS])
        kq = s.sb("gs_kq", [P, 2, GH, NS])
        qk, t, delta, qs, oT = (s.sb(f"gs_{n}", [P, GH, NS]) for n in ("qk", "t", "delta", "qs", "oT"))
        krow, drow = s.sb("gs_krow", [pairs, P]), s.sb("gs_drow", [pairs, P])
        own = s.sb("gs_own", [pairs, 2, 4, P])
        gb_ps = s.ps("gs_gb_ps", [P, 2, GH, NS])
        prod = s.ps("gs_prod", [P, 2, GH, NS])
        qk_ps = s.ps("gs_qk_ps", [P, GH, NS])
        rows = s.ps("gs_rows", [pairs, 2, P])
        upd = s.ps("gs_upd", [P, 2, 4, P])
        loaded, s_loaded, stored = s.sem("gs_loaded"), s.sem("gs_s_loaded"), s.sem("gs_stored")
        pe_step, step, scaled, owned, updated, added = (s.sem(f"gs_{n}") for n in ("pe_step", "step", "scaled", "owned", "updated", "added"))
        with nc.Block() as block:
            @block.sync
            def _(sp):
                sp.dma_start(diag[:], d["c_diag8"]).then_inc(loaded, 16)
                sp.dma_start(S[:], d["state_gdn"][0].rearrange("b h p v -> p b h v")).then_inc(s_loaded, 16)
                sp.wait_ge(step, 6)
                sp.dma_start(d["gdnT"][:, :, 0:NS].rearrange("h p t -> p h t"), oT[:]).then_inc(stored, 16)
                for h in range(GH):
                    sp.wait_ge(added, 2 * h + 2)
                    sp.dma_start(d["new_gdn_sample"][0, :, h].rearrange("b p v -> p b v"), S[:, :, h, :]).then_inc(stored, 16)
                sp.wait_ge(stored, 16 * (GH + 1))

            @block.tensor
            def _(pe):
                pe.wait_ge(step, 1)
                nc.tensor.matmul(gb_ps[:], k.ones[0:NS, :], gates[:], start=True, stop=True)
                nc.tensor.matmul(qk_ps[:], k.ones[:], qk[:], start=True, stop=True)
                nc.tensor.transpose(rows[:, 0, :], kq[:, 0], k.ident[:]).then_inc(pe_step, 1)
                pe.wait_ge(s_loaded, 16)
                for h in range(GH):
                    for b in range(NS):
                        last = nc.tensor.matmul(prod[:, :, h, b], S[:, b, h, :], kq[:, :, h, b], start=True, stop=True)
                last.then_inc(pe_step, 1)
                pe.wait_ge(step, 5)
                nc.tensor.transpose(rows[:, 1, :], delta[:], k.ident[:]).then_inc(pe_step, 1)
                for g in range(N4):
                    pe.wait_ge(owned, g + 2)
                    if g >= 2:
                        pe.wait_ge(added, g - 1)
                    nc.tensor.matmul(upd[:, g % 2], krow[:], own[:, g % 2], start=True, stop=True).then_inc(updated, 1)

            @block.gpsimd
            def _(pool):
                pool.wait_ge(step, 2)
                pool.wait_ge(pe_step, 2)
                for h in range(GH):
                    nc.gpsimd.tensor_tensor(S[:, :, h, :], S[:, :, h, :], gb[:, 0, h, :].unsqueeze(2).to_broadcast([P, NS, DK]), ALU.mult).then_inc(scaled, 1)

            @block.vector
            def _(dve):
                link = chained(dve, step)
                V = nc.vector
                dve.wait_ge(loaded, 16)
                eye = diag[:, :, 0].unsqueeze(1).to_broadcast([NS, GH, NS])
                V.tensor_tensor(gates[:, 0], k.g_exp[0:NS, :].unsqueeze(2).to_broadcast([NS, GH, NS]), eye, ALU.mult)
                V.tensor_tensor(gates[:, 1], k.beta[0:NS, NT, :].unsqueeze(2).to_broadcast([NS, GH, NS]), eye, ALU.mult)
                V.tensor_tensor(qk[:], k.convT[:, 0:GH, 0:NS], k.convT[:, GH:2 * GH, 0:NS], ALU.mult)
                V.tensor_copy(kq[:, 1], k.convT[:, 0:GH, 0:NS])
                link(V.tensor_copy(kq[:, 0], k.convT[:, GH:2 * GH, 0:NS]))
                dve.wait_ge(pe_step, 1)
                V.tensor_copy(krow[:], rows[:, 0, :])
                link(V.tensor_copy(gb[:], gb_ps[:]))
                dve.wait_ge(pe_step, 2)
                V.tensor_tensor(qs[:], prod[:, 1], gb[:, 0], ALU.mult)
                link(V.tensor_tensor(t[:], prod[:, 0], gb[:, 0], ALU.mult))
                link(V.tensor_tensor(t[:], k.convT[:, 2 * GH:, 0:NS], t[:], ALU.subtract))
                link(V.tensor_tensor(delta[:], t[:], gb[:, 1], ALU.mult))
                V.tensor_tensor(t[:], qk_ps[:], delta[:], ALU.mult).then_inc(owned, 1)
                dve.wait_ge(owned, 1)
                V.tensor_tensor(oT[:], qs[:], t[:], ALU.add).then_inc(step, 1)
                dve.wait_ge(pe_step, 3)
                V.tensor_copy(drow[:], rows[:, 1, :]).then_inc(step, 1)
                dve.wait_ge(step, 7)

                def pick(g):
                    if g >= 2:
                        dve.wait_ge(updated, g - 1)
                    V.tensor_tensor(own[:, g % 2], drow[:].unsqueeze(1).to_broadcast([pairs, 4, P]),
                                    k.ident[0:pairs, 4 * g:4 * g + 4].unsqueeze(2).to_broadcast([pairs, 4, P]), ALU.mult).then_inc(owned, 1)

                pick(0)
                for g in range(N4):
                    if g + 1 < N4:
                        pick(g + 1)
                    h, b0 = g // 2, 4 * (g % 2)
                    dve.wait_ge(scaled, h + 1)
                    dve.wait_ge(updated, g + 1)
                    mine = S[:, b0:b0 + 4, h, :]
                    V.tensor_tensor(mine, mine, upd[:, g % 2], ALU.add).then_inc(added, 1)


def gate_gdn(k):
    nc, d = k.nc, k.dram
    with k.scope() as s:
        o, z, g, sq, m = (s.sb(f"ge_{n}", [P, 2, ROWS]) for n in ("o", "z", "g", "square", "mix"))
        sums = s.ps("ge_sums", [P, 2, 3, BANK])
        loaded = [s.sem(f"ge_loaded{i}") for i in range(2)]
        squared, summed, logged, rooted, step, done = (s.sem(f"ge_{n}") for n in ("squared", "summed", "logged", "rooted", "step", "done"))
        stored = [s.sem(f"ge_stored{i}") for i in range(2)]
        with nc.Block() as block:
            @block.sync
            def _(sp):
                for h in range(GH):
                    if h >= 2:
                        sp.wait_ge(done, h - 1)
                    sp.dma_start(o[:, h % 2, :], d["gdnT"][h]).then_inc(loaded[h % 2], 16)
                    sp.dma_start(z[:, h % 2, :], d["projT"][Z0 + h]).then_inc(loaded[h % 2], 16)
                    sp.dma_start(g[:, h % 2, :], d["projT"][GG0 + h]).then_inc(loaded[h % 2], 16)
                    if h:
                        sp.wait_ge(done, h)
                        sp.dma_start(d["mixT"][h - 1], m[:, (h - 1) % 2, :]).then_inc(stored[(h - 1) % 2], 16)
                sp.wait_ge(done, GH)
                sp.dma_start(d["mixT"][GH - 1], m[:, 1, :]).then_inc(stored[1], 16)
                for i in range(2):
                    sp.wait_ge(stored[i], 16 * GH // 2)

            @block.scalar
            def _(act):
                def root(h):
                    act.wait_ge(summed, h + 1)
                    for b, (a0, a1) in enumerate(SPANS):
                        last = nc.scalar.activation(sq[:, h % 2, a0:a1], sums[:, h % 2, b, 0:a1 - a0], ACT.Ln, bias=k.eps[:], scale=1.0 / DK)
                    last.then_inc(logged, 1)
                    act.wait_ge(logged, h + 1)
                    nc.scalar.activation(sq[:, h % 2, :], sq[:, h % 2, :], ACT.Exp, scale=-0.5).then_inc(rooted, 1)

                for h in range(GH):
                    act.wait_ge(loaded[h % 2], 48 * (h // 2 + 1))
                    if h >= 2:
                        act.wait_ge(done, h - 1)
                    nc.scalar.activation(sq[:, h % 2, :], o[:, h % 2, :], ACT.Square).then_inc(squared, 1)
                    if h:
                        root(h - 1)
                root(GH - 1)

            @block.tensor
            def _(pe):
                for h in range(GH):
                    pe.wait_ge(squared, h + 1)
                    if h >= 2:
                        pe.wait_ge(logged, h - 1)
                    for b, (a0, a1) in enumerate(SPANS):
                        last = nc.tensor.matmul(sums[:, h % 2, b, 0:a1 - a0], k.ones[:], sq[:, h % 2, a0:a1], start=True, stop=True)
                    last.then_inc(summed, 1)

            @block.vector
            def _(dve):
                for h in range(GH):
                    i = h % 2
                    dve.wait_ge(loaded[i], 48 * (h // 2 + 1))
                    dve.wait_ge(squared, h + 1)
                    nc.vector.tensor_tensor(z[:, i], z[:, i], g[:, i], ALU.mult)
                    nc.vector.tensor_scalar(o[:, i], o[:, i], k.vecT[:, V_GDN:V_GDN + 1], None, ALU.mult).then_inc(step, 1)
                    dve.wait_ge(step, 2 * h + 1)
                    nc.vector.tensor_tensor(o[:, i], o[:, i], z[:, i], ALU.mult).then_inc(step, 1)
                    dve.wait_ge(step, 2 * h + 2)
                    dve.wait_ge(rooted, h + 1)
                    if h >= 2:
                        dve.wait_ge(stored[i], 16 * (h // 2))
                    nc.vector.tensor_tensor(m[:, i], o[:, i], sq[:, i], ALU.mult).then_inc(done, 1)


def mla_latents(k):
    nc, d = k.nc, k.dram
    with k.scope() as s:
        rope = k.rope
        qd, kvd = s.sb("ml_qd", [P, NT, QL]), s.sb("ml_kvd", [P, NT, CK])
        wkv = s.sb("ml_wkv", [P, CL])
        pad = s.sb("ml_pad", [P, NT, QK])
        ropeT = s.sb("ml_ropeT", [QK, ROWS])
        square = s.sb("ml_square", [P, QL])
        ss = s.sb("ml_ss", [P, 2, NT])
        t1, t2 = (s.sb(f"ml_t{i}", [P, NT, 2, HALF]) for i in range(2))
        turned = s.ps("ml_turned", [P, 2, 2, BANK])
        loaded, step, acted, turn_done, turn_kept = (s.sem(f"ml_{n}") for n in ("loaded", "step", "acted", "turned", "kept"))
        stored, spread = s.sem("ml_stored"), s.sem("ml_spread")
        rope_kept = s.sem("ml_rope_kept")
        with nc.Block() as block:
            @block.sync
            def _(sp):
                sp.dma_start(qd[:], d["latents"][:, :, 0:QL]).then_inc(loaded, 16)
                sp.dma_start(kvd[:], d["latents"][:, :, QL:]).then_inc(loaded, 16)
                sp.dma_start(rope[:], d["c_rope"]).then_inc(loaded, 16)
                sp.dma_start(wkv[:], d["kv_norm"][0].partition_broadcast(P)).then_inc(loaded, 16)
                sp.wait_ge(step, 7)
                lat, ro = kvd[:, :, 0:CL], pad[:, :, NOPE:QK]
                for name, src, w in (("latent", lat, CL), ("rope", ro, ROPE)):
                    op, os = d[f"new_{name}_prompt"][0, 0], d[f"new_{name}_sample"][0, :, 0, :]
                    sp.dma_start(os, src[0:NS, 0, :]).then_inc(stored, 16)
                    sp.dma_start(op[0:META], src[NS:HEAD_ROWS, 0, :]).then_inc(stored, 16)
                    sp.dma_start(op[META:].rearrange("(t p) c -> p t c", p=P), src[:, 1:, :]).then_inc(stored, 16)
                sp.wait_ge(turn_kept, NT)
                for h in range(HEADS):
                    sp.dma_start(k.keyT[NOPE:QK, h, :], ropeT[NOPE:QK, NS:]).then_inc(spread, 16)
                sp.wait_ge(spread, 16 * HEADS)
                sp.wait_ge(stored, 16 * 6)

            @block.vector
            def _(dve):
                link = chained(dve, step)
                nc.vector.memset(ss[:], 1.0)
                link(nc.vector.memset(pad[:], 0.0))
                dve.wait_ge(loaded, 64)
                x1, x2 = kvd[:, :, CL:CL + HALF], kvd[:, :, CL + HALF:CK]
                cos, sin = rope[:, :, 0:HALF], rope[:, :, HALF:ROPE]
                nc.vector.tensor_tensor(t1[:, :, 0, :], x1, cos, ALU.mult)
                nc.vector.tensor_tensor(t1[:, :, 1, :], x2, cos, ALU.mult)
                nc.vector.tensor_tensor(t2[:, :, 0, :], x2, sin, ALU.mult)
                link(nc.vector.tensor_tensor(t2[:, :, 1, :], x1, sin, ALU.mult))
                nc.vector.tensor_tensor(pad[:, :, NOPE:NOPE + HALF], t1[:, :, 0, :], t2[:, :, 0, :], ALU.subtract)
                link(nc.vector.tensor_tensor(pad[:, :, NOPE + HALF:QK], t1[:, :, 1, :], t2[:, :, 1, :], ALU.add))
                dve.wait_ge(acted, 2 * NT)
                nc.vector.tensor_scalar(ss[:, 0, :], ss[:, 0, :], 1.0 / CL, EPS, ALU.mult, ALU.add)
                link(nc.vector.tensor_scalar(ss[:, 1, :], ss[:, 1, :], 1.0 / QL, EPS, ALU.mult, ALU.add))
                link(nc.vector.reciprocal(ss[:], ss[:]))
                dve.wait_ge(acted, 2 * NT + 1)
                nc.vector.tensor_tensor(qd[:], qd[:], ss[:, 1, :].unsqueeze(2).to_broadcast([P, NT, QL]), ALU.mult)
                link(nc.vector.tensor_tensor(kvd[:, :, 0:CL], kvd[:, :, 0:CL], ss[:, 0, :].unsqueeze(2).to_broadcast([P, NT, CL]), ALU.mult))
                link(nc.vector.tensor_tensor(kvd[:, :, 0:CL], kvd[:, :, 0:CL], wkv[:].unsqueeze(1).to_broadcast([P, NT, CL]), ALU.mult))
                nc.vector.tensor_copy(k.new_row[:, 0:CL], kvd[0:NS, 0, 0:CL])
                nc.vector.tensor_copy(k.new_row[:, CL:CK], pad[0:NS, 0, NOPE:QK])
                for t, (r0, n) in enumerate(TILES):
                    dve.wait_ge(turn_done, t + 1)
                    bank = turned[:, t % 2]
                    nc.vector.tensor_copy(k.latT[:, :, r0:r0 + n], bank[:, 0, 0:2 * P].rearrange("p (c r) -> p c r", c=2)[:, :, 0:n])
                    nc.vector.tensor_copy(ropeT[:, r0:r0 + n], bank[0:QK, 0, 2 * P:2 * P + n])
                    nc.vector.tensor_tensor(k.qlT[:, :, r0:r0 + n], bank[:, 1, 0:KQ * P].rearrange("p (c r) -> p c r", c=KQ)[:, :, 0:n],
                                            k.vecT[:, V_Q:V_GDN].unsqueeze(2).to_broadcast([P, KQ, n]), ALU.mult).then_inc(turn_kept, 1)

            @block.scalar
            def _(act):
                act.wait_ge(step, 1)
                act.wait_ge(loaded, 64)
                at = 0
                for t, (r0, n) in enumerate(TILES):
                    for i, (src, w) in enumerate(((kvd, CL), (qd, QL))):
                        if at:
                            act.wait_ge(acted, at)
                        nc.scalar.activation(square[0:n, 0:w], src[0:n, t, 0:w], ACT.Square, accum_out=ss[0:n, i, t:t + 1]).then_inc(acted, 1)
                        at += 1
                act.wait_ge(step, 5)
                nc.scalar.activation(ss[:], ss[:], ACT.Sqrt).then_inc(acted, 1)

            @block.tensor
            def _(pe):
                pe.wait_ge(step, 7)
                for t, (r0, n) in enumerate(TILES):
                    if t >= 2:
                        pe.wait_ge(turn_kept, t - 1)
                    bank, eye = turned[:, t % 2], k.ident[0:n, 0:n]
                    for c in range(2):
                        nc.tensor.transpose(bank[:, 0, c * P:c * P + n], kvd[0:n, t, c * P:(c + 1) * P], eye)
                    nc.tensor.transpose(bank[0:QK, 0, 2 * P:2 * P + n], pad[0:n, t, :], eye)
                    for c in range(KQ):
                        last = nc.tensor.transpose(bank[:, 1, c * P:c * P + n], qd[0:n, t, c * P:(c + 1) * P], eye)
                    last.then_inc(turn_done, 1)


def mla_keys_values(k):
    nc, d = k.nc, k.dram
    KSP = [(0, 512), (512, 1024), (1024, PROMPT)]
    with k.scope() as s:
        wuk = s.sb("kv_wuk", [P, 2, HEADS * NOPE])
        wuv = s.sb("kv_wuv", [P, 2, D])
        acc = s.ps("kv_acc", [P, 2, 3, BANK])
        loaded, made, kept = s.sem("kv_loaded"), s.sem("kv_made"), s.sem("kv_kept")
        with nc.Block() as block:
            @block.sync
            def _(sp):
                sp.dma_start(wuk[:], d["w_uk"][0].rearrange("(c p) h n -> p c (h n)", p=P)).then_inc(loaded, 16)
                sp.dma_start(wuv[:], d["w_uv"][0].rearrange("(c p) h n -> p c (h n)", p=P)).then_inc(loaded, 16)

            @block.tensor
            def _(pe):
                pe.wait_ge(loaded, 32)
                for u in range(HEADS + NT):
                    if u >= 2:
                        pe.wait_ge(kept, u - 1)
                    if u < HEADS:
                        for c in range(2):
                            for b, (a0, a1) in enumerate(KSP):
                                last = nc.tensor.matmul(acc[0:NOPE, u % 2, b, 0:a1 - a0], wuk[:, c, u * NOPE:(u + 1) * NOPE],
                                                        k.latT[:, c, NS + a0:NS + a1], start=(c == 0), stop=(c == 1))
                    else:
                        r0, n = CHUNKS[u - HEADS]
                        for c in range(2):
                            for b in range(2):
                                last = nc.tensor.matmul(acc[0:n, u % 2, b, :], k.latT[:, c, r0:r0 + n],
                                                        wuv[:, c, b * BANK:(b + 1) * BANK], start=(c == 0), stop=(c == 1))
                    last.then_inc(made, 1)

            def keep(eng, copy, mine):
                for u in range(HEADS + NT):
                    if u % 2 == mine:
                        eng.wait_ge(made, u + 1)
                        if u >= 1:
                            eng.wait_ge(kept, u)
                        if u < HEADS:
                            for b, (a0, a1) in enumerate(KSP):
                                last = copy(k.keyT[0:NOPE, u, a0:a1], acc[0:NOPE, u % 2, b, 0:a1 - a0])
                        else:
                            n = CHUNKS[u - HEADS][1]
                            last = copy(k.val[0:n, u - HEADS, :].rearrange("p (b n) -> p b n", b=2), acc[0:n, u % 2, 0:2, :])
                        last.then_inc(kept, 1)

            @block.vector
            def _(dve):
                keep(dve, nc.vector.tensor_copy, 0)

            @block.scalar
            def _(act):
                keep(act, nc.scalar.copy, 1)


def attend_prompt(k):
    nc, d = k.nc, k.dram
    with k.scope() as s:
        wuq = s.sb("at_wuq", [P, KQ, HEADS * QK])
        future = s.sb("at_future", [P, P])
        q = s.sb("at_q", [P, HEADS, QK])
        t1, t2 = (s.sb(f"at_t{i}", [P, HEADS, 2, HALF]) for i in range(2))
        qT = s.sb("at_qT", [QK, 2, HEADS, P])
        gm = s.sb("at_gm", [P, 2, KD, P])
        mix = s.sb("at_mix", [P, 2, KD, P])
        p = s.sb("at_p", [P, 3, PROMPT])
        pT = s.sb("at_pT", [P, 3, 4, P])
        og = s.sb("at_og", [P, P])
        zero = s.sb("at_zero", [P, D])
        mx, nm, l, il = (s.sb(f"at_{n}", [P, 2]) for n in ("mx", "nm", "l", "il"))
        sc = s.ps("at_sc", [P, 5, BANK])
        scf = sc[:].rearrange("p b n -> p (b n)")
        mid = sc[:, 2, :]
        tp = s.ps("at_tp", [P, 2, 4, P])
        op = s.ps("at_op", [P, BANK])
        loaded, mix_stored = s.sem("at_loaded"), [s.sem(f"at_mix_stored{i}") for i in range(2)]
        gm_loaded = [s.sem(f"at_gm_loaded{i}") for i in range(2)]
        mid_made, mid_kept, roped, rotated, q0_kept = (s.sem(f"at_{n}") for n in ("mid_made", "mid_kept", "roped", "rotated", "q0_kept"))
        zero_made, zeroed = s.sem("at_zero_made"), s.sem("at_zeroed")
        scored, maxed, negated, expd, inverted, normed = (s.sem(f"at_{n}") for n in ("scored", "maxed", "negated", "expd", "inverted", "normed"))
        p_turned, pT_kept, valued, gated, mixed = (s.sem(f"at_{n}") for n in ("p_turned", "pT_kept", "valued", "gated", "mixed"))
        groups = []
        first = []
        for t in range(NT):
            for h in range(HEADS):
                first.append(len(groups))
                groups += [(t * HEADS + h, a, min(a + 4, t + 1)) for a in range(0, t + 1, 4)]
        first.append(len(groups))
        U = NT * HEADS
        STEPS = 7
        step_of_head = {1: 0, 2: 1, 3: 2, 6: 3, 7: 4, 8: 5, 9: 6}
        ROTATE_AT = 4

        def shape(u):
            t, h = divmod(u, HEADS)
            r0, n = CHUNKS[t]
            kl = META + P * t
            base = 0 if u % 2 == 0 else 3 * BANK - max(0, kl - 2 * BANK)
            return t, h, n, kl, base

        def keys(j):
            return (0, META) if j == 0 else (META + P * (j - 1), P)

        def pieces(a, b):
            while a < b:
                e = min(b, (a // BANK + 1) * BANK)
                yield a, e
                a = e

        with nc.Block() as block:
            @block.sync
            def _(sp):
                def load(t):
                    r0, n = CHUNKS[t]
                    sp.dma_start(gm[:, t % 2, :, 0:n], d["projT"][GM0:GM0 + KD, :, r0:r0 + n].rearrange("c p r -> p c r")).then_inc(gm_loaded[t % 2], 16)
                    sp.dma_start(mix[:, t % 2, :, 0:n], d["mixT"][:, :, r0:r0 + n].rearrange("c p r -> p c r")).then_inc(gm_loaded[t % 2], 16)

                sp.dma_start(wuq[:], d["w_uq"][0].rearrange("(c p) h n -> p c (h n)", p=P)).then_inc(loaded, 16)
                sp.dma_start(future[:], d["c_future"]).then_inc(loaded, 16)
                load(0)
                load(1)
                for t in range(NT):
                    r0, n = CHUNKS[t]
                    sp.wait_ge(mixed, HEADS * (t + 1))
                    sp.dma_start(d["mixT"][:, :, r0:r0 + n].rearrange("c p r -> p c r"), mix[:, t % 2, :, 0:n]).then_inc(mix_stored[t % 2], 16)
                    if t + 2 < NT:
                        sp.wait_ge(mix_stored[t % 2], 16 * (t // 2 + 1))
                        load(t + 2)
                sp.wait_ge(mix_stored[0], 16 * 5)
                sp.wait_ge(mix_stored[1], 16 * 4)

            @block.gpsimd
            def _(pool):
                nc.gpsimd.memset(zero[:], 0.0).then_inc(zero_made, 1)
                pool.wait_ge(zero_made, 1)
                with pool.Fori(2 * ROWS // P, BLOCKS) as b:
                    pool.dma_start(d["expert_out"][bass.ds(b * P, P), :], zero[:]).then_inc(zeroed, 16)
                pool.wait_ge(zeroed, 16 * (BLOCKS - 2 * ROWS // P))

            @block.tensor
            def _(pe):
                def make_queries(t, step):
                    r0, n = TILES[t]
                    if STEPS * t + step:
                        pe.wait_ge(mid_kept, STEPS * t + step)
                    if step < 3:
                        for c in range(KQ):
                            last = nc.tensor.matmul(mid[0:n], k.qlT[:, c, r0:r0 + n], wuq[:, c, step * BANK:(step + 1) * BANK],
                                                    start=(c == 0), stop=(c == KQ - 1))
                    else:
                        pe.wait_ge(roped, t + 1)
                        for x in range(4):
                            last = nc.tensor.transpose(mid[0:QK, x * P:x * P + n], q[0:n, 4 * (step - 3) + x, :], k.ident[0:n, 0:n])
                    last.then_inc(mid_made, 1)

                def scores(u, middle):
                    t, h, n, kl, base = shape(u)
                    q0 = NS if t == 0 else 0
                    for a, e in pieces(base, base + kl):
                        if (a // BANK == 2) != middle:
                            continue
                        last = nc.tensor.matmul(scf[0:n, a:e], qT[:, t % 2, h, q0:q0 + n], k.keyT[0:QK, h, a - base:e - base], start=True, stop=False, skip_group_check=True)
                    m0 = base + kl - n
                    for a, e in pieces(m0, m0 + n):
                        if (a // BANK == 2) == middle:
                            last = nc.tensor.matmul(scf[0:n, a:e], k.ident[0:n, 0:n], future[0:n, a - m0:e - m0], start=False, stop=True, skip_group_check=True)
                    return last

                def has_middle(u):
                    return shape(u)[3] > 2 * BANK

                def turn(u):
                    t, h, n, kl, base = shape(u)
                    pe.wait_ge(normed, u + 1)
                    for g in range(first[u], first[u + 1]):
                        if g >= 2:
                            pe.wait_ge(pT_kept, g - 1)
                        for j in range(groups[g][1], groups[g][2]):
                            k0, kn = keys(j)
                            last = nc.tensor.transpose(tp[0:kn, g % 2, j - groups[g][1], 0:n], p[0:n, u % 3, k0:k0 + kn], k.ident[0:n, 0:n])
                        last.then_inc(p_turned, 1)

                def values(u):
                    t, h, n, kl, base = shape(u)
                    if u:
                        pe.wait_ge(gated, u)
                    for g in range(first[u], first[u + 1]):
                        pe.wait_ge(pT_kept, g + 1)
                        for j in range(groups[g][1], groups[g][2]):
                            kn = keys(j)[1]
                            last = nc.tensor.matmul(op[:, 0:n], k.val[0:kn, j, (h // 2) * P:(h // 2 + 1) * P],
                                                    pT[0:kn, g % 3, j - groups[g][1], 0:n], start=(j == 0), stop=(j == t))
                    last.then_inc(valued, 1)

                pe.wait_ge(loaded, 32)
                for step in range(STEPS):
                    make_queries(0, step)
                for u in range(U + 2):
                    if u >= 2:
                        turn(u - 2)
                    if u < U:
                        t, h = divmod(u, HEADS)
                        if h == 0:
                            pe.wait_ge(mid_kept, STEPS * (t + 1))
                        if u >= 2:
                            pe.wait_ge(expd, u - 1)
                        last = scores(u, False)
                        if not has_middle(u):
                            last.then_inc(scored, 1)
                        if h in step_of_head and t + 1 < NT:
                            make_queries(t + 1, step_of_head[h])
                    if u >= 2:
                        values(u - 2)
                    if u < U and has_middle(u):
                        pe.wait_ge(expd, u)
                        scores(u, True).then_inc(scored, 1)

            @block.vector
            def _(dve):
                def rotate(t):
                    n = TILES[t][1]
                    cos = k.rope[0:n, t, 0:HALF].unsqueeze(1).to_broadcast([n, HEADS, HALF])
                    sin = k.rope[0:n, t, HALF:ROPE].unsqueeze(1).to_broadcast([n, HEADS, HALF])
                    x1, x2 = q[0:n, :, NOPE:NOPE + HALF], q[0:n, :, NOPE + HALF:QK]
                    dve.wait_ge(mid_kept, STEPS * t + 3)
                    nc.vector.tensor_tensor(t1[0:n, :, 0, :], x1, cos, ALU.mult)
                    nc.vector.tensor_tensor(t1[0:n, :, 1, :], x2, cos, ALU.mult)
                    nc.vector.tensor_tensor(t2[0:n, :, 0, :], x2, sin, ALU.mult)
                    nc.vector.tensor_tensor(t2[0:n, :, 1, :], x1, sin, ALU.mult).then_inc(rotated, 1)
                    dve.wait_ge(rotated, t + 1)
                    nc.vector.tensor_tensor(x1, t1[0:n, :, 0, :], t2[0:n, :, 0, :], ALU.subtract)
                    nc.vector.tensor_tensor(x2, t1[0:n, :, 1, :], t2[0:n, :, 1, :], ALU.add).then_inc(roped, 1)

                def softmax_max(u):
                    t, h, n, kl, base = shape(u)
                    i = u % 2
                    dve.wait_ge(scored, u + 1)
                    nc.vector.reduce_max(mx[0:n, i:i + 1], scf[0:n, base:base + kl], AX_X).then_inc(maxed, 1)
                    dve.wait_ge(maxed, u + 1)
                    nc.vector.tensor_scalar(nm[0:n, i:i + 1], mx[0:n, i:i + 1], -MLA_SCALE, None, ALU.mult).then_inc(negated, 1)

                def normalise(u):
                    t, h, n, kl, base = shape(u)
                    i = u % 2
                    dve.wait_ge(expd, u + 1)
                    nc.vector.reciprocal(il[0:n, i:i + 1], l[0:n, i:i + 1]).then_inc(inverted, 1)
                    dve.wait_ge(inverted, u + 1)
                    nc.vector.tensor_scalar(p[0:n, u % 3, 0:kl], p[0:n, u % 3, 0:kl], il[0:n, i:i + 1], None, ALU.mult).then_inc(normed, 1)

                def gate(u):
                    t, h, n, kl, base = shape(u)
                    half = slice(NOPE * (h % 2), NOPE * (h % 2) + NOPE)
                    dve.wait_ge(valued, u + 1)
                    if h == 0:
                        dve.wait_ge(gm_loaded[t % 2], 32 * (t // 2 + 1))
                    nc.vector.tensor_tensor(og[half, 0:n], op[half, 0:n], gm[half, t % 2, h // 2, 0:n], ALU.mult).then_inc(gated, 1)
                    dve.wait_ge(gated, u + 1)
                    nc.vector.tensor_tensor(mix[half, t % 2, h // 2, 0:n], mix[half, t % 2, h // 2, 0:n], og[half, 0:n], ALU.add).then_inc(mixed, 1)

                rotate(0)
                for u in range(U + 3):
                    if u >= 3:
                        gate(u - 3)
                    if 1 <= u <= U:
                        normalise(u - 1)
                    if u < U:
                        softmax_max(u)
                    t, h = divmod(u, HEADS)
                    if h == ROTATE_AT and t + 1 < NT:
                        rotate(t + 1)

            @block.scalar
            def _(act):
                def keep_queries(t, step):
                    m = TILES[t][1]
                    act.wait_ge(mid_made, STEPS * t + step + 1)
                    if step < 3:
                        to = q[0:m].rearrange("p h d -> p (h d)")[:, step * BANK:(step + 1) * BANK]
                        nc.scalar.copy(to, mid[0:m]).then_inc(mid_kept, 1)
                    else:
                        src = mid[0:QK].rearrange("p (x r) -> p x r", x=4)[:, :, 0:m]
                        nc.scalar.copy(qT[:, t % 2, 4 * (step - 3):4 * (step - 2), 0:m], src).then_inc(mid_kept, 1)

                def keep_turned(u):
                    for g in range(first[u], first[u + 1]):
                        x0, x1 = groups[g][1:]
                        m = shape(u)[2]
                        act.wait_ge(p_turned, g + 1)
                        if g >= 3:
                            act.wait_ge(valued, groups[g - 3][0] + 1)
                        if x0 == 0:
                            last = nc.scalar.copy(pT[0:META, g % 3, 0, 0:m], tp[0:META, g % 2, 0, 0:m])
                        lo = max(x0, 1)
                        if x1 > lo:
                            last = nc.scalar.copy(pT[:, g % 3, lo - x0:x1 - x0, 0:m], tp[:, g % 2, lo - x0:x1 - x0, 0:m])
                        last.then_inc(pT_kept, 1)

                for step in range(STEPS):
                    keep_queries(0, step)
                act.wait_ge(mid_kept, STEPS)
                nc.scalar.copy(k.q0T[:], qT[:, 0, :, 0:NS]).then_inc(q0_kept, 1)
                for u in range(U + 2):
                    if u >= 2:
                        keep_turned(u - 2)
                    if u < U:
                        t, h, n, kl, base = shape(u)
                        i = u % 2
                        act.wait_ge(negated, u + 1)
                        if u >= 3:
                            act.wait_ge(p_turned, first[u - 2])
                        nc.scalar.activation(p[0:n, u % 3, 0:kl], scf[0:n, base:base + kl], ACT.Exp, bias=nm[0:n, i:i + 1], scale=MLA_SCALE,
                                             accum_out=l[0:n, i:i + 1]).then_inc(expd, 1)
                        if h in step_of_head and t + 1 < NT:
                            keep_queries(t + 1, step_of_head[h])


def attend_sample(k):
    nc, d = k.nc, k.dram
    G = PAGES // 4
    W = HEADS
    STRIP = P + W
    with k.scope() as s:
        table = s.sb("as_table", [P, NS * PAGES], I32)
        table_f = s.sb("as_table_f", [P, G, 4, NS])
        quarter = s.sb("as_quarter", [P, 1])
        rows_of = s.sb("as_rows_of", [P, G, NS], I32)
        rows_now = s.sb("as_rows_now", [P, 3, NS], I32)
        wuv = s.sb("as_wuv", [P, 2, D])
        rep, pick = s.sb("as_rep", [NS, P]), s.sb("as_pick", [P, NS])
        qrp = s.sb("as_qrp", [QK, NS, W])
        qr4 = s.sb("as_qr4", [P, P])
        qlat = s.sb("as_qlat", [P, 2, P])
        qz = s.sb("as_qz", [P, 2, NS * STRIP])
        qzr = s.sb("as_qzr", [P, 4, NS * STRIP])
        lat = s.sb("as_lat", [P, 3, NS, 4 * CL])
        rop = s.sb("as_rop", [P, 3, NS, 4 * ROPE])
        spare = lat[:, 2].rearrange("p b n -> p (b n)")
        wuk = spare[:, 0:2 * HEADS * NOPE].rearrange("p (c n) -> p c n", c=2)
        wukT = spare[0:NOPE, 2 * HEADS * NOPE:2 * HEADS * NOPE + HEADS * CL].rearrange("p (h n) -> p h n", h=HEADS)
        cT = s.sb("as_cT", [P, 2, 2, BANK])
        rT = s.sb("as_rT", [P, 2, P])
        pr = s.sb("as_p", [P, BANK])
        pz = s.sb("as_pz", [P, 4, NS * STRIP])
        acc = s.sb("as_acc", [P, CL])
        m, nm, corr, rs = (s.sb(f"as_{n}", [P, 2]) for n in ("m", "nm", "corr", "rs"))
        smax, l, snew, pnew = (s.sb(f"as_{n}", [P, 1]) for n in ("smax", "l", "snew", "pnew"))
        newT = s.sb("as_newT", [P, 3, NS])
        picked = s.sb("as_picked", [P, NS])
        accT = s.sb("as_accT", [P, 2, P])
        gm, mix, og = (s.sb(f"as_{n}", [P, KD, NS]) for n in ("gm", "mix", "og"))
        tp = s.ps("as_tp", [P, 2, 3, BANK])
        sp_ = s.ps("as_s", [P, BANK])
        vp = s.ps("as_v", [P, BANK])
        loaded, setup, set_pe, repl = s.sem("as_loaded"), s.sem("as_setup"), s.sem("as_set_pe"), s.sem("as_repl")
        pages = [s.sem(f"as_pages{i}") for i in range(3)]
        placed, placed_f, rows_made, load_due = s.sem("as_placed"), s.sem("as_placed_f"), s.sem("as_rows_made"), s.sem("as_load_due")
        turned, kept_a, kept_v, unit_done = (s.sem(f"as_{n}") for n in ("turned", "kept_a", "kept_v", "unit_done"))
        cleared = s.sem("as_cleared")
        maxed, negated, expd, p_turned, pz_kept, pv_done, acc_kept = (s.sem(f"as_{n}") for n in (
            "maxed", "negated", "expd", "p_turned", "pz_kept", "pv_done", "acc_kept"))
        fin_v, fin_a, fin_p, stored = (s.sem(f"as_fin_{n}") for n in ("v", "a", "p", "stored"))

        lat_rows = d["cache_kv_latent"].rearrange("a g (q r) c -> (a g q) (r c)", r=4)
        rop_rows = d["cache_k_rope"].rearrange("a g (q r) c -> (a g q) (r c)", r=4)

        def strips(ap):
            return ap.rearrange("p (b x) -> p b x", x=STRIP)[:, :, 0:W]

        def turns(eng, body):
            for j in range(4):
                body(j, j % 2, j % 3, j // 3, j == 0)
            with eng.Fori(0, (G - 4) // 6) as i:
                for j in range(4, 10):
                    body(i * 6 + j, j % 2, j % 3, i * 2 + j // 3, False)

        with nc.Block() as block:
            @block.sync
            def _(sp):
                sp.dma_start(table[:], d["page_table"].rearrange("b n -> (b n)").partition_broadcast(P)).then_inc(placed, 16)
                sp.dma_start(quarter[:], d["c_quarter"]).then_inc(placed, 16)
                sp.dma_start(wuk, d["w_uk"][0].rearrange("(c p) h n -> p c (h n)", p=P)).then_inc(loaded, 16)
                sp.dma_start(wuv[:], d["w_uv"][0].rearrange("(c p) h n -> p c (h n)", p=P)).then_inc(loaded, 16)
                sp.dma_start(rep[:], d["c_rep16"]).then_inc(loaded, 16)
                sp.dma_start(pick[:], d["c_pick16"]).then_inc(loaded, 16)
                sp.dma_start(gm[:], d["projT"][GM0:GM0 + KD, :, 0:NS].rearrange("c p r -> p c r")).then_inc(loaded, 16)
                sp.dma_start(mix[:], d["mixT"][:, :, 0:NS].rearrange("c p r -> p c r")).then_inc(loaded, 16)
                sp.wait_ge(fin_v, 13)
                sp.dma_start(d["mixT"][:, :, 0:NS].rearrange("c p r -> p c r"), mix[:]).then_inc(stored, 16)
                sp.wait_ge(stored, 16)

            @block.gpsimd
            def _(pool):
                def load(j, x, y, rounds, first):
                    if not isinstance(j, int) or j >= 3:
                        pool.wait_ge(pv_done, j - 2)
                        pool.sem_inc(load_due, 1)
                    nc.gpsimd.tensor_copy(rows_now[:, y, :], rows_of[:, bass.ds(j, 1), :].rearrange("p g b -> p (g b)")).then_inc(rows_made, 1)
                    pool.wait_ge(rows_made, j + 1)
                    pool.sem_inc(load_due, 1)
                    for b in range(NS):
                        at = bass.IndirectOffsetOnAxis(ap=rows_now[:, y, b:b + 1], axis=0)
                        nc.gpsimd.indirect_dma_start(out=lat[:, y, b, :], out_offset=None, in_=lat_rows, in_offset=at).then_inc(pages[y], 16)
                        nc.gpsimd.indirect_dma_start(out=rop[:, y, b, :], out_offset=None, in_=rop_rows, in_offset=at).then_inc(pages[y], 16)
                    if isinstance(j, int) and j == 1:
                        prepare()

                def prepare():
                    nc.gpsimd.memset(qz[:], 0.0)
                    nc.gpsimd.memset(qzr[:], 0.0)
                    nc.gpsimd.memset(pz[:], 0.0)
                    nc.gpsimd.memset(acc[:], 0.0)
                    nc.gpsimd.memset(l[:], 0.0)
                    nc.gpsimd.memset(m[:], NEG).then_inc(cleared, 1)
                    pool.wait_ge(setup, 1)
                    for r in range(4):
                        pool.dma_start(qr4[32 * r:32 * r + 32, :], qrp[NOPE:QK].rearrange("p b h -> p (b h)")).then_inc(repl, 16)
                    pool.wait_ge(set_pe, 9)

                pool.wait_ge(placed_f, 2)
                turns(pool, load)

            @block.tensor
            def _(pe):
                pe.wait_ge(loaded, 16 * 6)
                for u in range(8):
                    if u >= 2:
                        pe.wait_ge(setup, u)
                    for x in range(4):
                        h, c = 2 * u + x // 2, x % 2
                        last = nc.tensor.transpose(tp[0:NOPE, u % 2, 0, x * P:(x + 1) * P], wuk[:, c, h * NOPE:(h + 1) * NOPE], k.ident[:])
                    last.then_inc(set_pe, 1)
                pe.wait_ge(setup, 9)
                for c in range(2):
                    for h in range(HEADS):
                        nc.tensor.matmul(vp[:, c * P + h:(c + 1) * P:W], wukT[:, h, c * P:(c + 1) * P], k.q0T[0:NOPE, h, :], start=True, stop=True)
                nc.tensor.transpose(vp[:, 256:256 + NS], k.new_row[:, 0:P], k.ident[0:NS, 0:NS])
                nc.tensor.transpose(vp[:, 264:264 + NS], k.new_row[:, P:2 * P], k.ident[0:NS, 0:NS])
                nc.tensor.transpose(vp[0:ROPE, 272:272 + NS], k.new_row[:, CL:CK], k.ident[0:NS, 0:NS]).then_inc(set_pe, 1)
                pe.wait_ge(setup, 11)

                def finish(j):
                    pe.wait_ge(expd, j * 2 + 2)
                    pe.wait_ge(acc_kept, j)
                    for r in range(4):
                        last = nc.tensor.transpose(vp[:, r * P:(r + 1) * P], pr[:, r * P:(r + 1) * P], k.ident[:])
                    last.then_inc(p_turned, 1)

                def products(j, y):
                    pe.wait_ge(pz_kept, j + 1)
                    for b in range(NS):
                        for r in range(4):
                            last = nc.tensor.matmul(vp[:, 0:CL], pz[:, r, b * P:(b + 1) * P], lat[:, y, b, r * CL:(r + 1) * CL],
                                                    start=(b == 0 and r == 0), stop=(b == NS - 1 and r == 3))
                    last.then_inc(pv_done, 1)

                def group(j, x, y, rounds, first):
                    def turn(b):
                        if b >= 2 or not first:
                            pe.wait_ge(kept_a, j * 8 + (b - 1))
                            pe.wait_ge(kept_v, j * 8 + (b - 1))
                        bank = tp[:, b % 2]
                        for c in range(2):
                            for r in range(4):
                                nc.tensor.transpose(bank[:, c, r * P:(r + 1) * P], lat[:, y, b, r * CL + c * P:r * CL + (c + 1) * P], k.ident[:])
                        nc.tensor.transpose(bank[:, 2, 0:P], rop[:, y, b, :], k.ident[:]).then_inc(turned, 1)

                    def score(b):
                        pe.wait_ge(kept_a, j * 8 + (b + 1))
                        pe.wait_ge(kept_v, j * 8 + (b + 1))
                        if b == 0 and not first:
                            pe.wait_ge(expd, j * 2)
                        for c in range(2):
                            nc.tensor.matmul(sp_[:], qz[:, c, b * P:(b + 1) * P], cT[:, b % 2, c, :],
                                             start=(b == 0 and c == 0), stop=False, skip_group_check=True)
                        for r in range(4):
                            last = nc.tensor.matmul(sp_[:, r * P:(r + 1) * P], qzr[:, r, b * P:(b + 1) * P], rT[:, b % 2, :], start=False,
                                                    stop=(b == NS - 1), skip_group_check=True)
                        last.then_inc(unit_done, 1)

                    pe.wait_ge(pages[y], (rounds + 1) * (2 * NS * 16))
                    turn(0)
                    for b in range(NS):
                        if b < NS - 1:
                            turn(b + 1)
                        score(b)
                        if b == 1 and not first:
                            finish(j - 1)
                        if b == 2 and not first:
                            products(j - 1, (y + 2) % 3)

                turns(pe, group)
                finish(G - 1)
                products(G - 1, (G - 1) % 3)
                pe.wait_ge(acc_kept, G)
                for c in range(2):
                    nc.tensor.matmul(vp[:, 0:NS], qlat[:, c, :], newT[:, c, :], start=(c == 0), stop=False)
                nc.tensor.matmul(vp[:, 0:NS], qr4[0:ROPE, :], newT[0:ROPE, 2, :], start=False, stop=True)
                nc.tensor.matmul(sp_[:, 0:CL], rep[:], k.new_row[:, 0:CL], start=True, stop=True).then_inc(fin_p, 1)
                pe.wait_ge(fin_v, 10)
                for c in range(2):
                    last = nc.tensor.transpose(vp[:, c * P:(c + 1) * P], acc[:, c * P:(c + 1) * P], k.ident[:])
                last.then_inc(fin_p, 1)
                pe.wait_ge(fin_v, 11)
                for h in range(HEADS):
                    for c in range(2):
                        last = nc.tensor.matmul(sp_[:, h * NS:(h + 1) * NS], wuv[:, c, (h // 2) * P:(h // 2 + 1) * P],
                                                accT[:, c, h::W], start=(c == 0), stop=(c == 1))
                last.then_inc(fin_p, 1)

            @block.vector
            def _(dve):
                dve.wait_ge(placed, 32)
                nc.vector.tensor_copy(table_f[:], table[:].rearrange("p (b j i) -> p j i b", b=NS, i=4)).then_inc(placed_f, 1)
                dve.wait_ge(placed_f, 1)
                for i in range(4):
                    rows = slice(32 * i, 32 * i + 32)
                    last = nc.vector.tensor_scalar(rows_of[rows], table_f[rows, :, i, :], float(PAGE // 4), quarter[rows], ALU.mult, ALU.add)
                last.then_inc(placed_f, 1)
                nc.vector.tensor_copy(qrp[NOPE:QK].rearrange("p b h -> p h b"), k.q0T[NOPE:QK]).then_inc(setup, 1)
                for u in range(8):
                    dve.wait_ge(set_pe, u + 1)
                    nc.vector.tensor_copy(wukT[:, 2 * u:2 * u + 2, :], tp[0:NOPE, u % 2, 0, :].rearrange("p (h c) -> p h c", h=2)).then_inc(setup, 1)
                dve.wait_ge(set_pe, 9)
                dve.wait_ge(cleared, 1)
                dve.wait_ge(repl, 64)
                nc.vector.tensor_copy(qlat[:], vp[:, 0:2 * P].rearrange("p (c x) -> p c x", c=2)).then_inc(setup, 1)
                nc.vector.tensor_copy(newT[:, 0:2, :], vp[:, 256:272].rearrange("p (c x) -> p c x", c=2))
                nc.vector.tensor_copy(newT[0:ROPE, 2, :], vp[0:ROPE, 272:280])
                for c in range(2):
                    nc.vector.tensor_copy(strips(qz[:, c, :]), vp[:, c * P:(c + 1) * P].rearrange("p (b h) -> p b h", h=W))
                for r in range(4):
                    rows = slice(32 * r, 32 * r + 32)
                    last = nc.vector.tensor_copy(strips(qzr[rows, r, :]), qr4[rows].rearrange("p (b h) -> p b h", h=W))
                last.then_inc(setup, 1)

                def finish(j, x):
                    dve.wait_ge(p_turned, j + 1)
                    for r in range(4):
                        last = nc.vector.tensor_copy(strips(pz[:, r, :]), vp[:, r * P:(r + 1) * P].rearrange("p (b h) -> p b h", h=W))
                    last.then_inc(pz_kept, 1)
                    nc.vector.scalar_tensor_tensor(out=l[:], in0=l[:], scalar=corr[:, x:x + 1], in1=rs[:, x:x + 1], op0=ALU.mult, op1=ALU.add)

                def collect(j, x):
                    dve.wait_ge(pv_done, j + 1)
                    nc.vector.scalar_tensor_tensor(out=acc[:], in0=acc[:], scalar=corr[:, x:x + 1], in1=vp[:, 0:CL],
                                                   op0=ALU.mult, op1=ALU.add).then_inc(acc_kept, 1)

                def group(j, x, y, rounds, first):
                    for b in range(NS):
                        dve.wait_ge(turned, j * 8 + (b + 1))
                        if b >= 2 or not first:
                            dve.wait_ge(unit_done, j * 8 + (b - 1))
                        nc.vector.tensor_copy(cT[:, b % 2, 1, :], tp[:, b % 2, 1, :])
                        nc.vector.tensor_copy(rT[:, b % 2, :], tp[:, b % 2, 2, 0:P]).then_inc(kept_v, 1)
                        if b == 2 and not first:
                            finish(j - 1, 1 - x)
                        if b == 3 and not first:
                            collect(j - 1, 1 - x)
                    dve.wait_ge(unit_done, j * 8 + 8)
                    nc.vector.reduce_max(smax[:], sp_[:], AX_X).then_inc(maxed, 1)
                    dve.wait_ge(maxed, j * 2 + 1)
                    nc.vector.tensor_tensor(m[:, 1 - x:2 - x], m[:, x:x + 1], smax[:], ALU.max).then_inc(maxed, 1)
                    dve.wait_ge(maxed, j * 2 + 2)
                    nc.vector.tensor_scalar(nm[:, x:x + 1], m[:, 1 - x:2 - x], -MLA_SCALE, None, ALU.mult).then_inc(negated, 1)

                turns(dve, group)
                finish(G - 1, 1)
                collect(G - 1, 1)
                link = chained(dve, fin_v)
                dve.wait_ge(fin_p, 1)
                link(nc.vector.tensor_tensor(picked[:], vp[:, 0:NS], pick[:], ALU.mult))
                link(nc.vector.reduce_sum(snew[:], picked[:], AX_X))
                link(nc.vector.tensor_tensor(m[:, 1:2], m[:, 0:1], snew[:], ALU.max))
                link(nc.vector.tensor_scalar(nm[:, 0:1], m[:, 1:2], -MLA_SCALE, None, ALU.mult))
                dve.wait_ge(fin_a, 2)
                dve.wait_ge(acc_kept, G)
                link(nc.vector.tensor_scalar(acc[:], acc[:], corr[:, 0:1], None, ALU.mult))
                link(nc.vector.scalar_tensor_tensor(out=acc[:], in0=sp_[:, 0:CL], scalar=pnew[:], in1=acc[:], op0=ALU.mult, op1=ALU.add))
                link(nc.vector.tensor_tensor(l[:], l[:], corr[:, 0:1], ALU.mult))
                link(nc.vector.tensor_tensor(l[:], l[:], pnew[:], ALU.add))
                link(nc.vector.reciprocal(l[:], l[:]))
                link(nc.vector.tensor_scalar(acc[:], acc[:], l[:], None, ALU.mult))
                dve.wait_ge(fin_p, 2)
                link(nc.vector.tensor_copy(accT[:], vp[:, 0:2 * P].rearrange("p (c x) -> p c x", c=2)))
                dve.wait_ge(fin_p, 3)
                for half in (slice(0, NOPE), slice(NOPE, P)):
                    par = 0 if half.start == 0 else 1
                    last = nc.vector.tensor_tensor(og[half], sp_[half, 0:P].rearrange("p (c y b) -> p c y b", y=2, b=NS)[:, :, par, :],
                                                   gm[half], ALU.mult)
                link(last)
                link(nc.vector.tensor_tensor(mix[:], mix[:], og[:], ALU.add))

            @block.scalar
            def _(act):
                def group(j, x, y, rounds, first):
                    for b in range(NS):
                        act.wait_ge(turned, j * 8 + (b + 1))
                        if b >= 2 or not first:
                            act.wait_ge(unit_done, j * 8 + (b - 1))
                        nc.scalar.copy(cT[:, b % 2, 0, :], tp[:, b % 2, 0, :]).then_inc(kept_a, 1)
                    act.wait_ge(negated, j + 1)
                    if not first:
                        act.wait_ge(p_turned, j)
                    nc.scalar.activation(corr[:, x:x + 1], m[:, x:x + 1], ACT.Exp, bias=nm[:, x:x + 1], scale=MLA_SCALE).then_inc(expd, 1)
                    nc.scalar.activation(pr[:], sp_[:], ACT.Exp, bias=nm[:, x:x + 1], scale=MLA_SCALE, accum_out=rs[:, x:x + 1]).then_inc(expd, 1)

                turns(act, group)
                act.wait_ge(fin_v, 4)
                nc.scalar.activation(corr[:, 0:1], m[:, 0:1], ACT.Exp, bias=nm[:, 0:1], scale=MLA_SCALE).then_inc(fin_a, 1)
                nc.scalar.activation(pnew[:], snew[:], ACT.Exp, bias=nm[:, 0:1], scale=MLA_SCALE).then_inc(fin_a, 1)


def project_output(k):
    nc, d = k.nc, k.dram
    NL = GROUPS + EXPERTS
    with k.scope() as s:
        w = s.sb("po_w", [P, KD, D])
        mix = s.sb("po_mix", [P, KD, ROWS])
        wr = s.sb("po_wr", [P, KD, NL])
        br = s.sb("po_br", [P, NL])
        nf = s.sb("po_nf", [P, D])
        x, h = s.sb("po_x", [P, 2, D]), s.sb("po_h", [P, 2, D])
        square = s.sb("po_square", [P, D])
        hT = s.sb("po_hT", [P, KD, P])
        ss, mean, inv, rstd = (s.sb(f"po_{n}", [P, NT]) for n in ("ss", "mean", "inv", "rstd"))
        acc = s.ps("po_acc", [P, 2, 2, BANK])
        turned = s.ps("po_turned", [P, KD, P])
        lps = s.ps("po_lps", [P, BANK])
        loaded = s.sem("po_loaded")
        x_loaded = [s.sem(f"po_x_loaded{i}") for i in range(2)]
        stored = [s.sem(f"po_stored{i}") for i in range(2)]
        made, added, squared, meaned, inverted, rooted, normed, turn_done, hT_kept, routed, logits_kept = (
            s.sem(f"po_{n}") for n in ("made", "added", "squared", "meaned", "inverted", "rooted", "normed", "turned",
                                       "hT_kept", "routed", "logits_kept"))
        with nc.Block() as block:
            @block.sync
            def _(sp):
                sp.dma_start(w[:], d["w_out"][0].rearrange("(c p) n -> p c n", p=P)).then_inc(loaded, 16)
                sp.dma_start(mix[:], d["mixT"].rearrange("c p r -> p c r")).then_inc(loaded, 16)
                sp.dma_start(wr[:, :, 0:GROUPS], d["w_group"][0].rearrange("(c p) n -> p c n", p=P)).then_inc(loaded, 16)
                sp.dma_start(wr[:, :, GROUPS:NL], d["w_router"][0].rearrange("(c p) n -> p c n", p=P)).then_inc(loaded, 16)
                sp.dma_start(br[:, 0:GROUPS], d["b_group"][0].partition_broadcast(P)).then_inc(loaded, 16)
                sp.dma_start(br[:, GROUPS:NL], d["b_router"][0].partition_broadcast(P)).then_inc(loaded, 16)
                sp.dma_start(nf[:], d["norm_ffn"][0].partition_broadcast(P)).then_inc(loaded, 16)
                for t in range(NT):
                    if t >= 2:
                        sp.wait_ge(stored[t % 2], 32 * (t // 2))
                    if t == 0:
                        sp.dma_start(x[0:NS, 0, :], d["x_sample"].rearrange("b t d -> (b t) d")).then_inc(x_loaded[0], 16)
                        sp.dma_start(x[NS:HEAD_ROWS, 0, :], d["meta_tokens"]).then_inc(x_loaded[0], 16)
                    else:
                        sp.dma_start(x[:, t % 2, :], d["x_prompt"][0, (t - 1) * P:t * P, :]).then_inc(x_loaded[t % 2], 16)

            @block.gpsimd
            def _(pool):
                for t, (r0, n) in enumerate(TILES):
                    pool.wait_ge(added, t + 1)
                    pool.wait_ge(normed, t + 1)
                    pool.dma_start(d["resid"][r0:r0 + n, :], x[0:n, t % 2, :]).then_inc(stored[t % 2], 16)
                    pool.dma_start(d["ffn_in"][r0:r0 + n, :], h[0:n, t % 2, :]).then_inc(stored[t % 2], 16)
                pool.wait_ge(stored[0], 32 * 5)
                pool.wait_ge(stored[1], 32 * 4)

            @block.tensor
            def _(pe):
                def route(t):
                    n = TILES[t][1]
                    pe.wait_ge(normed, t + 1)
                    if t:
                        pe.wait_ge(hT_kept, t)
                    for c in range(KD):
                        last = nc.tensor.transpose(turned[:, c, 0:n], h[0:n, t % 2, c * P:(c + 1) * P], k.ident[0:n, 0:n])
                    last.then_inc(turn_done, 1)
                    pe.wait_ge(hT_kept, t + 1)
                    if t:
                        pe.wait_ge(logits_kept, t)
                    for c in range(KD):
                        last = nc.tensor.matmul(lps[0:n, 0:NL], hT[:, c, 0:n], wr[:, c, :], start=(c == 0), stop=(c == KD - 1))
                    last.then_inc(routed, 1)

                pe.wait_ge(loaded, 16 * 7)
                for t, (r0, n) in enumerate(TILES):
                    if t >= 2:
                        pe.wait_ge(added, t - 1)
                    for b in range(2):
                        for c in range(KD):
                            last = nc.tensor.matmul(acc[0:n, t % 2, b, :], mix[:, c, r0:r0 + n], w[:, c, b * BANK:(b + 1) * BANK],
                                                    start=(c == 0), stop=(c == KD - 1))
                    last.then_inc(made, 1)
                    if t:
                        route(t - 1)
                route(NT - 1)

            @block.vector
            def _(dve):
                nc.vector.memset(k.logits[:], 0.0)
                dve.wait_ge(loaded, 16 * 7)

                def keep_logits(t):
                    n = TILES[t][1]
                    dve.wait_ge(routed, t + 1)
                    nc.vector.tensor_tensor(k.logits[0:n, t, :], lps[0:n, 0:NL], br[0:n, :], ALU.add).then_inc(logits_kept, 1)

                for t, (r0, n) in enumerate(TILES):
                    i = t % 2
                    dve.wait_ge(x_loaded[i], 16 * (t // 2 + 1) + (16 if i == 0 else 0))
                    dve.wait_ge(made, t + 1)
                    nc.vector.tensor_tensor(x[0:n, i, :].rearrange("p (b n) -> p b n", b=2), x[0:n, i, :].rearrange("p (b n) -> p b n", b=2),
                                            acc[0:n, i], ALU.add).then_inc(added, 1)
                    dve.wait_ge(squared, t + 1)
                    nc.vector.tensor_scalar(mean[0:n, t:t + 1], ss[0:n, t:t + 1], 1.0 / D, EPS, ALU.mult, ALU.add).then_inc(meaned, 1)
                    dve.wait_ge(meaned, t + 1)
                    nc.vector.reciprocal(inv[0:n, t:t + 1], mean[0:n, t:t + 1]).then_inc(inverted, 1)
                    dve.wait_ge(rooted, t + 1)
                    if t >= 2:
                        dve.wait_ge(stored[i], 32 * (t // 2))
                        dve.wait_ge(turn_done, t - 1)
                    nc.vector.scalar_tensor_tensor(out=h[0:n, i, :], in0=x[0:n, i, :], scalar=rstd[0:n, t:t + 1], in1=nf[0:n, :],
                                                   op0=ALU.mult, op1=ALU.mult).then_inc(normed, 1)
                    if t:
                        keep_logits(t - 1)
                keep_logits(NT - 1)

            @block.scalar
            def _(act):
                def keep(t):
                    n = TILES[t][1]
                    act.wait_ge(turn_done, t + 1)
                    if t:
                        act.wait_ge(routed, t)
                    nc.scalar.copy(hT[:, :, 0:n], turned[:, :, 0:n]).then_inc(hT_kept, 1)

                for t, (r0, n) in enumerate(TILES):
                    act.wait_ge(added, t + 1)
                    if t:
                        act.wait_ge(squared, t)
                    nc.scalar.activation(square[0:n, :], x[0:n, t % 2, :], ACT.Square, accum_out=ss[0:n, t:t + 1]).then_inc(squared, 1)
                    act.wait_ge(inverted, t + 1)
                    nc.scalar.activation(rstd[0:n, t:t + 1], inv[0:n, t:t + 1], ACT.Sqrt).then_inc(rooted, 1)
                    if t:
                        keep(t - 1)
                keep(NT - 1)


def route(k):
    nc, d = k.nc, k.dram
    with k.scope() as s:
        before = s.sb("ro_before", [P, P])
        iota = s.sb("ro_iota", [P, 64])
        valid = s.sb("ro_valid", [P, NT])
        token = s.sb("ro_token", [P, NT], I32)
        zero = s.sb("ro_zero", [P, BLOCKS], I32)
        gmax, gsum, gate, vmin, m1, m2, dd, ed, rec = (s.sb(f"ro_{n}", [P, NT]) for n in (
            "gmax", "gsum", "gate", "vmin", "m1", "m2", "dd", "ed", "rec"))
        gd, eq4, og, pen = (s.sb(f"ro_{n}", [P, NT, GROUPS]) for n in ("gd", "eq4", "og", "pen"))
        lem, eq, A1, A2, M, pos, tmp = (s.sb(f"ro_{n}", [P, NT, EXPERTS]) for n in ("lem", "eq", "a1", "a2", "m", "pos", "tmp"))
        base = s.sb("ro_base", [P, NT + 1, EXPERTS])
        nbi = s.sb("ro_nbi", [P, EXPERTS], I32)
        nb, incl, start, zeros = (s.sb(f"ro_{n}", [P, EXPERTS]) for n in ("nb", "incl", "start", "zeros"))
        destf = s.sb("ro_destf", [P, 2, NT])
        cmp = s.sb("ro_cmp", [1, BLOCKS, EXPERTS])
        bef = s.sb("ro_bef", [1, BLOCKS])
        rank_ps = s.ps("ro_rank", [P, NT, EXPERTS])
        tot_ps = s.ps("ro_tot", [P, NT, EXPERTS])
        loaded, step, acted, summed = s.sem("ro_loaded"), s.sem("ro_step"), s.sem("ro_acted"), s.sem("ro_summed")
        exps_asked, weights_asked, counted, placed = (s.sem(f"ro_{n}") for n in ("exps_asked", "weights_asked", "counted", "placed"))
        cleared, zeroed, scattered = s.sem("ro_cleared"), s.sem("ro_zeroed"), s.sem("ro_scattered")
        lg = k.logits[:, :, 0:GROUPS]
        le = k.logits[:, :, GROUPS:]

        def per_tile(ap, w):
            return ap.unsqueeze(2).to_broadcast([P, NT, w])

        with nc.Block() as block:
            @block.sync
            def _(sp):
                sp.dma_start(before[:], d["c_before"]).then_inc(loaded, 16)
                sp.dma_start(iota[:], d["c_iota"]).then_inc(loaded, 16)
                sp.dma_start(valid[:], d["c_valid"]).then_inc(loaded, 16)
                sp.dma_start(token[:], d["c_token"]).then_inc(loaded, 16)

            @block.gpsimd
            def _(pool):
                nc.gpsimd.memset(zero[:], 0).then_inc(cleared, 1)
                pool.wait_ge(cleared, 1)
                pool.dma_start(d["slot_token"].rearrange("(p b) o -> p (b o)", p=P), zero[:]).then_inc(zeroed, 16)
                pool.wait_ge(zeroed, 16)
                pool.wait_ge(loaded, 64)
                pool.wait_ge(placed, 1)
                for t, (r0, n) in enumerate(TILES):
                    for i in range(2):
                        nc.gpsimd.indirect_dma_start(
                            out=d["slot_token"], out_offset=bass.IndirectOffsetOnAxis(ap=k.dest[0:n, i, t:t + 1], axis=0),
                            in_=token[0:n, t:t + 1], in_offset=None).then_inc(scattered, 16)
                pool.wait_ge(scattered, 16 * 2 * NT)

            @block.tensor
            def _(pe):
                pe.wait_ge(counted, 1)
                nc.tensor.matmul(rank_ps[:], before[:], M[:], start=True, stop=True)
                nc.tensor.matmul(tot_ps[:], k.ones[:], M[:], start=True, stop=True).then_inc(summed, 1)

            @block.scalar
            def _(act):
                act.wait_ge(exps_asked, 1)
                nc.scalar.activation(gd[:], gd[:], ACT.Exp).then_inc(acted, 1)
                act.wait_ge(weights_asked, 1)
                nc.scalar.activation(ed[:], dd[:], ACT.Exp).then_inc(acted, 1)

            @block.vector
            def _(dve):
                link = chained(dve, step)
                V = nc.vector

                def first_of(out, x, top, width, scratch):
                    link(V.tensor_tensor(scratch, x, per_tile(top, width), ALU.is_equal))
                    link(V.scalar_tensor_tensor(out=scratch, in0=scratch, scalar=-64.0,
                                                in1=iota[:, 0:width].unsqueeze(1).to_broadcast([P, NT, width]), op0=ALU.mult, op1=ALU.add))
                    link(V.tensor_reduce(vmin[:], scratch, AX_X, ALU.min))
                    link(V.tensor_tensor(out, scratch, per_tile(vmin[:], width), ALU.is_equal))

                dve.wait_ge(loaded, 64)
                V.memset(zeros[:], 0.0)
                V.memset(base[:, 0, :], 0.0)
                link(V.reduce_max(gmax[:], lg, AX_X))
                V.tensor_tensor(gd[:], lg, per_tile(gmax[:], GROUPS), ALU.subtract).then_inc(exps_asked, 1)
                first_of(og[:], lg, gmax[:], GROUPS, eq4[:])
                link(V.tensor_scalar(pen[:], og[:], 1.0, -NEG, ALU.subtract, ALU.mult))
                for t in range(NT):
                    last = V.tensor_tensor(lem[:, t, :].rearrange("p (g e) -> p g e", g=GROUPS), le[:, t, :].rearrange("p (g e) -> p g e", g=GROUPS),
                                           pen[:, t, :].unsqueeze(2).to_broadcast([P, GROUPS, PER_GROUP]), ALU.add)
                link(last)
                link(V.reduce_max(m1[:], lem[:], AX_X))
                first_of(A1[:], lem[:], m1[:], EXPERTS, eq[:])
                link(V.scalar_tensor_tensor(out=lem[:], in0=A1[:], scalar=3 * NEG, in1=lem[:], op0=ALU.mult, op1=ALU.add))
                link(V.reduce_max(m2[:], lem[:], AX_X))
                first_of(A2[:], lem[:], m2[:], EXPERTS, eq[:])
                V.tensor_tensor(dd[:], m2[:], m1[:], ALU.subtract).then_inc(weights_asked, 1)
                link(V.tensor_tensor(M[:], A1[:], A2[:], ALU.add))
                link(V.tensor_tensor(M[:], M[:], per_tile(valid[:], EXPERTS), ALU.mult))
                V.memset(incl[:], 0.0).then_inc(counted, 1)
                dve.wait_ge(acted, 2)
                link(V.reduce_sum(gsum[:], gd[:], AX_X))
                link(V.reciprocal(gate[:], gsum[:]))
                link(V.tensor_scalar(rec[:], ed[:], 1.0, None, ALU.add))
                link(V.reciprocal(rec[:], rec[:]))
                link(V.tensor_tensor(k.weight[:, 0, :], rec[:], gate[:], ALU.mult))
                link(V.tensor_tensor(k.weight[:, 1, :], k.weight[:, 0, :], ed[:], ALU.mult))
                dve.wait_ge(summed, 1)
                for t in range(NT):
                    link(V.tensor_tensor(base[:, t + 1, :], base[:, t, :], tot_ps[:, t, :], ALU.add))
                link(V.tensor_scalar(nbi[:], base[:, NT, :], float(P - 1), None, ALU.add))
                link(V.tensor_scalar(nbi[:], nbi[:], 7, None, ALU.logical_shift_right))
                link(V.tensor_copy(nb[:], nbi[:]))
                link(V.tensor_tensor_scan(incl[:], nb[:], zeros[:], 0.0, ALU.add, ALU.add))
                link(V.tensor_tensor(start[:], incl[:], nb[:], ALU.subtract))
                link(V.tensor_scalar(start[:], start[:], float(P), None, ALU.mult))
                link(V.tensor_tensor(pos[:], rank_ps[:], base[:, 0:NT, :], ALU.add))
                link(V.tensor_tensor(pos[:], pos[:], start[:].unsqueeze(1).to_broadcast([P, NT, EXPERTS]), ALU.add))
                for i, A in enumerate((A1, A2)):
                    link(V.tensor_tensor(tmp[:], A[:], pos[:], ALU.mult))
                    link(V.reduce_sum(destf[:, i, :], tmp[:], AX_X))
                link(V.tensor_copy(k.dest[:], destf[:]))
                V.tensor_scalar(dd[:], dd[:], 0.0, None, ALU.mult).then_inc(placed, 1)
                link(V.tensor_tensor(cmp[:], incl[0:1, :].unsqueeze(1).to_broadcast([1, BLOCKS, EXPERTS]),
                                     iota[0:1, 0:BLOCKS].unsqueeze(2).to_broadcast([1, BLOCKS, EXPERTS]), ALU.is_le))
                link(V.reduce_sum(bef[:], cmp[:], AX_X))
                link(V.tensor_scalar(k.block_expert[:], bef[:], float(EXPERTS - 1), None, ALU.min))
                link(V.tensor_scalar(k.turns[:], incl[0:1, EXPERTS - 1:EXPERTS], -2.0, None, ALU.add))
                link(V.tensor_scalar(k.turns[:], k.turns[:], 1, None, ALU.logical_shift_right))


def experts(k):
    nc, d = k.nc, k.dram
    KE = DE // P
    wg_d = d["w_gate"][0].rearrange("e (p c) f -> e p (c f)", p=P)
    wu_d = d["w_up"][0].rearrange("e (p c) f -> e p (c f)", p=P)
    wd_d = d["w_down"][0].rearrange("e (p c) n -> e p (c n)", p=P)
    with k.scope() as s:
        wg, wu = (s.sb(f"ex_{n}", [P, 2, KD * DE]) for n in ("wg", "wu"))
        wd = s.sb("ex_wd", [P, 2, KE * D])
        idx = [s.sb(f"ex_idx{i}", [P, 1], I32) for i in range(2)]
        slots, slots_f = s.sb("ex_slots", [BLOCKS, P], I32), s.sb("ex_slots_f", [BLOCKS, P])
        idx_all = s.sb("ex_idx_all", [P, BLOCKS], I32)
        x = [s.sb(f"ex_x{i}", [P, D]) for i in range(2)]
        xT = s.sb("ex_xT", [P, 2, KD, P])
        act_g, h = s.sb("ex_act_g", [P, 2, DE]), s.sb("ex_h", [P, 2, DE])
        hT = s.sb("ex_hT", [P, 2, KE, P])
        y = s.sb("ex_y", [P, 2, 2, BANK])
        xps = s.ps("ex_xps", [P, 2, KD // 2, P])
        gu = s.ps("ex_gu", [P, 2, 2, DE])
        hps = s.ps("ex_hps", [P, KE, P])
        yps = s.ps("ex_yps", [P, 2, BANK])
        w_loaded = [s.sem(f"ex_w_loaded{i}") for i in range(2)]
        slots_loaded, slots_kept, slots_turned, idx_ready = (s.sem(f"ex_{n}") for n in ("slots_loaded", "slots_kept", "slots_turned", "idx_ready"))
        gathered = [s.sem(f"ex_gathered{i}") for i in range(2)]
        stored = [s.sem(f"ex_stored{i}") for i in range(2)]
        gather_due, load_due = s.sem("ex_gather_due"), s.sem("ex_load_due")
        x_turned, x_kept_a, x_kept_v, gu_done, silu_done, h_done, h_turned, h_kept, y_done, y_kept_a, y_kept_v = (
            s.sem(f"ex_{n}") for n in ("x_turned", "x_kept_a", "x_kept_v", "gu_done", "silu_done", "h_done", "h_turned",
                                       "h_kept", "y_done", "y_kept_a", "y_kept_v"))

        TURNS = (BLOCKS - 3) // 2

        def turns(eng, body):
            busy = eng.value_load(k.turns[0:1, 0:1], min_val=(2 * ROWS // P - 2) // 2, max_val=TURNS)
            body(0, 0, False)
            body(1, 1, False)
            with eng.Fori(0, TURNS) as i:
                with eng.If(i < busy):
                    body(i * 2 + 2, 0, False)
                    body(i * 2 + 3, 1, False)
            body(busy * 2 + 2, 0, True)
            return busy

        def fixed(b):
            return isinstance(b, int)

        with nc.Block() as block:
            @block.sync
            def _(sp):
                def load(b, i):
                    if not fixed(b) or b >= 2:
                        sp.wait_ge(y_done, b - 1)
                        sp.sem_inc(load_due, 1)
                    e = sp.value_load(k.block_expert[0:1, bass.ds(b, 1)], min_val=0, max_val=EXPERTS - 1)
                    sp.dma_start(wg[:, i, :], wg_d[bass.ds(e, 1)].rearrange("e p n -> p (e n)")).then_inc(w_loaded[i], 16)
                    sp.dma_start(wu[:, i, :], wu_d[bass.ds(e, 1)].rearrange("e p n -> p (e n)")).then_inc(w_loaded[i], 16)
                    sp.dma_start(wd[:, i, :], wd_d[bass.ds(e, 1)].rearrange("e p n -> p (e n)")).then_inc(w_loaded[i], 16)

                def body(b, i, last_one):
                    if not last_one:
                        load(b + 1, 1 - i)
                    sp.wait_ge(y_kept_a, b + 1)
                    sp.wait_ge(y_kept_v, b + 1)
                    sp.dma_start(d["expert_out"][bass.ds(b * P, P), :], y[:, i].rearrange("p b n -> p (b n)")).then_inc(stored[i], 16)

                sp.dma_start(slots[:], d["slot_token"].rearrange("(b p) o -> b (p o)", p=P)).then_inc(slots_loaded, 16)
                load(0, 0)
                busy = turns(sp, body)
                sp.wait_ge(stored[0], busy * 16 + 32)
                sp.sem_inc(load_due, 1)
                sp.wait_ge(stored[1], busy * 16 + 16)
                sp.sem_inc(load_due, 1)

            @block.gpsimd
            def _(pool):
                def gather(b, i):
                    if not fixed(b) or b >= 2:
                        pool.wait_ge(x_turned, b - 1)
                    pool.sem_inc(gather_due, 1)
                    nc.gpsimd.tensor_copy(idx[i][:], idx_all[:, bass.ds(b, 1)]).then_inc(idx_ready, 1)
                    pool.wait_ge(idx_ready, b + 1)
                    pool.sem_inc(gather_due, 1)
                    nc.gpsimd.indirect_dma_start(out=x[i][:], out_offset=None, in_=d["ffn_in"],
                                                 in_offset=bass.IndirectOffsetOnAxis(ap=idx[i][:, 0:1], axis=0)).then_inc(gathered[i], 16)

                def body(b, i, last_one):
                    if not last_one:
                        gather(b + 1, 1 - i)

                pool.wait_ge(slots_kept, 2)
                gather(0, 0)
                turns(pool, body)

            @block.tensor
            def _(pe):
                def turn(b, i):
                    pe.wait_ge(gathered[i], (b - i) * 8 + 16)
                    if not fixed(b) or b >= 1:
                        pe.wait_ge(x_kept_a, b)
                        pe.wait_ge(x_kept_v, b)
                    for c in range(KD):
                        last = nc.tensor.transpose(xps[:, c // 4, c % 4, :], x[i][:, c:D:KD], k.ident[:])
                    last.then_inc(x_turned, 1)

                def body(b, i, last_one):
                    pe.wait_ge(w_loaded[i], (b - i) * 24 + 48)
                    pe.wait_ge(x_kept_a, b + 1)
                    pe.wait_ge(x_kept_v, b + 1)
                    if not fixed(b) or b >= 2:
                        pe.wait_ge(h_done, b - 1)
                    for j, w in enumerate((wg, wu)):
                        for c in range(KD):
                            last = nc.tensor.matmul(gu[:, i, j, :], xT[:, i, c, :], w[:, i, c * DE:(c + 1) * DE], start=(c == 0), stop=(c == KD - 1))
                    last.then_inc(gu_done, 1)
                    if not last_one:
                        turn(b + 1, 1 - i)
                    pe.wait_ge(h_done, b + 1)
                    if not fixed(b) or b >= 1:
                        pe.wait_ge(h_kept, b)
                    for c in range(KE):
                        last = nc.tensor.transpose(hps[:, c, :], h[:, i, c:DE:KE], k.ident[:])
                    last.then_inc(h_turned, 1)
                    pe.wait_ge(h_kept, b + 1)
                    if not fixed(b) or b >= 1:
                        pe.wait_ge(y_kept_a, b)
                        pe.wait_ge(y_kept_v, b)
                    for n in range(2):
                        for c in range(KE):
                            last = nc.tensor.matmul(yps[:, n, :], hT[:, i, c, :], wd[:, i, c * D + n * BANK:c * D + (n + 1) * BANK], start=(c == 0), stop=(c == KE - 1))
                    last.then_inc(y_done, 1)

                pe.wait_ge(slots_kept, 1)
                nc.tensor.transpose(hps[:, 0, 0:BLOCKS], slots_f[:], k.ident[0:BLOCKS, 0:BLOCKS]).then_inc(slots_turned, 1)
                pe.wait_ge(slots_kept, 2)
                turn(0, 0)
                turns(pe, body)

            def keep_x(eng, copy, half, kept, b, i):
                eng.wait_ge(x_turned, b + 1)
                if not fixed(b) or b >= 2:
                    eng.wait_ge(gu_done, b - 1)
                copy(xT[:, i, half * 4:half * 4 + 4, :], xps[:, half]).then_inc(kept, 1)

            def keep_y(eng, copy, half, kept, b, i):
                eng.wait_ge(y_done, b + 1)
                if not fixed(b) or b >= 2:
                    eng.wait_ge(stored[i], (b - i) * 8)
                copy(y[:, i, half, :], yps[:, half, :]).then_inc(kept, 1)

            @block.scalar
            def _(act):
                def body(b, i, last_one):
                    act.wait_ge(gu_done, b + 1)
                    if not fixed(b) or b >= 2:
                        act.wait_ge(h_done, b - 1)
                    nc.scalar.activation(act_g[:, i, :], gu[:, i, 0, :], ACT.Silu).then_inc(silu_done, 1)
                    if not last_one:
                        keep_x(act, nc.scalar.copy, 0, x_kept_a, b + 1, 1 - i)
                    act.wait_ge(h_turned, b + 1)
                    if not fixed(b) or b >= 2:
                        act.wait_ge(y_done, b - 1)
                    nc.scalar.copy(hT[:, i], hps[:]).then_inc(h_kept, 1)
                    keep_y(act, nc.scalar.copy, 0, y_kept_a, b, i)

                keep_x(act, nc.scalar.copy, 0, x_kept_a, 0, 0)
                turns(act, body)

            @block.vector
            def _(dve):
                def body(b, i, last_one):
                    dve.wait_ge(silu_done, b + 1)
                    if not fixed(b) or b >= 2:
                        dve.wait_ge(h_turned, b - 1)
                    nc.vector.tensor_tensor(h[:, i, :], act_g[:, i, :], gu[:, i, 1, :], ALU.mult).then_inc(h_done, 1)
                    if not last_one:
                        keep_x(dve, nc.vector.tensor_copy, 1, x_kept_v, b + 1, 1 - i)
                    keep_y(dve, nc.vector.tensor_copy, 1, y_kept_v, b, i)

                dve.wait_ge(slots_loaded, 16)
                nc.vector.tensor_copy(slots_f[:], slots[:]).then_inc(slots_kept, 1)
                dve.wait_ge(slots_turned, 1)
                nc.vector.tensor_copy(idx_all[:], hps[:, 0, 0:BLOCKS]).then_inc(slots_kept, 1)
                keep_x(dve, nc.vector.tensor_copy, 1, x_kept_v, 0, 0)
                turns(dve, body)


def combine(k):
    nc, d = k.nc, k.dram
    with k.scope() as s:
        nf = s.sb("co_nf", [P, D])
        y = [[s.sb(f"co_y{j}{i}", [P, D]) for i in range(2)] for j in range(2)]
        r, out = s.sb("co_r", [P, 2, D]), s.sb("co_out", [P, 2, D])
        square = s.sb("co_square", [P, D])
        ss, mean, inv, rstd = (s.sb(f"co_{n}", [P, NT]) for n in ("ss", "mean", "inv", "rstd"))
        nf_loaded = s.sem("co_nf_loaded")
        r_loaded, gathered, stored = ([s.sem(f"co_{n}{i}") for i in range(2)] for n in ("r_loaded", "gathered", "stored"))
        half, added, squared, meaned, inverted, rooted, normed = (s.sem(f"co_{n}") for n in (
            "half", "added", "squared", "meaned", "inverted", "rooted", "normed"))
        with nc.Block() as block:
            @block.sync
            def _(sp):
                sp.dma_start(nf[:], d["norm_final"].partition_broadcast(P)).then_inc(nf_loaded, 16)

                def load(t):
                    r0, n = TILES[t]
                    sp.dma_start(r[0:n, t % 2, :], d["resid"][r0:r0 + n, :]).then_inc(r_loaded[t % 2], 16)

                load(0)
                load(1)
                for t in range(NT):
                    sp.wait_ge(normed, t + 1)
                    if t == 0:
                        sp.dma_start(d["y_sample"].rearrange("b t d -> (b t) d"), out[0:NS, 0, :]).then_inc(stored[0], 16)
                    else:
                        sp.dma_start(d["y_prompt"][0, (t - 1) * P:t * P, :], out[:, t % 2, :]).then_inc(stored[t % 2], 16)
                    if t + 2 < NT:
                        load(t + 2)
                sp.wait_ge(stored[0], 16 * 5)
                sp.wait_ge(stored[1], 16 * 4)

            @block.gpsimd
            def _(pool):
                for t, (r0, n) in enumerate(TILES):
                    if t >= 2:
                        pool.wait_ge(added, t - 1)
                    for j in range(2):
                        nc.gpsimd.indirect_dma_start(out=y[j][t % 2][0:n, :], out_offset=None, in_=d["expert_out"],
                                                     in_offset=bass.IndirectOffsetOnAxis(ap=k.dest[0:n, j, t:t + 1], axis=0)).then_inc(gathered[t % 2], 16)

            @block.vector
            def _(dve):
                dve.wait_ge(nf_loaded, 16)
                for t, (r0, n) in enumerate(TILES):
                    i = t % 2
                    dve.wait_ge(r_loaded[i], 16 * (t // 2 + 1))
                    dve.wait_ge(gathered[i], 32 * (t // 2 + 1))
                    rt = r[0:n, i, :]
                    nc.vector.scalar_tensor_tensor(out=rt, in0=y[0][i][0:n, :], scalar=k.weight[0:n, 0, t:t + 1], in1=rt, op0=ALU.mult, op1=ALU.add).then_inc(half, 1)
                    dve.wait_ge(half, t + 1)
                    nc.vector.scalar_tensor_tensor(out=rt, in0=y[1][i][0:n, :], scalar=k.weight[0:n, 1, t:t + 1], in1=rt, op0=ALU.mult, op1=ALU.add).then_inc(added, 1)
                    dve.wait_ge(squared, t + 1)
                    nc.vector.tensor_scalar(mean[0:n, t:t + 1], ss[0:n, t:t + 1], 1.0 / D, EPS, ALU.mult, ALU.add).then_inc(meaned, 1)
                    dve.wait_ge(meaned, t + 1)
                    nc.vector.reciprocal(inv[0:n, t:t + 1], mean[0:n, t:t + 1]).then_inc(inverted, 1)
                    dve.wait_ge(rooted, t + 1)
                    if t >= 2:
                        dve.wait_ge(stored[i], 16 * (t // 2))
                    nc.vector.scalar_tensor_tensor(out=out[0:n, i, :], in0=rt, scalar=rstd[0:n, t:t + 1], in1=nf[0:n, :], op0=ALU.mult, op1=ALU.mult).then_inc(normed, 1)

            @block.scalar
            def _(act):
                for t, (r0, n) in enumerate(TILES):
                    act.wait_ge(added, t + 1)
                    if t:
                        act.wait_ge(squared, t)
                    nc.scalar.activation(square[0:n, :], r[0:n, t % 2, :], ACT.Square, accum_out=ss[0:n, t:t + 1]).then_inc(squared, 1)
                    act.wait_ge(inverted, t + 1)
                    nc.scalar.activation(rstd[0:n, t:t + 1], inv[0:n, t:t + 1], ACT.Sqrt).then_inc(rooted, 1)


def decoder_step(nc, dram):
    k = Core(nc, dram)
    with k:
        load_constants(k)
        with k.scope() as s:
            k.qd, k.kvd = s.sb("qd", [P, NT, QL]), s.sb("kvd", [P, NT, CK])
            k.hT_hi, k.hT_lo = (s.sb(n, [P, KD, ROWS], F32R) for n in ("hT_hi", "hT_lo"))
            normalise_input(k)
            project_input(k)
        with k.scope() as s:
            k.g, k.beta = s.sb("g", [P, NT + 1, GH]), s.sb("beta", [P, NT + 1, GH])
            k.G, k.left, k.total_exp = (s.sb(n, [P, NT, GH]) for n in ("G", "left", "total_exp"))
            k.g_exp = s.sb("g_exp", [P, GH])
            gdn_gates(k)
            k.convT = s.sb("convT", [P, GC, ROWS])
            convolve(k)
            gdn_prompt(k)
            gdn_sample(k)
        gate_gdn(k)
        k.q0T = k.sb("q0T", [QK, HEADS, NS])
        k.new_row = k.sb("new_row", [NS, CK])
        with k.scope() as s:
            k.rope = s.sb("rope", [P, NT, ROPE])
            k.keyT = s.sb("keyT", [QK, HEADS, PROMPT])
            k.qlT = s.sb("qlT", [P, KQ, ROWS])
            k.val = s.sb("val", [P, NT, D])
            with k.scope() as s2:
                k.latT = s2.sb("latT", [P, 2, ROWS])
                mla_latents(k)
                mla_keys_values(k)
            attend_prompt(k)
        attend_sample(k)
        k.logits = k.sb("logits", [P, NT, GROUPS + EXPERTS])
        k.dest = k.sb("dest", [P, 2, NT], I32)
        k.weight = k.sb("weight", [P, 2, NT])
        k.block_expert = k.sb("block_expert", [1, BLOCKS], I32)
        k.turns = k.sb("turns", [1, 1], I32)
        project_output(k)
        route(k)
        experts(k)
        combine(k)


_INPUTS = ["x_prompt", "x_sample", "cache_kv_latent", "cache_k_rope", "page_table", "state_conv", "state_gdn",
           "meta_tokens", "norm_mix", "w_in", "q_norm", "w_uq", "kv_norm", "w_uk", "w_uv", "conv_w", "a_log",
           "dt_bias", "gdn_norm", "w_out", "norm_ffn", "w_group", "b_group", "w_router", "b_router", "w_gate",
           "w_up", "w_down", "norm_final"]
_OUTPUTS = [("y_prompt", (1, SEQ, D)), ("y_sample", (NS, 1, D)),
            ("new_latent_prompt", (1, 1, PROMPT, CL)), ("new_rope_prompt", (1, 1, PROMPT, ROPE)),
            ("new_latent_sample", (1, NS, 1, CL)), ("new_rope_sample", (1, NS, 1, ROPE)),
            ("new_conv_prompt", (1, 1, 3, 3 * D)), ("new_conv_sample", (1, NS, 3, 3 * D)),
            ("new_gdn_prompt", (1, 1, GH, DK, DK)), ("new_gdn_sample", (1, NS, GH, DK, DK))]
_SCRATCH = [("projT", (GC + 3 * GH, P, ROWS), F32), ("gdnT", (GH, P, ROWS), F32),
            ("latents", (P, NT, QL + CK), F32), ("mixT", (GH, P, ROWS), F32), ("ffn_in", (ROWS, D), F32),
            ("slot_token", (SLOTS, 1), I32), ("expert_out", (SLOTS, D), F32), ("resid", (ROWS, D), F32)]


def shape_constants():
    import numpy as np

    i = np.arange(P)
    f = np.float32
    levels = np.stack([((i[None, :] >> l) == (i[:, None] >> l) + 1) & (((i[None, :] >> l) & 1) == 1)
                       for l in range(7)], 1)
    inv_freq = np.float32(10000.0) ** (-np.arange(0, ROPE, 2, dtype=f) / f(ROPE))
    pos = np.concatenate([np.full(NS, PAGES * PAGE), np.arange(PROMPT)]).astype(f)
    ang = (pos[:, None] * inv_freq[None, :]).astype(f)
    rope = np.concatenate([np.cos(ang), np.sin(ang)], 1).astype(f)
    table = np.zeros((NT, P, ROPE), f)
    for t, (r0, n) in enumerate(TILES):
        table[t, :n] = rope[r0:r0 + n]
    valid = np.zeros((P, NT), f)
    for t, (_, n) in enumerate(TILES):
        valid[:n, t] = 1
    token = np.stack([np.arange(P) + r0 for r0, _ in TILES], 1)
    return {
        "c_ident": np.eye(P, dtype=f),
        "c_upto": (i[:, None] <= i[None, :]).astype(f),
        "c_before": (i[:, None] < i[None, :]).astype(f),
        "c_levels": levels.astype(f),
        "c_rope": np.ascontiguousarray(table.transpose(1, 0, 2)),
        "c_future": np.where(i[None, :] > i[:, None], f(NEG), f(0)).astype(f),
        "c_diag8": np.repeat(np.eye(NS, dtype=f)[:, :, None], P, 2),
        "c_rep16": np.repeat(np.eye(NS, dtype=f), HEADS, 1),
        "c_pick16": np.repeat(np.eye(NS, dtype=f), HEADS, 0),
        "c_quarter": (i % 32).astype(f)[:, None].copy(),
        "c_iota": np.broadcast_to(np.arange(64, dtype=f), (P, 64)).copy(),
        "c_valid": valid,
        "c_token": token.astype(np.int32),
    }


def kernel(**inputs):
    import concourse.bacc as _bacc
    import numpy as _np
    from concourse.bass_utils import run_bass_kernel_spmd as _run

    nc = _bacc.Bacc("TRN2", target_bir_lowering=False, num_devices=1)
    arrays = {name: _np.ascontiguousarray(inputs[name]) for name in _INPUTS}
    arrays.update(shape_constants())
    dram = {}
    for name, a in arrays.items():
        dram[name] = nc.dram_tensor(name, a.shape, mybir.dt.from_np(a.dtype), kind="ExternalInput").ap()
    for name, shape in _OUTPUTS:
        dram[name] = nc.dram_tensor(name, shape, F32, kind="ExternalOutput").ap()
    for name, shape, dt in _SCRATCH:
        dram[name] = nc.dram_tensor(name, shape, dt).ap()
    decoder_step(nc, dram)
    r = _run(nc, [arrays], core_ids=[0])
    return tuple(r.results[0][name] for name, _ in _OUTPUTS)
```
